# Optimizing a Trainium2 kernel written in Bass

```python
import jax, jax.numpy as jnp
from jax import lax
import numpy as np

D_MODEL = 1024
BATCH = 1
SEQ = 256
DEPTH = 1

SSD_INNER = 2 * D_MODEL
SSD_HEAD_DIM = 64
SSD_HEADS = SSD_INNER // SSD_HEAD_DIM
SSD_GROUPS = 8
SSD_HEADS_PER_GROUP = SSD_HEADS // SSD_GROUPS
SSD_STATE = 128
SSD_CONV = 4
SSD_CHUNK = 128
SSD_CONV_DIM = SSD_INNER + 2 * SSD_GROUPS * SSD_STATE
SC_WIDTH = D_MODEL
SC_KERNEL = 3
N_EXPERTS = 64
TOP_K = 8
N_EXPERT_GROUPS = 8
TOPK_EXPERT_GROUPS = 4
D_EXPERT = 256
ROUTED_SCALE = 2.5
MOE_BLOCK = 128
LN_EPS = 1e-5
RMS_EPS = 1e-5
ALPHA = (2.0 * DEPTH) ** 0.25
BETA = (8.0 * DEPTH) ** -0.25
_IN_SIZES = (SSD_INNER, SSD_CONV_DIM, SSD_HEADS, SC_WIDTH, SC_WIDTH, SC_WIDTH, D_MODEL, D_MODEL)
IN_COLS = int(sum(_IN_SIZES))
IN_SPLITS = [int(v) for v in np.cumsum(_IN_SIZES)[:-1]]


def layer_norm(x):
    xf = x.astype(jnp.float32)
    mu = jnp.mean(xf, axis=-1, keepdims=True)
    xc = xf - mu
    var = jnp.mean(xc * xc, axis=-1, keepdims=True)
    return xc * lax.rsqrt(var + LN_EPS)

def causal_depthwise_conv(u, w):
    k = w.shape[0]
    return lax.conv_general_dilated(
        u, w[:, None, :].astype(u.dtype), window_strides=(1,), padding=[(k - 1, 0)],
        dimension_numbers=("NWC", "WIO", "NWC"), feature_group_count=u.shape[-1])

def gated_rmsnorm(y, z, w):
    g = y.astype(jnp.float32) * jax.nn.silu(z.astype(jnp.float32))
    g = g.reshape(*y.shape[:-1], SSD_GROUPS, -1)
    g = g * lax.rsqrt(jnp.mean(g * g, axis=-1, keepdims=True) + RMS_EPS)
    return g.reshape(y.shape) * w.astype(jnp.float32)

def ssd_chunked(xg, dt, A, Bg, Cg):
    b, s, g, r, p = xg.shape
    n = Bg.shape[-1]
    nc = s // SSD_CHUNK
    l = SSD_CHUNK
    X = (xg * dt[..., None]).reshape(b, nc, l, g, r, p)
    dA = (dt * A).reshape(b, nc, l, g, r).transpose(0, 1, 3, 4, 2)
    Bc = Bg.reshape(b, nc, l, g, n)
    Cc = Cg.reshape(b, nc, l, g, n)
    A_cs = jnp.cumsum(dA, axis=-1)
    seg = A_cs[..., :, None] - A_cs[..., None, :]
    causal = jnp.tril(jnp.ones((l, l), dtype=bool))
    Lmat = jnp.exp(jnp.where(causal, seg, -jnp.inf))
    CB = jnp.einsum("bclgn,bcsgn->bcgls", Cc, Bc)
    scores = CB[:, :, :, None] * Lmat
    y_diag = jnp.einsum("bcgrls,bcsgrp->bclgrp", scores, X)
    decay_states = jnp.exp(A_cs[..., -1:] - A_cs).transpose(0, 1, 4, 2, 3)
    states = jnp.einsum("bclgn,bclgrp->bcgrpn", Bc, X * decay_states[..., None])
    chunk_decay = jnp.exp(A_cs[..., -1])

    def step(h, inp):
        st, dec = inp
        return dec[..., None, None] * h + st, h

    h0 = jnp.zeros((b, g, r, p, n), jnp.float32)
    _, prev = lax.scan(step, h0, (states.transpose(1, 0, 2, 3, 4, 5).astype(jnp.float32),
                                  chunk_decay.transpose(1, 0, 2, 3)))
    prev = prev.transpose(1, 0, 2, 3, 4, 5)
    out_decay = jnp.exp(A_cs).transpose(0, 1, 4, 2, 3)
    y_off = jnp.einsum("bclgn,bcgrpn->bclgrp", Cc, prev) * out_decay[..., None]
    return (y_diag + y_off).reshape(b, s, g, r, p)

def hybrid_mixer(h, w_in, ssd_conv_w, ssd_conv_b, ssd_dt_bias, ssd_A_log, ssd_D, ssd_norm_w,
                 w_ssd_out, sc_conv_w, w_sc_out, w_o):
    b, s, _ = h.shape
    z, xbc, dt_raw, sc_b, sc_c, sc_h, gate_a, gate_b = jnp.split(h @ w_in, IN_SPLITS, axis=-1)
    xbc = jax.nn.silu(causal_depthwise_conv(xbc, ssd_conv_w) + ssd_conv_b)
    xs, Bm, Cm = jnp.split(xbc, [SSD_INNER, SSD_INNER + SSD_GROUPS * SSD_STATE], axis=-1)
    dt = jax.nn.softplus(dt_raw.astype(jnp.float32) + ssd_dt_bias.astype(jnp.float32))
    A = -jnp.exp(ssd_A_log.astype(jnp.float32))
    G, R = SSD_GROUPS, SSD_HEADS_PER_GROUP
    xg = xs.reshape(b, s, G, R, SSD_HEAD_DIM)
    y = ssd_chunked(xg, dt.reshape(b, s, G, R), A.reshape(G, R),
                    Bm.reshape(b, s, G, SSD_STATE), Cm.reshape(b, s, G, SSD_STATE))
    y = y + ssd_D.reshape(G, R)[:, :, None] * xg
    y = gated_rmsnorm(y.reshape(b, s, SSD_INNER), z, ssd_norm_w).astype(h.dtype)
    y_a = y @ w_ssd_out
    u = causal_depthwise_conv(sc_c * sc_h, sc_conv_w)
    y_b = (sc_b * u) @ w_sc_out
    merged = jax.nn.sigmoid(gate_a) * y_a + jax.nn.sigmoid(gate_b) * y_b
    return merged @ w_o

def moe_ffn(h, router_w, router_bias, w_gate, w_up, w_down, sh_gate, sh_up, sh_down):
    b, s, d = h.shape
    T = b * s
    hf = h.reshape(T, d)
    scores = jax.nn.sigmoid((hf @ router_w).astype(jnp.float32))
    biased = scores + router_bias.astype(jnp.float32)
    grp = biased.reshape(T, N_EXPERT_GROUPS, N_EXPERTS // N_EXPERT_GROUPS)
    grp_score = lax.top_k(grp, 2)[0].sum(-1)
    _, grp_idx = lax.top_k(grp_score, TOPK_EXPERT_GROUPS)
    grp_mask = jax.nn.one_hot(grp_idx, N_EXPERT_GROUPS, dtype=jnp.float32).sum(1) > 0
    expert_mask = jnp.repeat(grp_mask, N_EXPERTS // N_EXPERT_GROUPS, axis=1)
    _, e_idx = lax.top_k(jnp.where(expert_mask, biased, -jnp.inf), TOP_K)
    gate = jnp.take_along_axis(scores, e_idx, axis=1)
    gate = gate / jnp.sum(gate, axis=-1, keepdims=True) * ROUTED_SCALE
    n_assign = T * TOP_K
    nb = (n_assign + MOE_BLOCK - 1) // MOE_BLOCK + N_EXPERTS
    n_rows = nb * MOE_BLOCK
    e_flat = e_idx.reshape(-1)
    tok_flat = jnp.arange(n_assign, dtype=jnp.int32) // TOP_K
    order = jnp.argsort(e_flat)
    e_sorted = e_flat[order]
    tok_sorted = tok_flat[order]
    gate_sorted = gate.reshape(-1)[order]
    counts = jnp.bincount(e_flat, length=N_EXPERTS)
    padded = (counts + MOE_BLOCK - 1) // MOE_BLOCK * MOE_BLOCK
    start = jnp.cumsum(counts) - counts
    pend = jnp.cumsum(padded)
    pstart = pend - padded
    dest = pstart[e_sorted] + (jnp.arange(n_assign) - start[e_sorted])
    row_tok = jnp.full((n_rows,), T, jnp.int32).at[dest].set(tok_sorted)
    row_gate = jnp.zeros((n_rows,), jnp.float32).at[dest].set(gate_sorted)
    block_expert = jnp.minimum(
        jnp.searchsorted(pend, jnp.arange(nb) * MOE_BLOCK, side="right"), N_EXPERTS - 1)
    h_pad = jnp.concatenate([hf, jnp.zeros((1, d), hf.dtype)], axis=0)
    xin = h_pad[row_tok].reshape(nb, MOE_BLOCK, d)

    def expert_block(args):
        xb, e = args
        return (jax.nn.silu(xb @ w_gate[e]) * (xb @ w_up[e])) @ w_down[e]

    yb = lax.map(expert_block, (xin, block_expert)).reshape(n_rows, d)
    routed = jax.ops.segment_sum(yb * row_gate[:, None], row_tok, num_segments=T + 1)[:T]
    shared = (jax.nn.silu(hf @ sh_gate) * (hf @ sh_up)) @ sh_down
    return (routed + shared).reshape(b, s, d)

def first_inputs(seed: int = 0) -> dict:
    key = jax.random.key(seed)
    ks = jax.random.split(key, 32)
    L, D, E = DEPTH, D_MODEL, N_EXPERTS
    f32 = jnp.float32

    def nrm(k, shape, fan_in, scale=1.0):
        return jax.random.normal(k, shape, f32) * (scale * fan_in ** -0.5)

    u = jax.random.uniform(ks[5], (L, SSD_HEADS), f32)
    dt0 = jnp.exp(u * (np.log(0.1) - np.log(1e-3)) + np.log(1e-3))
    return {
        "x": jax.random.normal(ks[0], (BATCH, SEQ, D), f32),
        "c": jax.random.normal(ks[1], (BATCH, D), f32),
        "w_ada": nrm(ks[2], (L, D, 6 * D), D),
        "b_ada": 0.02 * jax.random.normal(ks[3], (L, 6 * D), f32),
        "w_in": nrm(ks[4], (L, D, IN_COLS), D),
        "ssd_conv_w": nrm(ks[6], (L, SSD_CONV, SSD_CONV_DIM), SSD_CONV),
        "ssd_conv_b": 0.02 * jax.random.normal(ks[7], (L, SSD_CONV_DIM), f32),
        "ssd_dt_bias": dt0 + jnp.log(-jnp.expm1(-dt0)),
        "ssd_A_log": jnp.log(jax.random.uniform(ks[8], (L, SSD_HEADS), f32, 1.0, 16.0)),
        "ssd_D": 1.0 + 0.1 * jax.random.normal(ks[9], (L, SSD_HEADS), f32),
        "ssd_norm_w": 1.0 + 0.1 * jax.random.normal(ks[10], (L, SSD_INNER), f32),
        "w_ssd_out": nrm(ks[11], (L, SSD_INNER, D), SSD_INNER, BETA),
        "sc_conv_w": nrm(ks[12], (L, SC_KERNEL, SC_WIDTH), SC_KERNEL),
        "w_sc_out": nrm(ks[13], (L, SC_WIDTH, D), SC_WIDTH, BETA),
        "w_o": nrm(ks[14], (L, D, D), D, BETA),
        "ln1_g": 1.0 + 0.1 * jax.random.normal(ks[15], (L, D), f32),
        "ln1_b": 0.02 * jax.random.normal(ks[16], (L, D), f32),
        "router_w": nrm(ks[17], (L, D, E), D),
        "router_bias": 0.01 * jax.random.normal(ks[18], (L, E), f32),
        "w_gate": nrm(ks[19], (L, E, D, D_EXPERT), D, BETA),
        "w_up": nrm(ks[20], (L, E, D, D_EXPERT), D, BETA),
        "w_down": nrm(ks[21], (L, E, D_EXPERT, D), D_EXPERT, BETA),
        "sh_gate": nrm(ks[22], (L, D, D_EXPERT), D, BETA),
        "sh_up": nrm(ks[23], (L, D, D_EXPERT), D, BETA),
        "sh_down": nrm(ks[24], (L, D_EXPERT, D), D_EXPERT, BETA),
        "ln2_g": 1.0 + 0.1 * jax.random.normal(ks[25], (L, D), f32),
        "ln2_b": 0.02 * jax.random.normal(ks[26], (L, D), f32),
    }

def first_block(x, c, w_ada, b_ada, w_in, ssd_conv_w, ssd_conv_b, ssd_dt_bias, ssd_A_log, ssd_D,
              ssd_norm_w, w_ssd_out, sc_conv_w, w_sc_out, w_o, ln1_g, ln1_b, router_w,
              router_bias, w_gate, w_up, w_down, sh_gate, sh_up, sh_down, ln2_g, ln2_b):
    dtype = x.dtype
    for l in range(DEPTH):
        mod = jax.nn.silu(c) @ w_ada[l] + b_ada[l]
        sh1, sc1, g1, sh2, sc2, g2 = jnp.split(mod[:, None, :], 6, axis=-1)
        h = (layer_norm(x) * (1.0 + sc1) + sh1).astype(dtype)
        mix = hybrid_mixer(h, w_in[l], ssd_conv_w[l], ssd_conv_b[l], ssd_dt_bias[l], ssd_A_log[l],
                           ssd_D[l], ssd_norm_w[l], w_ssd_out[l], sc_conv_w[l], w_sc_out[l], w_o[l])
        x = (layer_norm(ALPHA * x + g1 * mix) * ln1_g[l] + ln1_b[l]).astype(dtype)
        h = (layer_norm(x) * (1.0 + sc2) + sh2).astype(dtype)
        ffn = moe_ffn(h, router_w[l], router_bias[l], w_gate[l], w_up[l], w_down[l],
                      sh_gate[l], sh_up[l], sh_down[l])
        x = (layer_norm(ALPHA * x + g2 * ffn) * ln2_g[l] + ln2_b[l]).astype(dtype)
    return x


CHUNK = 64
N_PREV_CHUNKS = 8
BAND = (N_PREV_CHUNKS + 1) * CHUNK
HEAD_DIM = 64
H_A = 8
H_B = 8
W_A = H_A * HEAD_DIM
W_B = H_B * HEAD_DIM
W_MIX = W_A + W_B
W_IN = 3 * W_MIX
REL_CLIP = 128
SB_BLOCK = 128
D_FF = 2816
CONV_WIDTH = 3
N_MOD = 6
EPS = 1e-6


def rms_norm(x):
    xf = x.astype(jnp.float32)
    y = xf * lax.rsqrt(jnp.mean(xf * xf, axis=-1, keepdims=True) + EPS)
    return y.astype(x.dtype)

def modulate(h, shift, scale):
    return h * (1 + scale[:, None, :]) + shift[:, None, :]

def rel_bias_band(rel_bias):
    q_pos = N_PREV_CHUNKS * CHUNK + jnp.arange(CHUNK)
    k_pos = jnp.arange(BAND)
    dist = jnp.clip(q_pos[:, None] - k_pos[None, :], -REL_CLIP, REL_CLIP) + REL_CLIP
    return rel_bias[:, dist]

def chunked_rel_attention(q, k, v, rel_bias):
    b, s, h, dh = q.shape
    n_chunks = s // CHUNK
    qc = q.reshape(b, n_chunks, CHUNK, h, dh)
    pad = ((0, 0), (N_PREV_CHUNKS, 0), (0, 0), (0, 0), (0, 0))
    kp = jnp.pad(k.reshape(b, n_chunks, CHUNK, h, dh), pad)
    vp = jnp.pad(v.reshape(b, n_chunks, CHUNK, h, dh), pad)
    band_idx = jnp.arange(n_chunks)[:, None] + jnp.arange(N_PREV_CHUNKS + 1)[None, :]
    kb = kp[:, band_idx].reshape(b, n_chunks, BAND, h, dh)
    vb = vp[:, band_idx].reshape(b, n_chunks, BAND, h, dh)
    scores = jnp.einsum("bcqhd,bckhd->bhcqk", qc, kb).astype(jnp.float32) * (dh ** -0.5)
    scores = scores + rel_bias_band(rel_bias).astype(jnp.float32)[None, :, None]
    key_chunk = (jnp.arange(n_chunks)[:, None] - N_PREV_CHUNKS
                 + (jnp.arange(BAND) // CHUNK)[None, :])
    scores = jnp.where((key_chunk >= 0)[None, None, :, None, :], scores, -jnp.inf)
    probs = jax.nn.softmax(scores, axis=-1).astype(v.dtype)
    out = jnp.einsum("bhcqk,bckhd->bcqhd", probs, vb)
    return out.reshape(b, s, h * dh)

def stick_breaking_attention(q, k, v):
    b, s, h, dh = q.shape
    scale = dh ** -0.5
    outs = []
    for blk in range(s // SB_BLOCK):
        q_start = blk * SB_BLOCK
        k_end = q_start + SB_BLOCK
        logits = jnp.einsum("bqhd,bkhd->bhqk", q[:, q_start:k_end],
                            k[:, :k_end]).astype(jnp.float32) * scale
        strict = (q_start + jnp.arange(SB_BLOCK))[:, None] > jnp.arange(k_end)[None, :]
        log_beta = jax.nn.log_sigmoid(logits)
        log_keep = jnp.where(strict, jax.nn.log_sigmoid(-logits), 0.0)
        log_tail = lax.cumsum(log_keep, axis=3, reverse=True) - log_keep
        weights = jnp.where(strict, jnp.exp(log_beta + log_tail), 0.0).astype(v.dtype)
        outs.append(jnp.einsum("bhqk,bkhd->bqhd", weights, v[:, :k_end]))
    return jnp.concatenate(outs, axis=1).reshape(b, s, h * dh)

def causal_depthwise_conv_2(u, w, bias):
    s = u.shape[1]
    up = jnp.pad(u, ((0, 0), (CONV_WIDTH - 1, 0), (0, 0)))
    y = w[0] * up[:, 0:s]
    for i in range(1, CONV_WIDTH):
        y = y + w[i] * up[:, i:i + s]
    return y + bias

def hybrid_layer(x, c_act, w_ada, b_ada, w_in, rel_bias, g_a, g_b, w_out,
                 w_up, conv_w, conv_b, w_down):
    b, s, _ = x.shape
    mod = c_act @ w_ada + b_ada
    shift_mix, scale_mix, gate_mix, shift_ffn, scale_ffn, gate_ffn = jnp.split(mod, N_MOD, axis=-1)

    h = modulate(rms_norm(x), shift_mix, scale_mix)
    proj = h @ w_in
    cuts = [W_A, 2 * W_A, 3 * W_A, 3 * W_A + W_B, 3 * W_A + 2 * W_B]
    qa, ka, va, qb, kb, vb = jnp.split(proj, cuts, axis=-1)
    oa = chunked_rel_attention(qa.reshape(b, s, H_A, HEAD_DIM), ka.reshape(b, s, H_A, HEAD_DIM),
                               va.reshape(b, s, H_A, HEAD_DIM), rel_bias)
    ob = stick_breaking_attention(qb.reshape(b, s, H_B, HEAD_DIM), kb.reshape(b, s, H_B, HEAD_DIM),
                                  vb.reshape(b, s, H_B, HEAD_DIM))
    mixed = jnp.concatenate([rms_norm(oa) * g_a, rms_norm(ob) * g_b], axis=-1) @ w_out
    x = x + gate_mix[:, None, :] * mixed

    h = modulate(rms_norm(x), shift_ffn, scale_ffn)
    gate, val = jnp.split(causal_depthwise_conv_2(h @ w_up, conv_w, conv_b), 2, axis=-1)
    x = x + gate_ffn[:, None, :] * ((jax.nn.silu(gate) * val) @ w_down)
    return x

def second_inputs(seed: int = 0) -> dict:
    key = jax.random.key(seed)
    ks = jax.random.split(key, 14)
    f32 = jnp.float32
    nrm = lambda k, shape: jax.random.normal(k, shape, dtype=f32)
    return {
        "x": nrm(ks[0], (BATCH, SEQ, D_MODEL)),
        "c": nrm(ks[1], (BATCH, D_MODEL)),
        "w_ada": nrm(ks[2], (DEPTH, D_MODEL, N_MOD * D_MODEL)) * D_MODEL ** -0.5,
        "b_ada": nrm(ks[3], (DEPTH, N_MOD * D_MODEL)) * 0.02,
        "w_in": nrm(ks[4], (DEPTH, D_MODEL, W_IN)) * D_MODEL ** -0.5,
        "rel_bias": nrm(ks[5], (DEPTH, H_A, 2 * REL_CLIP + 1)) * 0.5,
        "g_a": 1.0 + 0.1 * nrm(ks[6], (DEPTH, W_A)),
        "g_b": 1.0 + 0.1 * nrm(ks[7], (DEPTH, W_B)),
        "w_out": nrm(ks[8], (DEPTH, W_MIX, D_MODEL)) * W_MIX ** -0.5,
        "w_up": nrm(ks[9], (DEPTH, D_MODEL, 2 * D_FF)) * D_MODEL ** -0.5,
        "conv_w": nrm(ks[10], (DEPTH, CONV_WIDTH, 2 * D_FF)) * CONV_WIDTH ** -0.5,
        "conv_b": nrm(ks[11], (DEPTH, 2 * D_FF)) * 0.02,
        "w_down": nrm(ks[12], (DEPTH, D_FF, D_MODEL)) * D_FF ** -0.5,
        "final_g": 1.0 + 0.1 * nrm(ks[13], (D_MODEL,)),
    }

def second_block(x, c, w_ada, b_ada, w_in, rel_bias, g_a, g_b, w_out, w_up, conv_w,
              conv_b, w_down, final_g):
    c_act = jax.nn.silu(c)
    for l in range(DEPTH):
        x = hybrid_layer(x, c_act, w_ada[l], b_ada[l], w_in[l], rel_bias[l], g_a[l], g_b[l],
                         w_out[l], w_up[l], conv_w[l], conv_b[l], w_down[l])
    return rms_norm(x) * final_g


def setup_inputs(seed=0):
    out = dict(first_inputs(seed))
    for name, value in second_inputs(seed + 1).items():
        if name != "x":
            out[name + "_2"] = value
    return out


def reference(
    x, c, w_ada, b_ada, w_in, ssd_conv_w, ssd_conv_b, ssd_dt_bias, ssd_A_log, ssd_D, ssd_norm_w,
    w_ssd_out, sc_conv_w, w_sc_out, w_o, ln1_g, ln1_b, router_w, router_bias, w_gate, w_up,
    w_down, sh_gate, sh_up, sh_down, ln2_g, ln2_b, c_2, w_ada_2, b_ada_2, w_in_2, rel_bias_2,
    g_a_2, g_b_2, w_out_2, w_up_2, conv_w_2, conv_b_2, w_down_2, final_g_2,
):
    x = first_block(
        x, c, w_ada, b_ada, w_in, ssd_conv_w, ssd_conv_b, ssd_dt_bias, ssd_A_log, ssd_D,
        ssd_norm_w, w_ssd_out, sc_conv_w, w_sc_out, w_o, ln1_g, ln1_b, router_w, router_bias,
        w_gate, w_up, w_down, sh_gate, sh_up, sh_down, ln2_g, ln2_b,
    )
    return second_block(
        x, c_2, w_ada_2, b_ada_2, w_in_2, rel_bias_2, g_a_2, g_b_2, w_out_2, w_up_2, conv_w_2,
        conv_b_2, w_down_2, final_g_2,
    )


_drawn_inputs = setup_inputs


def setup_inputs(seed=0):
    import zlib

    import numpy as np

    out = dict(_drawn_inputs(seed))
    spreads = {}
    factors = {'b_ada': 2.786, 'ssd_conv_b': 8.0, 'ssd_D': 8.0, 'ssd_norm_w': 3.783, 'conv_b_2': 5.254}
    for name, (base, spread) in spreads.items():
        noise = np.random.default_rng([zlib.crc32(name.encode()), seed]).standard_normal(out[name].shape)
        drawn = base * np.exp(spread * noise) if base else spread * noise
        out[name] = __import__('jax').numpy.asarray(drawn.astype(out[name].dtype))
    for name, factor in factors.items():
        out[name] = (out[name] * factor).astype(out[name].dtype)
    return out
```

```python
import concourse.bass as bass
from concourse import mybir
from contextlib import ExitStack

T = 256
NS = 8
ALPHA = 2.0 ** 0.25
N_EXP = 64

_PAR = {}


def par_columns():
    at = 0
    for name, n in (("b_ada", 48), ("cw", 128), ("cb", 32), ("D", 16), ("nw", 16), ("scw", 24),
                    ("ln1g", 8), ("ln1b", 8), ("ln2g", 8), ("ln2b", 8), ("b_ada2", 48), ("gab", 8),
                    ("cw2", 132), ("cb2", 44), ("fg", 8), ("c", 8), ("c2", 8)):
        _PAR[name] = (at, n)
        at += n
    return at


NPAR = par_columns()


class Queue:

    def __init__(self, sem):
        self.sem, self.count, self.items, self.seen = sem, 0, [], {}

    def wait(self, *tokens):
        for t in tokens:
            if t is None:
                continue
            if isinstance(t, list):
                self.wait(*t)
                continue
            sem, value = t
            if self.seen.get(sem.name, 0) < value:
                self.seen[sem.name] = value
                self.items.append(lambda e, s=sem, v=value: e.wait_ge(s, v))

    def do(self, fn, *tokens):
        self.wait(*tokens)
        self.count += 1
        self.items.append(lambda e, f=fn: f(e).then_inc(self.sem, 1))
        return (self.sem, self.count)

    def quiet(self, fn, *tokens):
        self.wait(*tokens)
        self.items.append(fn)

    def dma(self, out, in_, sem, value, *tokens):
        self.wait(*tokens)
        self.items.append(lambda e: e.dma_start(out, in_).then_inc(sem, 16))
        return (sem, value)

    def play(self, eng):
        for item in self.items:
            item(eng)


def build(nc, a, out):
    fp = mybir.dt.float32
    ALU = mybir.AluOpType
    ACT = mybir.ActivationFunctionType
    AX = mybir.AxisListType
    ctx = ExitStack()
    with ctx:
        def sb(name, shape):
            return ctx.enter_context(nc.sbuf_tensor(name, shape, fp))

        def sem(name):
            return ctx.enter_context(nc.semaphore(name))

        ring = [sb(f"ring{i}", [128, 2048]) for i in range(NS)]
        X = sb("X", [128, 8, T])
        H = sb("H", [128, 8, T])
        par = sb("par", [128, NPAR])
        mod = sb("mod", [128, 96])
        ones = sb("ones", [128, 128])
        ident = sb("ident", [128, 128])
        triU = sb("triU", [128, 128])
        triS = sb("triS", [128, 128])
        triG = sb("triG", [128, 128])
        small = sb("small", [128, 2048])
        wdt = sb("wdt", [128, 8, 32])
        wrt = sb("wrt", [128, 8, 64])
        rowb = sb("rowb", [128, 128])
        AR = sb("AR", [128, 108 * 256])
        bank = [ctx.enter_context(nc.psum_tensor(f"bank{i}", [128, 512], fp)) for i in range(8)]

        def arena(kb, n, cols=T):
            return AR[:, kb * 256:kb * 256 + n * cols].rearrange("p (n t) -> p n t", t=cols)

        s_pe, s_act, s_dve, s_pool = sem("s_pe"), sem("s_act"), sem("s_dve"), sem("s_pool")
        s_ring = [sem(f"s_ring{i}") for i in range(NS)]
        s_par, s_x, s_wdt, s_wrt, s_row, s_bias, s_out = (
            sem("s_par"), sem("s_x"), sem("s_wdt"), sem("s_wrt"), sem("s_row"), sem("s_bias"), sem("s_out"))
        PE, AC, DV, PO, SP = Queue(s_pe), Queue(s_act), Queue(s_dve), Queue(s_pool), Queue(None)

        def tt(q, o, x, y, op, *w):
            return q.do(lambda e: e.tensor_tensor(o, x, y, op), *w)

        def ts(q, o, x, s1, s2, op0, op1, *w):
            if s2 is None:
                return q.do(lambda e: e.tensor_scalar(o, x, s1, None, op0), *w)
            return q.do(lambda e: e.tensor_scalar(o, x, s1, s2, op0, op1), *w)

        def stt(o, x, s, y, op0, op1, *w):
            return DV.do(lambda e: e.scalar_tensor_tensor(out=o, in0=x, scalar=s, in1=y, op0=op0, op1=op1), *w)

        def act(o, x, f, *w, bias=0.0, scale=1.0, accum=None):
            if accum is not None:
                return AC.do(lambda e: e.activation(o, x, f, bias=bias, scale=scale, accum_out=accum), *w)
            return AC.do(lambda e: e.activation(o, x, f, bias=bias, scale=scale), *w)

        def mm(o, l, r, start, stop, *w, last=False, skip=False):
            f = lambda e: e.matmul(o, l, r, start=start, stop=stop, skip_group_check=skip)
            if last:
                return PE.do(f, *w)
            PE.quiet(f, *w)

        def tr(o, i, *w, last=False):
            k = i.shape[0]
            f = lambda e: e.transpose(o, i, ident[0:k, 0:k])
            if last:
                return PE.do(f, *w)
            PE.quiet(f, *w)

        normed = []
        free = [[] for _ in range(8)]
        stream = []

        def tile_in(src):
            n = len(stream)
            stream.append([src, None])
            PE.wait((s_ring[n % NS], 16 * (n // NS + 1)))
            return ring[n % NS]

        def tile_used(tok):
            stream[-1][1] = tok

        def P(name, i=0, n=1):
            at = _PAR[name][0] + i
            return par[:, at:at + n]

        t_par = AC.dma(par[:, :], a["par"], s_par, 16)
        t_x = AC.dma(X[:, :, :], a["xT"], s_x, 16)
        t_wdt = AC.dma(wdt[:, :, :], a["wdt"], s_wdt, 16)
        AC.dma(rowb[:, 0:32], a["dtb"].partition_broadcast(128), s_row, 16)
        AC.dma(rowb[:, 32:64], a["alog"].partition_broadcast(128), s_row, 32)
        t_row = AC.dma(rowb[:, 64:128], a["rb"].partition_broadcast(128), s_row, 48)
        t_wrt = AC.dma(wrt[:, :, :], a["wrt"], s_wrt, 16)

        t_ones = PO.do(lambda e: e.memset(ones[:, :], 1.0))
        t_z = PO.do(lambda e: e.memset(ident[:, :], 0.0))
        t_id = PO.do(lambda e: e.affine_select(out=ident[:, :], in_=ident[:, :], compare_op=ALU.not_equal,
                     fill=1.0, base=0, pattern=[[-1, 128]], channel_multiplier=1), t_z)
        def tri(dst, step, base):
            return PO.do(lambda e: e.affine_select(out=dst[:, :], in_=ones[:, :], compare_op=ALU.is_ge,
                         fill=0.0, base=base, pattern=[[step, 128]], channel_multiplier=-step), t_ones)
        t_triU = tri(triU, 1, 0)
        t_triS = tri(triS, 1, -1)
        t_triG = tri(triG, -1, 0)
        t_const = t_triG

        t_sc = act(small[:, 0:16], P("c", 0, 16), ACT.Silu, t_par)
        PE.wait(t_sc)
        t_mod = {}

        def ada_tile(which, i, b):
            w = tile_in(a["ada2" if which else "ada"][i])
            PE.wait(free[b])
            for c in range(2):
                for k in range(8):
                    j = (c * 8 + k) * 128
                    tok = mm(bank[b][:, c:c + 1], w[:, j:j + 128], small[:, which * 8 + k:which * 8 + k + 1],
                             k == 0, k == 7, last=(c == 1 and k == 7))
            tile_used(tok)
            at = 48 * which + 2 * i
            t = tt(DV, mod[:, at:at + 2], bank[b][:, 0:2], P("b_ada2" if which else "b_ada", 2 * i, 2), ALU.add, tok)
            free[b] = [t]
            if (i % 24) // 4 in (1, 4) and (which, 1) is not None:
                t = ts(DV, mod[:, at:at + 2], mod[:, at:at + 2], 1.0, None, ALU.add, None, t)
            t_mod[which, i] = t
            return t

        def norm(S, Q, toks, b1, b2, center, rms_n, eps, chunks=8, q_free=()):
            n = chunks
            pairs = [slice(2 * p, 2 * p + 2) for p in range(n // 2)]
            done = list(toks)
            if center:
                for k in range(n):
                    tok = mm(bank[b1][:, 0:T], ones[:, :], S[:, k, :], k == 0, k == n - 1, t_ones, toks[k],
                             free[b1] if k == 0 else None, last=(k == n - 1))
                mean = bank[b1][:, 0:T].unsqueeze(1).to_broadcast([128, 2, T])
                done = []
                for p in pairs:
                    t = stt(S[:, p, :], mean, -1.0 / 1024.0, S[:, p, :], ALU.mult, ALU.add, tok)
                    done += [t, t]
                free[b1] = [done[-1]]
            for i, p in enumerate(pairs):
                t = act(Q[:, p, :], S[:, p, :], ACT.Square, done[2 * i], done[2 * i + 1], *(q_free if i == 0 else ()))
                for k in (2 * i, 2 * i + 1):
                    tok = mm(bank[b2][:, 0:T], ones[:, :], Q[:, k, :], k == 0, k == n - 1, t, t_ones,
                             free[b2] if k == 0 else None, last=(k == n - 1))
            r = small[:, 256:256 + T]
            t = ts(DV, r, bank[b2][:, 0:T], 1.0 / rms_n, eps, ALU.mult, ALU.add, tok, normed)
            free[b2] = [t]
            t = act(r, r, ACT.Sqrt, t)
            t = DV.do(lambda e: e.reciprocal(r, r), t)
            rb = r.unsqueeze(1).to_broadcast([128, 2, T])
            res = []
            for p in pairs:
                t = tt(DV, S[:, p, :], S[:, p, :], rb, ALU.mult, t)
                res += [t, t]
            normed[:] = [t]
            return res

        def affine(O, S, scale, bias, toks, *w):
            res = []
            for k in range(8):
                if k % 2:
                    res.append(act(O[:, k, :], S[:, k, :], ACT.Identity, toks[k], *w, bias=bias(k), scale=scale(k)))
                else:
                    res.append(ts(DV, O[:, k, :], S[:, k, :], scale(k), bias(k), ALU.mult, ALU.add, toks[k], *w))
            return res

        def M(i, which=0):
            return mod[:, 48 * which + i:48 * which + i + 1]

        def gemm(src, R, toks, b):
            w = tile_in(src)
            for c in range(2):
                for k in range(8):
                    j = (c * 8 + k) * 128
                    tok = mm(bank[b][:, c * T:c * T + T], w[:, j:j + 128], R[:, k, :], k == 0, k == 7,
                             free[b] if c == k == 0 else None, toks[k], last=(c == 1 and k == 7))
            tile_used(tok)
            free[b] = []
            return tok

        Q8 = arena(96, 8)
        for i in range(8):
            ada_tile(0, i, i % 2)
        XC = arena(0, 8)
        t_cp = [ts(DV, XC[:, 2 * p:2 * p + 2, :], X[:, 2 * p:2 * p + 2, :], 1.0, None, ALU.mult, None, t_x)
                for p in range(4)]
        t_ln = norm(XC, Q8, [t_cp[k // 2] for k in range(8)], 2, 3, True, 1024.0, 1e-5)
        t_h = affine(H, XC, lambda k: M(8 + k), lambda k: M(k), t_ln, t_mod[0, 3], t_mod[0, 7])

        dt = small[:, 512:576]
        e1 = small[:, 576:640]
        u1 = small[:, 640:704]
        r1 = small[:, 704:768]
        dA = small[:, 768:832]
        acsT = small[:, 832:896]
        dec = small[:, 896:928]
        dtd = small[:, 928:960]
        acsF = small[0:32, 1024:1280]
        for t in range(2):
            for k in range(8):
                tok = mm(bank[2][:, t * 32:t * 32 + 32], H[:, k, t * 128:t * 128 + 128], wdt[:, k, :],
                         k == 0, k == 7, t_wdt, t_h[k], free[2], last=(t == 1 and k == 7))
        v2 = lambda x: x.rearrange("p (t h) -> p t h", t=2)
        t0 = tt(DV, v2(dt), v2(bank[2][:, 0:64]), rowb[:, 0:32].unsqueeze(1).to_broadcast([128, 2, 32]),
                ALU.add, tok, t_row)
        free[2] = [t0]
        t1 = act(e1, dt, ACT.Abs, t0)
        t1 = act(e1, e1, ACT.Exp, t1, scale=-1.0)
        t_A = act(small[:, 960:992], rowb[:, 32:64], ACT.Exp, t_row)
        t2 = ts(DV, u1, e1, 1.0, None, ALU.add, None, t1)
        t3 = act(r1, u1, ACT.Ln, t2)
        t4 = stt(e1, u1, -1.0, e1, ALU.add, ALU.subtract, t2)
        t5 = DV.do(lambda e: e.reciprocal(u1, u1), t3, t4)
        t5 = tt(DV, e1, e1, u1, ALU.mult, t5)
        t5 = tt(DV, r1, r1, e1, ALU.subtract, t5, t3)
        t5 = stt(dt, dt, 0.0, r1, ALU.max, ALU.add, t5)
        t_dt = t5
        t6 = stt(v2(dA), v2(dt), -1.0, small[:, 960:992].unsqueeze(1).to_broadcast([128, 2, 32]),
                 ALU.mult, ALU.mult, t5, t_A)
        for c in range(2):
            mm(bank[3][:, c * 32:c * 32 + 32], triU[:, :], dA[:, c * 32:c * 32 + 32], True, True, t_const, t6, free[3])
        tok = mm(bank[3][:, 64:96], ones[:, :], dA[:, 0:32], True, True, last=True)
        for c in range(2):
            tokF = mm(bank[2][0:32, c * 128:c * 128 + 128], dA[:, c * 32:c * 32 + 32], triU[:, :], True, True,
                      free[2], last=(c == 1))
        t7 = DV.do(lambda e: e.tensor_copy(acsT, bank[3][:, 0:64]), tok)
        t8 = tt(DV, dec, bank[3][:, 64:96], acsT[:, 0:32], ALU.subtract, t7)
        free[3] = [t8]
        t8 = act(dec, dec, ACT.Exp, t8)
        t_dtd = tt(DV, dtd, dt[:, 0:32], dec, ALU.mult, t8)
        t_acs = DV.do(lambda e: e.tensor_copy(acsF, bank[2][0:32, 0:256]), tokF)
        free[2] = [t_acs]
        t_acsT = t7

        XS, Z, BB, CC = arena(0, 16), arena(16, 16), arena(32, 8), arena(40, 8)

        def conv(o, x, cw, n, K, at, bias, tok):
            if bias is None:
                t = ts(DV, o, x, P(cw, (K - 1) * n + at), None, ALU.mult, None, tok)
            else:
                t = ts(DV, o, x, P(cw, (K - 1) * n + at), bias, ALU.mult, ALU.add, tok)
            for s in range(1, K):
                t = stt(o[:, s:T], x[:, 0:T - s], P(cw, (K - 1 - s) * n + at), o[:, s:T], ALU.mult, ALU.add, t)
            return t

        nb = [0]

        def next_bank():
            nb[0] ^= 1
            return nb[0]

        def xbc_tile(i, dst, at, chunk, *w):
            b = next_bank()
            tok = gemm(a["w_in"][i], H, t_h, b)
            res = []
            for c in range(2):
                t = conv(dst[:, at + c, :], bank[b][:, c * T:c * T + T], "cw", 32, 4, chunk + c,
                         P("cb", chunk + c), [tok, *w])
                res.append(t)
            free[b] = [t]
            t = act(dst[:, at:at + 2, :], dst[:, at:at + 2, :], ACT.Silu, *res)
            return t

        t_B, t_C, t_XS = {}, {}, {}
        for i in range(4):
            t_B[i] = xbc_tile(i, BB, 2 * i, 16 + 2 * i)
        for i in range(4):
            t_C[i] = xbc_tile(4 + i, CC, 2 * i, 24 + 2 * i)
        for g in range(8):
            t_XS[g] = xbc_tile(8 + g, XS, 2 * g, 2 * g, t_h)

        SCB, U = arena(48, 8), arena(56, 8)
        t_z = [None] * 8
        t_u = [None] * 8

        def z_tile(i):
            b = next_bank()
            tok = gemm(a["w_in"][16 + i], H, t_h, b)
            t_z[i] = act(Z[:, 2 * i:2 * i + 2, :], bank[b][:, :].rearrange("p (n t) -> p n t", n=2), ACT.Copy, tok)
            free[b] = [t_z[i]]

        sc_tmp = arena(104, 2)

        def sc_tile(j):
            b = next_bank()
            tok = gemm(a["w_in"][24 + j], H, t_h, b)
            prev = t_u[j - 1] if j else None
            t1 = act(sc_tmp[:, 0, :], bank[b][:, 0:T], ACT.Copy, tok, prev)
            t2 = tt(DV, sc_tmp[:, 1, :], bank[b][:, T:2 * T], sc_tmp[:, 0, :], ALU.mult, t1)
            free[b] = [t2]
            t_u[j] = conv(U[:, j, :], sc_tmp[:, 1, :], "scw", 8, 3, j, None, t2)

        def scb_tile(i):
            b = next_bank()
            tok = gemm(a["w_in"][32 + i], H, t_h, b)
            t = tt(DV, U[:, 2 * i:2 * i + 2, :], U[:, 2 * i:2 * i + 2, :],
                   bank[b][:, :].rearrange("p (n t) -> p n t", n=2), ALU.mult, tok, t_u[2 * i], t_u[2 * i + 1])
            free[b] = [t]
            t_u[2 * i] = t_u[2 * i + 1] = t

        fill = []
        main = [lambda i=i: z_tile(i) for i in range(8)] + [lambda j=j: sc_tile(j) for j in range(8)] \
            + [lambda i=i: scb_tile(i) for i in range(4)]
        adas = [lambda i=i: ada_tile(0, i, next_bank()) for i in range(8, 24)] \
            + [lambda i=i: ada_tile(1, i, next_bank()) for i in range(24)]
        for n, m in enumerate(main):
            fill.append((m, adas[2 * n], adas[2 * n + 1]))

        def filler():
            if fill:
                for f in fill.pop(0):
                    f()

        scr = [arena(64, 16), arena(80, 16)]
        t_Y = [None] * 8
        prevY = {}
        for g in range(8):
            S = AR[:, (64 + 16 * (g % 2)) * 256:(80 + 16 * (g % 2)) * 256]
            Xdt, Xd, BT = S[:, 0:512], S[:, 512:768], S[:, 768:896]
            CBm, D = S[:, 896:1152], S[:, 1152:2176]
            CE, PV = S[:, 2176:2688], S[:, 2688:2944]
            RM = S[0:32, 2944:3968]
            old = prevY.get(g - 2)
            r3 = lambda x, n: x.rearrange("p (n t) -> p n t", n=n)
            for c in range(2):
                tR = tt(PO, r3(RM[:, c * 512:c * 512 + 512], 4),
                        acsF[:, c * 128:c * 128 + 128].unsqueeze(1).to_broadcast([32, 4, 128]),
                        ident[0:32, 4 * g:4 * g + 4].unsqueeze(2).to_broadcast([32, 4, 128]), ALU.mult,
                        t_acs, t_id, old)
            PE.wait(free[2], free[3], t_XS[g], t_B[g // 2], t_C[g // 2], t_id)
            for t in range(2):
                for j in range(2):
                    tX = tr(bank[2][:, (2 * t + j) * 128:(2 * t + j) * 128 + 128],
                            XS[:, 2 * g + j, t * 128:t * 128 + 128], last=(t == j == 1))
            tr(bank[3][:, 0:128], BB[:, g, 0:128])
            for c in range(2):
                tC = mm(bank[3][:, 128 + c * 128:256 + c * 128], BB[:, g, c * 128:c * 128 + 128],
                        CC[:, g, c * 128:c * 128 + 128], True, True, last=(c == 1))
            for c in range(2):
                tS = mm(bank[4 + c][:, :], ones[0:32, :], RM[:, c * 512:c * 512 + 512], True, True,
                        tR, free[4 + c], last=(c == 1))
            tBT = act(BT, bank[3][:, 0:128], ACT.Copy, tC, old)
            tE = act(CE, bank[5][:, :], ACT.Exp, tS)
            t1 = tt(DV, Xdt.rearrange("p (t r q) -> p t r q", t=2, r=4),
                    bank[2][:, :].rearrange("p (t r q) -> p t r q", t=2, r=4),
                    v2(dt)[:, :, 4 * g:4 * g + 4].unsqueeze(3).to_broadcast([128, 2, 4, 64]), ALU.mult, tX, t_dt, old)
            t1b = tt(DV, r3(Xd, 4), r3(bank[2][:, 0:256], 4),
                     dtd[:, 4 * g:4 * g + 4].unsqueeze(2).to_broadcast([128, 4, 64]), ALU.mult, t_dtd)
            free[2] = [t1b]
            t2 = tt(DV, r3(CBm, 2), r3(bank[3][:, 128:384], 2),
                    triU[:, :].unsqueeze(1).to_broadcast([128, 2, 128]), ALU.mult, tC, tBT, t_const)
            free[3] = [t2, tBT]
            for c in range(2):
                for r in range(4):
                    o = c * 512 + r * 128
                    t3 = ts(DV, D[:, o:o + 128], bank[4 + c][:, r * 128:r * 128 + 128],
                            acsT[:, c * 32 + 4 * g + r:c * 32 + 4 * g + r + 1], 0.0, ALU.subtract, ALU.min,
                            tS, tE, t_acsT)
                free[4 + c] = [t3]
                t3 = act(D[:, c * 512:c * 512 + 512], D[:, c * 512:c * 512 + 512], ACT.Exp, t3)
                tD = tt(DV, r3(D[:, c * 512:c * 512 + 512], 4), r3(D[:, c * 512:c * 512 + 512], 4),
                        CBm[:, c * 128:c * 128 + 128].unsqueeze(1).to_broadcast([128, 4, 128]), ALU.mult, t3, t2)
            tCE = tt(PO, r3(CE, 4), r3(CE, 4), CC[:, g, 128:256].unsqueeze(1).to_broadcast([128, 4, 128]),
                     ALU.mult, tE)
            filler()
            tok = mm(bank[6][:, 0:256], BT, Xd, True, True, tBT, t1b, free[6], last=True)
            tPV = act(PV, bank[6][:, 0:256], ACT.Copy, tok)
            free[6] = [tPV]
            filler()
            PE.wait(tPV, tD, tCE, t1, free[7])
            for j in range(2):
                for h in range(2):
                    r = 2 * j + h
                    o = bank[7][h * 64:h * 64 + 64, j * T:j * T + T]
                    mm(o[:, 0:128], Xdt[:, r * 64:r * 64 + 64], D[:, r * 128:r * 128 + 128], True, True)
                    mm(o[:, 128:256], Xdt[:, 256 + r * 64:256 + r * 64 + 64],
                       D[:, 512 + r * 128:512 + r * 128 + 128], True, False)
                    tok = mm(o[:, 128:256], PV[:, r * 64:r * 64 + 64], CE[:, r * 128:r * 128 + 128],
                             False, True, last=(r == 3))
            for j in range(2):
                t = stt(XS[:, 2 * g + j, :], XS[:, 2 * g + j, :], P("D", 2 * g + j), bank[7][:, j * T:j * T + T],
                        ALU.mult, ALU.add, tok)
            free[7] = [t]
            t_Y[g] = t
            prevY[g] = [t, tok]
            filler()
        while fill:
            filler()

        GA, GB = BB, CC
        t_g = []
        for i in range(8):
            b = next_bank()
            tok = gemm(a["w_in"][36 + i], H, t_h, b)
            dst = (GA if i < 4 else GB)[:, 2 * (i % 4):2 * (i % 4) + 2, :]
            t = act(dst, bank[b][:, :].rearrange("p (n t) -> p n t", n=2), ACT.Sigmoid, tok, t_Y[7], tCE)
            free[b] = [t]
            t_g.append(t)

        for p in range(4):
            t_sz = act(Z[:, 4 * p:4 * p + 4, :], Z[:, 4 * p:4 * p + 4, :], ACT.Silu, t_z[2 * p], t_z[2 * p + 1])
            t_z[2 * p] = t_z[2 * p + 1] = t_sz
        GQ = [arena(96, 2), arena(98, 2)]
        rs = [small[:, 1280:1536], small[:, 1536:1792]]
        t_gq, t_yn, t_rs = {}, {}, {}
        for g in range(8):
            sl = slice(2 * g, 2 * g + 2)
            t = tt(DV, XS[:, sl, :], XS[:, sl, :], Z[:, sl, :], ALU.mult, t_Y[g], t_z[g])
            t = act(GQ[g % 2], XS[:, sl, :], ACT.Square, t, t_gq.get(g - 2))
            b = 2 + g % 2
            for k in range(2):
                tok = mm(bank[b][:, 0:T], ones[:, :], GQ[g % 2][:, k, :], k == 0, k == 1, t, free[b], last=(k == 1))
            t_gq[g] = tok
            r = rs[g % 2]
            t = ts(DV, r, bank[b][:, 0:T], 1.0 / 256.0, 1e-5, ALU.mult, ALU.add, tok, t_rs.get(g - 2))
            free[b] = [t]
            t = act(r, r, ACT.Sqrt, t)
            t = DV.do(lambda e, r=r: e.reciprocal(r, r), t)
            for k in range(2):
                t = stt(XS[:, 2 * g + k, :], XS[:, 2 * g + k, :], P("nw", 2 * g + k), r, ALU.mult, ALU.mult, t)
            t_rs[g] = t
            t_yn[2 * g] = t_yn[2 * g + 1] = t

        t_m = [None] * 8
        for i in range(4):
            b = next_bank()
            for c in range(2):
                w = tile_in(a["ssd_out"][2 * i + c])
                for k in range(16):
                    tok = mm(bank[b][:, c * T:c * T + T], w[:, k * 128:k * 128 + 128], XS[:, k, :],
                             k == 0, k == 15, free[b], t_yn[k], last=(k == 15))
                tile_used(tok)
            t = tt(DV, GA[:, 2 * i:2 * i + 2, :], GA[:, 2 * i:2 * i + 2, :],
                   bank[b][:, :].rearrange("p (n t) -> p n t", n=2), ALU.mult, tok, t_g[i])
            free[b] = [t]
            b = next_bank()
            tok = gemm(a["sc_out"][i], U, t_u, b)
            t = tt(DV, GB[:, 2 * i:2 * i + 2, :], GB[:, 2 * i:2 * i + 2, :],
                   bank[b][:, :].rearrange("p (n t) -> p n t", n=2), ALU.mult, tok, t_g[4 + i], t)
            free[b] = [t]
            t = tt(DV, GA[:, 2 * i:2 * i + 2, :], GA[:, 2 * i:2 * i + 2, :], GB[:, 2 * i:2 * i + 2, :], ALU.add, t)
            t_m[2 * i] = t_m[2 * i + 1] = t
        for k in range(8):
            t_xa = ts(DV, X[:, k, :], X[:, k, :], ALPHA, None, ALU.mult, None, t_cp[3])

        def residual(tok, b, i, gcol, which):
            for c in range(2):
                t = stt(X[:, 2 * i + c, :], bank[b][:, c * T:c * T + T], M(gcol + 2 * i + c, which),
                        X[:, 2 * i + c, :], ALU.mult, ALU.add, tok)
            free[b] = [t]
            return [t, t]

        t_x1 = []
        for i in range(4):
            b = next_bank()
            tok = gemm(a["w_o"][i], GA, t_m, b)
            t_x1 += residual([tok, t_xa, t_mod[0, 11]], b, i, 16, 0)
        t_ln = norm(X, Q8, t_x1, 2, 3, True, 1024.0, 1e-5)
        t_x1 = affine(X, X, lambda k: P("ln1g", k), lambda k: P("ln1b", k), t_ln)
        XC = arena(88, 8)
        t_cp = [DV.do(lambda e, k=k, XC=XC: e.tensor_copy(XC[:, k, :], X[:, k, :]), t_x1[k]) for k in range(8)]
        t_ln = norm(XC, Q8, t_cp, 2, 3, True, 1024.0, 1e-5)
        t_h = affine(H, XC, lambda k: M(32 + k), lambda k: M(24 + k), t_ln, t_mod[0, 15], t_mod[0, 19])
        for k in range(8):
            t_xa = ts(DV, X[:, k, :], X[:, k, :], ALPHA, None, ALU.mult, None, t_cp[k])

        for t in range(2):
            for k in range(8):
                tok = mm(bank[2][:, t * 64:t * 64 + 64], H[:, k, t * 128:t * 128 + 128], wrt[:, k, :],
                         k == 0, k == 7, t_wrt, t_h[k], free[2], last=(t == 1 and k == 7))
        sc = small[:, 256 + 256:256 + 384]
        bi = small[:, 640:768]
        m8 = small[:, 768:896]
        gs = small[:, 896:912]
        rk = small[:, 912:928]
        rk2 = small[:, 928:944]
        lt = small[:, 1024:1088]
        cmpb = small[:, 1088:1216]
        v8 = small[:, 944:960]
        rep = small[:, 1280:1408]
        gate = small[:, 1408:1536]
        s1 = small[:, 960:962]
        v3 = lambda x: x.rearrange("p (t g h) -> p t g h", t=2, g=8)
        t = PO.do(lambda e: e.memset(lt, 1.0), t_acs, t_rs[7])
        t_lt = PO.do(lambda e: e.affine_select(out=lt, in_=lt, compare_op=ALU.is_ge, fill=0.0, base=-1,
                     pattern=[[1, 8], [-1, 8]], channel_multiplier=0), t)
        t0 = act(sc, bank[2][:, 0:128], ACT.Sigmoid, tok)
        free[2] = [t0]
        t0 = tt(DV, v2(bi), v2(sc), rowb[:, 64:128].unsqueeze(1).to_broadcast([128, 2, 64]), ALU.add, t0)
        for t in range(2):
            for g in range(8):
                o = (t * 8 + g) * 8
                t1 = DV.do(lambda e, o=o: e.max(m8[:, o:o + 8], bi[:, o:o + 8]), t0)
        m8v = m8.rearrange("p (n k) -> p n k", k=8)
        t1 = tt(DV, gs.unsqueeze(2), m8v[:, :, 0:1], m8v[:, :, 1:2], ALU.add, t1)
        gsv = gs.rearrange("p (t g) -> p t g", t=2)
        inner = gsv.unsqueeze(2).to_broadcast([128, 2, 8, 8])
        outer = gsv.unsqueeze(3).to_broadcast([128, 2, 8, 8])
        t2 = tt(DV, v3(cmpb), inner, outer, ALU.is_gt, t1)
        t2 = DV.do(lambda e: e.tensor_reduce(rk, cmpb.rearrange("p (n k) -> p n k", k=8), AX.X, ALU.add), t2)
        t3 = tt(DV, v3(cmpb), inner, outer, ALU.is_equal, t2)
        t3 = tt(DV, v3(cmpb), v3(cmpb), lt.rearrange("p (g h) -> p g h", g=8).unsqueeze(1)
                .to_broadcast([128, 2, 8, 8]), ALU.mult, t3, t_lt)
        t3 = DV.do(lambda e: e.tensor_reduce(rk2, cmpb.rearrange("p (n k) -> p n k", k=8), AX.X, ALU.add), t3)
        t3 = tt(DV, rk, rk, rk2, ALU.add, t3, t2)
        t3 = ts(DV, rk, rk, 3.5, None, ALU.is_lt, None, t3)
        t3 = ts(DV, rk, rk, -1.0, 1e30, ALU.add, ALU.mult, t3)
        t3 = tt(DV, bi.rearrange("p (n k) -> p n k", k=8), bi.rearrange("p (n k) -> p n k", k=8),
                rk.unsqueeze(2).to_broadcast([128, 16, 8]), ALU.add, t3)
        for t in range(2):
            bt, vt, rt = bi[:, t * 64:t * 64 + 64], v8[:, t * 8:t * 8 + 8], rep[:, t * 64:t * 64 + 64]
            t4 = DV.do(lambda e, bt=bt, vt=vt: e.max(vt, bt), t3)
            t4 = DV.do(lambda e, bt=bt, vt=vt, rt=rt: e.match_replace(rt, vt, bt, -3e30), t4)
            t4 = ts(DV, rt, rt, -2e30, None, ALU.is_lt, None, t4)
            gt = gate[:, t * 64:t * 64 + 64]
            t4 = tt(DV, gt, rt, sc[:, t * 64:t * 64 + 64], ALU.mult, t4)
            t4 = DV.do(lambda e, t=t, gt=gt: e.tensor_reduce(s1[:, t:t + 1], gt, AX.X, ALU.add), t4)
            t4 = DV.do(lambda e, t=t: e.reciprocal(s1[:, t:t + 1], s1[:, t:t + 1]), t4)
            t_gate = ts(DV, gt, gt, s1[:, t:t + 1], 2.5, ALU.mult, ALU.mult, t4)

        HID = [arena(64 + 2 * i, 2) for i in range(4)]
        SG = [arena(72 + 2 * i, 2) for i in range(2)]
        GATES = arena(0, 64)
        t_hid, t_down, t_sg = {}, {}, {}
        t_GB = [None] * N_EXP

        def up_part(n, gsrc, usrc):
            b0, b1 = (0, 1) if n % 2 == 0 else (2, 3)
            tg = gemm(gsrc, H, t_h, b0)
            tu = gemm(usrc, H, t_h, b1)
            t = act(SG[n % 2], bank[b0][:, :].rearrange("p (n t) -> p n t", n=2), ACT.Silu, tg, t_hid.get(n - 2))
            free[b0] = [t]
            t = tt(DV, HID[n % 4], bank[b1][:, :].rearrange("p (n t) -> p n t", n=2), SG[n % 2], ALU.mult,
                   t, tu, t_down.get(n - 4))
            free[b1] = [t]
            if n > 0:
                t = tt(PO, HID[n % 4], HID[n % 4], GATES[:, n - 1, :].unsqueeze(1).to_broadcast([128, 2, T]),
                       ALU.mult, t, t_GB[n - 1])
            t_hid[n] = t

        def down_part(n, src):
            w = tile_in(src)
            PE.wait(t_hid[n])
            for j in range(8):
                for i in range(2):
                    o = bank[4 + j // 2][:, (j % 2) * T:(j % 2) * T + T]
                    tok = mm(o, w[:, (2 * j + i) * 128:(2 * j + i) * 128 + 128], HID[n % 4][:, i, :],
                             n == 0 and i == 0 and j % 2 == 0, n == N_EXP and i == 1 and j % 2 == 1,
                             free[4 + j // 2] if n == 0 else None, last=(j == 7 and i == 1), skip=True)
            tile_used(tok)
            t_down[n] = tok
            return tok

        up_part(0, a["sh_gate"][0], a["sh_up"][0])
        gT = small[0:64, 0:256]
        gT = small[0:64, 1792:2048]
        for t in range(2):
            tok = tr(bank[2][0:64, t * 128:t * 128 + 128], gate[:, t * 64:t * 64 + 64], t_gate, free[2], t_id,
                     last=(t == 1))
        t_gT = DV.do(lambda e: e.tensor_copy(gT, bank[2][0:64, 0:256]), tok)
        free[2] = [t_gT]
        GM = [small[0:64, 256:512], small[0:64, 1024:1280]]
        t_gm = {}
        for e_ in range(N_EXP):
            b = 2 + e_ % 2
            t = ts(DV, GM[e_ % 2], gT, ident[0:64, e_:e_ + 1], None, ALU.mult, None, t_gT, t_gm.get(e_ - 2), t_gate)
            tok = mm(bank[b][:, 0:T], ones[0:64, :], GM[e_ % 2], True, True, t, free[b], last=True)
            t_gm[e_] = tok
            t_GB[e_] = act(GATES[:, e_, :], bank[b][:, 0:T], ACT.Copy, tok, t_m, t_ln)
            free[b] = [t_GB[e_]]
        for n in range(1, N_EXP + 1):
            up_part(n, a["w_gate"][n - 1], a["w_up"][n - 1])
            down_part(n - 1, a["w_down"][n - 2] if n > 1 else a["sh_down"][0])
        tok = down_part(N_EXP, a["w_down"][N_EXP - 1])
        t_x2 = []
        for i in range(4):
            t_x2 += residual([tok, t_xa, t_mod[0, 23]], 4 + i, i, 40, 0)
        t_ln = norm(X, Q8, t_x2, 2, 3, True, 1024.0, 1e-5)
        t_x2 = affine(X, X, lambda k: P("ln2g", k), lambda k: P("ln2b", k), t_ln)

        XC = arena(0, 8)
        t_cp = [DV.do(lambda e, k=k, XC=XC: e.tensor_copy(XC[:, k, :], X[:, k, :]), t_x2[k], t_hid[N_EXP]) for k in range(8)]
        t_ln = norm(XC, Q8, t_cp, 2, 3, False, 1024.0, 1e-6)
        t_h = affine(H, XC, lambda k: M(8 + k, 1), lambda k: M(k, 1), t_ln, t_mod[1, 3], t_mod[1, 7], tok)

        BIAS = arena(84, 8, 384)
        t_bias = SP
        t_bias = AC.dma(BIAS, a["relb"], s_bias, 16, t_ln)
        for o in (0, 256):
            t_bias = PO.do(lambda e, o=o: e.memset(BIAS[0:64, :, o + 64:o + 128], -1e30), t_bias)
        QK = arena(8, 16)
        VV = arena(24, 4, 512)
        t_qk = {}
        for i in range(8):
            b = next_bank()
            tok = gemm(a["qk"][i], H, t_h, b)
            t = act(QK[:, 2 * i:2 * i + 2, :], bank[b][:, :].rearrange("p (n t) -> p n t", n=2), ACT.Copy, tok)
            free[b] = [t]
            t_qk[2 * i] = t_qk[2 * i + 1] = t
        t_v = {}
        for sec in range(2):
            for half in range(2):
                w = tile_in(a["vv"][2 * sec + half])
                for t in range(2):
                    for k in range(4):
                        kk = 4 * half + k
                        tok = mm(bank[4 + t][:, :], H[:, kk, t * 128:t * 128 + 128], w[:, k * 512:k * 512 + 512],
                                 kk == 0, kk == 7, t_h[kk], free[4 + t] if kk == 0 else None,
                                 last=(k == 3))
                    if half == 1:
                        t_v[sec, t] = DV.do(lambda e, sec=sec, t=t: e.tensor_copy(
                            VV[:, 2 * sec + t, :], bank[4 + t][:, :]), tok)
                        free[4 + t] = [t_v[sec, t]]
                tile_used(tok)

        OA, OB = arena(32, 4), arena(36, 4)
        SB = [arena(40 + 6 * i, 1, 384)[:, 0, :] for i in range(2)]
        PT = [arena(42 + 6 * i, 1, 384)[:, 0, :] for i in range(2)]
        ZB = [arena(52 + 8 * i, 1, 384)[:, 0, :] for i in range(2)]
        EB = [arena(54 + 8 * i, 1, 384)[:, 0, :] for i in range(2)]
        SPB = [arena(56 + 8 * i, 1, 384)[:, 0, :] for i in range(2)]
        nm = [small[:, 512 + 8 * i:520 + 8 * i] for i in range(2)]
        MK = arena(68, 1, 384)[:, 0, :]
        for o, s in ((0, triS), (128, ones), (256, triS)):
            t_mk = PO.do(lambda e, o=o, s=s: e.tensor_copy(MK[:, o:o + 128], s[:, :]), t_const, t_hid[N_EXP])
        ta, tb = {}, {}

        def a_scores(h):
            r0, cq = (h % 2) * 64, h // 2
            q, k = QK[r0:r0 + 64, cq, :], QK[r0:r0 + 64, 4 + cq, :]
            PE.wait(t_qk[cq], t_qk[4 + cq], free[2])
            mm(bank[2][:, 0:128], q[:, 0:128], k[:, 0:128], True, True)
            tok = mm(bank[2][:, 128:384], q[:, 128:256], k[:, 0:256], True, True, last=True)
            S, n = SB[h % 2], nm[h % 2]
            t = stt(S, bank[2][:, 0:384], 0.125, BIAS[:, h, :], ALU.mult, ALU.add, tok, t_bias, ta.get(("pt", h - 2)))
            free[2] = [t]
            DV.do(lambda e: e.tensor_reduce(n[:, 0:1], S[:, 0:128], AX.X, ALU.max), t)
            t = DV.do(lambda e: e.tensor_reduce(n[:, 1:2], S[:, 128:384], AX.X, ALU.max), t)
            t = ts(DV, n[:, 2:4], n[:, 0:2], -1.0, None, ALU.mult, None, t)
            act(S[:, 0:128], S[:, 0:128], ACT.Exp, t, bias=n[:, 2:3], accum=n[:, 4:5])
            t = act(S[:, 128:384], S[:, 128:384], ACT.Exp, t, bias=n[:, 3:4], accum=n[:, 5:6])
            t = DV.do(lambda e: e.reciprocal(n[:, 6:8], n[:, 4:6]), t)
            ts(DV, S[:, 0:128], S[:, 0:128], n[:, 6:7], None, ALU.mult, None, t)
            ta["p", h] = ts(DV, S[:, 128:384], S[:, 128:384], n[:, 7:8], None, ALU.mult, None, t)

        def a_turn(h):
            PE.wait(ta["p", h], free[3], t_id)
            for i in range(3):
                tok = tr(bank[3][:, i * 128:i * 128 + 128], SB[h % 2][:, i * 128:i * 128 + 128], last=(i == 2))
            ta["pt", h] = tok
            t = act(PT[h % 2], bank[3][:, 0:384], ACT.Copy, tok, ta.get(("o", h - 2)))
            free[3] = [t]
            ta["c", h] = t

        def a_out(h):
            r0, b = (h % 2) * 64, 6
            PE.wait(ta["c", h], t_v[0, 0], t_v[0, 1], free[b] if h % 2 == 0 else None)
            o = bank[b][r0:r0 + 64, 0:T]
            mm(o, VV[:, 0, h * 64:h * 64 + 64], PT[h % 2][:, 0:256], True, False)
            tok = mm(o[:, 128:256], VV[:, 1, h * 64:h * 64 + 64], PT[h % 2][:, 256:384], False, True, last=True)
            ta["o", h] = tok
            if h % 2:
                t = act(OA[:, h // 2, :], bank[b][:, 0:T], ACT.Copy, tok)
                free[b] = [t]
                ta["e", h // 2] = t

        def b_scores(h):
            r0, cq = (h % 2) * 64, h // 2
            q, k = QK[r0:r0 + 64, 8 + cq, :], QK[r0:r0 + 64, 12 + cq, :]
            PE.wait(t_qk[8 + cq], t_qk[12 + cq], free[4])
            mm(bank[4][:, 0:256], k[:, 0:128], q[:, 0:256], True, True)
            tok = mm(bank[4][:, 256:384], k[:, 128:256], q[:, 128:256], True, True, last=True)
            Zb, E, S = ZB[h % 2], EB[h % 2], SPB[h % 2]
            t = act(Zb, bank[4][:, 0:384], ACT.Copy, tok, tb.get(("w", h - 2)), scale=0.125)
            free[4] = [t]
            t1 = act(E, Zb, ACT.Abs, t, tb.get(("o", h - 2)))
            t1 = act(E, E, ACT.Exp, t1, scale=-1.0)
            t1 = act(E, E, ACT.Ln, t1, bias=1.0)
            t2 = stt(S, Zb, 0.0, E, ALU.max, ALU.add, t1, tb.get(("r", h - 2)))
            tb["s", h] = tt(PO, S, S, MK, ALU.mult, t2, t_mk)

        def b_tail(h):
            Zb, E, S = ZB[h % 2], EB[h % 2], SPB[h % 2]
            PE.wait(tb["s", h], free[5], t_const)
            mm(bank[5][:, 0:256], triG[:, :], S[:, 0:256], True, False)
            mm(bank[5][:, 128:256], ones[:, :], S[:, 256:384], False, True)
            tok = mm(bank[5][:, 256:384], triG[:, :], S[:, 256:384], True, True, last=True)
            tb["r", h] = tok
            t = tt(DV, Zb, Zb, bank[5][:, 0:384], ALU.subtract, tok)
            free[5] = [t]
            t = ts(DV, Zb, Zb, 0.0, None, ALU.min, None, t)
            t = act(E, Zb, ACT.Exp, t)
            tb["w", h] = t
            tb["m", h] = tt(PO, E, E, MK, ALU.mult, t)

        def b_out(h):
            r0, b = (h % 2) * 64, 7
            PE.wait(tb["m", h], t_v[1, 0], t_v[1, 1], free[b] if h % 2 == 0 else None)
            o = bank[b][r0:r0 + 64, 0:T]
            mm(o, VV[:, 2, h * 64:h * 64 + 64], EB[h % 2][:, 0:256], True, False)
            tok = mm(o[:, 128:256], VV[:, 3, h * 64:h * 64 + 64], EB[h % 2][:, 256:384], False, True, last=True)
            tb["o", h] = tok
            if h % 2:
                t = act(OB[:, h // 2, :], bank[b][:, 0:T], ACT.Copy, tok)
                free[b] = [t]
                tb["e", h // 2] = t

        for s in range(10):
            if s >= 2:
                a_out(s - 2)
                b_out(s - 2)
            if s < 8:
                a_scores(s)
                b_scores(s)
            if 1 <= s < 9:
                a_turn(s - 1)
                b_tail(s - 1)
        t_o = []
        for O, tk in ((OA, ta), (OB, tb)):
            t_o += norm(O, Q8, [tk["e", k] for k in range(4)], 2, 3, False, 512.0, 1e-6, chunks=4)
        OO = arena(32, 8)
        t_o = [ts(DV, OO[:, k, :], OO[:, k, :], P("gab", k), None, ALU.mult, None, t_o[k]) for k in range(8)]
        t_x3 = []
        for i in range(4):
            b = next_bank()
            tok = gemm(a["w_out2"][i], OO, t_o, b)
            t_x3 += residual([tok, t_mod[1, 11]], b, i, 16, 1)
        XC = arena(0, 8)
        t_cp = [DV.do(lambda e, k=k, XC=XC: e.tensor_copy(XC[:, k, :], X[:, k, :]), t_x3[k]) for k in range(8)]
        t_ln = norm(XC, Q8, t_cp, 2, 3, False, 1024.0, 1e-6)
        t_h = affine(H, XC, lambda k: M(32 + k, 1), lambda k: M(24 + k, 1), t_ln, t_mod[1, 15], t_mod[1, 19])
        HF = arena(8, 22)
        CV = [arena(30 + 2 * i, 2) for i in range(4)]
        t_f = {}
        for i in range(22):
            b = next_bank()
            tok = gemm(a["w_up2"][i], H, t_h, b)
            cv = CV[i % 4]
            for c in range(2):
                t = conv(cv[:, c, :], bank[b][:, c * T:c * T + T], "cw2", 44, 3, i + 22 * c, P("cb2", i + 22 * c),
                         [tok, t_f.get(i - 4)] if c == 0 else tok)
            free[b] = [t]
            t = act(cv[:, 0, :], cv[:, 0, :], ACT.Silu, t)
            t_f[i] = tt(PO, HF[:, i, :], cv[:, 0, :], cv[:, 1, :], ALU.mult, t)
        t_x4 = []
        n = 0
        for j in range(8):
            if j % 2 == 0:
                b = next_bank()
            for k in range(22):
                if n % 16 == 0:
                    w = tile_in(a["w_down2"][n // 16])
                o = (n % 16) * 128
                n += 1
                tok = mm(bank[b][:, (j % 2) * T:(j % 2) * T + T], w[:, o:o + 128], HF[:, k, :], k == 0, k == 21,
                         free[b] if k == 0 and j % 2 == 0 else None, t_f[k], last=(k == 21 or n % 16 == 0))
                if n % 16 == 0:
                    tile_used(tok)
            if j % 2:
                t_x4 += residual([tok, t_mod[1, 23]], b, j // 2, 40, 1)
        t_ln = norm(X, Q8, t_x4, 2, 3, False, 1024.0, 1e-6)
        t_y = [ts(DV, H[:, k, :], X[:, k, :], P("fg", k), None, ALU.mult, None, t_ln[k]) for k in range(8)]
        AC.dma(out, H[:, :, :], s_out, 16, t_y)
        AC.wait((s_out, 16))

        for n, (src, _) in enumerate(stream):
            SP.dma(ring[n % NS][:, :], src, s_ring[n % NS], 0, stream[n - NS][1] if n >= NS else None)

        block = ctx.enter_context(nc.Block())

        @block.sync
        def _(eng):
            SP.play(eng)

        @block.scalar
        def _(eng):
            AC.play(eng)

        @block.vector
        def _(eng):
            DV.play(eng)

        @block.gpsimd
        def _(eng):
            PO.play(eng)

        @block.tensor
        def _(eng):
            PE.play(eng)


def pack_blocks(w):
    k, n = w.shape
    b = w.reshape(k // 128, 128, n // 128, 128).transpose(2, 0, 1, 3).reshape(-1, 16, 128, 128)
    return b.transpose(0, 2, 1, 3).reshape(-1, 128, 2048)


def lay_out(np, x):
    chunk = lambda v: v.reshape(-1, 128).T
    a = {}
    w_in = x["w_in"][0]
    pair = lambda m, first, second: np.concatenate(
        [np.concatenate([m[:, first + 128 * j:first + 128 * j + 128], m[:, second + 128 * j:second + 128 * j + 128]],
                        axis=1) for j in range((second - first) // 128)], axis=1)
    a["w_in"] = pack_blocks(np.concatenate(
        [w_in[:, 4096:6144], w_in[:, 2048:4096], w_in[:, 0:2048], pair(w_in, 7200, 8224), w_in[:, 6176:7200],
         w_in[:, 9248:11296]], axis=1))
    a["wdt"] = w_in[:, 6144:6176].reshape(8, 128, 32).transpose(1, 0, 2)
    a["wrt"] = x["router_w"][0].reshape(8, 128, 64).transpose(1, 0, 2)
    a["dtb"], a["alog"], a["rb"] = x["ssd_dt_bias"][0], x["ssd_A_log"][0], x["router_bias"][0]
    a["xT"] = x["x"][0].T.reshape(8, 128, T).transpose(1, 0, 2)
    a["ada"], a["ada2"] = pack_blocks(x["w_ada"][0]), pack_blocks(x["w_ada_2"][0])
    a["ssd_out"], a["sc_out"], a["w_o"] = (pack_blocks(x[n][0]) for n in ("w_ssd_out", "w_sc_out", "w_o"))
    for n in ("sh_gate", "sh_up", "sh_down"):
        a[n] = pack_blocks(x[n][0])
    for n in ("w_gate", "w_up", "w_down"):
        a[n] = np.concatenate([pack_blocks(x[n][0, e]) for e in range(N_EXP)], axis=0)
    w2 = x["w_in_2"][0]
    a["qk"] = pack_blocks(np.concatenate([w2[:, 0:1024], w2[:, 1536:2560]], axis=1))
    a["vv"] = np.concatenate([w2[:, c:c + 512].reshape(2, 4, 128, 512).transpose(0, 2, 1, 3).reshape(2, 128, 2048)
                              for c in (1024, 2560)], axis=0)
    a["w_out2"], a["w_down2"] = pack_blocks(x["w_out_2"][0]), pack_blocks(x["w_down_2"][0])
    a["w_up2"] = pack_blocks(pair(x["w_up_2"][0], 0, 2816))
    taps = lambda w: np.concatenate([chunk(w[k]) for k in range(w.shape[0])], axis=1)
    cols = {
        "b_ada": chunk(x["b_ada"][0]), "cw": taps(x["ssd_conv_w"][0]), "cb": chunk(x["ssd_conv_b"][0]),
        "D": chunk(np.repeat(x["ssd_D"][0], 64)), "nw": chunk(x["ssd_norm_w"][0]), "scw": taps(x["sc_conv_w"][0]),
        "ln1g": chunk(x["ln1_g"][0]), "ln1b": chunk(x["ln1_b"][0]), "ln2g": chunk(x["ln2_g"][0]),
        "ln2b": chunk(x["ln2_b"][0]), "b_ada2": chunk(x["b_ada_2"][0]),
        "gab": chunk(np.concatenate([x["g_a_2"][0], x["g_b_2"][0]])), "cw2": taps(x["conv_w_2"][0]),
        "cb2": chunk(x["conv_b_2"][0]), "fg": chunk(x["final_g_2"]), "c": chunk(x["c"][0]), "c2": chunk(x["c_2"][0]),
    }
    a["par"] = np.concatenate([cols[n] for n in _PAR], axis=1)
    q, k = np.arange(128)[:, None], np.arange(128)[None, :]
    at = lambda d: np.clip(d, -128, 128) + 128
    idx = np.concatenate([at(q - k), at(q + 128 - k), at(q - k)], axis=1)
    a["relb"] = x["rel_bias_2"][0][:, idx].transpose(1, 0, 2)
    return a


def kernel(**inputs):
    import numpy as np
    import concourse.bacc as bacc
    from concourse.bass_utils import run_bass_kernel_spmd

    x = {n: np.asarray(v) for n, v in inputs.items()}
    laid = {n: np.ascontiguousarray(v) for n, v in lay_out(np, x).items()}
    nc = bacc.Bacc("TRN2", target_bir_lowering=False, num_devices=1)
    aps = {n: nc.dram_tensor(f"in_{n}", v.shape, mybir.dt.from_np(v.dtype), kind="ExternalInput").ap()
           for n, v in laid.items()}
    out = nc.dram_tensor("out_x", (128, 8, T), mybir.dt.float32, kind="ExternalOutput").ap()
    build(nc, aps, out)
    r = run_bass_kernel_spmd(nc, [{f"in_{n}": v for n, v in laid.items()}], core_ids=[0])
    y = r.results[0]["out_x"]
    return np.ascontiguousarray(y.transpose(2, 1, 0).reshape(1, T, 1024))
```

```python
import concourse.bass as bass
from concourse import mybir
from contextlib import ExitStack

T = 256
NS = 4
POOL_HALF = (1,)
NW = 3
NX = 12
BLK = 64
NBLK = 96
ALPHA = 2.0 ** 0.25
N_EXP = 64

_PAR = {}


def par_columns():
    at = 0
    for name, n in (("b_ada", 48), ("cw", 128), ("cb", 32), ("D", 16), ("nw", 16), ("scw", 24),
                    ("ln1g", 8), ("ln1b", 8), ("ln2g", 8), ("ln2b", 8), ("b_ada2", 48), ("gab", 8),
                    ("cw2", 132), ("cb2", 44), ("fg", 8), ("c", 8), ("c2", 8)):
        _PAR[name] = (at, n)
        at += n
    return at


NPAR = par_columns()


class Queue:

    def __init__(self, sem):
        self.sem, self.count, self.items, self.seen = sem, 0, [], {}

    def wait(self, *tokens):
        for t in tokens:
            if t is None:
                continue
            if isinstance(t, list):
                self.wait(*t)
                continue
            sem, value = t
            if self.seen.get(sem.name, 0) < value:
                self.seen[sem.name] = value
                self.items.append(lambda e, s=sem, v=value: e.wait_ge(s, v))

    def do(self, fn, *tokens):
        self.wait(*tokens)
        self.count += 1
        self.items.append(lambda e, f=fn, s=self.sem: f(e).then_inc(s, 1))
        return (self.sem, self.count)

    def quiet(self, fn, *tokens):
        self.wait(*tokens)
        self.items.append(fn)

    def branch(self, fn):
        self.items.append(fn)

    def dma(self, out, in_, sem, value, *tokens):
        self.wait(*tokens)
        self.items.append(lambda e: e.dma_start(out, in_).then_inc(sem, 16))
        return (sem, value)

    def play(self, eng):
        for item in self.items:
            item(eng)


def build(nc, a, out):
    fp = mybir.dt.float32
    fr = mybir.dt.float32r
    ALU = mybir.AluOpType
    ACT = mybir.ActivationFunctionType
    AX = mybir.AxisListType
    ctx = ExitStack()
    with ctx:
        def sb(name, shape):
            return ctx.enter_context(nc.sbuf_tensor(name, shape, fp))

        def sem(name):
            return ctx.enter_context(nc.semaphore(name))

        ring = [sb(f"ring{i}", [128, 2048]) for i in range(NS)]
        X = sb("X", [128, 8, T])
        H = sb("H", [128, 8, T])
        par = sb("par", [128, NPAR])
        mod = sb("mod", [128, 96])
        ones = sb("ones", [128, 128])
        ident = sb("ident", [128, 128])
        triU = sb("triU", [128, 128])
        triS = sb("triS", [128, 128])
        triG = sb("triG", [128, 128])
        small = sb("small", [128, 2048])
        wdt = sb("wdt", [128, 8, 32])
        wrt = sb("wrt", [128, 8, 64])
        rowb = sb("rowb", [128, 128])
        AR = sb("AR", [128, 94 * 256])
        FR = ctx.enter_context(nc.sbuf_tensor("FR", [128, (16 + 8 * NW) * 256], fr))
        tab = ctx.enter_context(nc.sbuf_tensor("tab", [1, 104], mybir.dt.int32))
        bank = [ctx.enter_context(nc.psum_tensor(f"bank{i}", [128, 512], fp)) for i in range(8)]

        def arena(kb, n, cols=T):
            return AR[:, kb * 256:kb * 256 + n * cols].rearrange("p (n t) -> p n t", t=cols)

        s_pe, s_act, s_dve, s_pool = sem("s_pe"), sem("s_act"), sem("s_dve"), sem("s_pool")
        s_xr = [sem(f"s_xr{i}") for i in range(NX)]
        s_late = [sem(f"s_late{i}") for i in range(NS)]
        s_pe2, s_act2, s_dve2, s_pool2 = sem("s_pe2"), sem("s_act2"), sem("s_dve2"), sem("s_pool2")
        s_ring = [sem(f"s_ring{i}") for i in range(NS)]
        s_par, s_x, s_wdt, s_wrt, s_row, s_bias, s_out = (
            sem("s_par"), sem("s_x"), sem("s_wdt"), sem("s_wrt"), sem("s_row"), sem("s_bias"), sem("s_out"))
        PE, AC, DV, PO, SP = Queue(s_pe), Queue(s_act), Queue(s_dve), Queue(s_pool), Queue(None)

        def tt(q, o, x, y, op, *w):
            return q.do(lambda e: e.tensor_tensor(o, x, y, op), *w)

        def ts(q, o, x, s1, s2, op0, op1, *w):
            if s2 is None:
                return q.do(lambda e: e.tensor_scalar(o, x, s1, None, op0), *w)
            return q.do(lambda e: e.tensor_scalar(o, x, s1, s2, op0, op1), *w)

        def stt(o, x, s, y, op0, op1, *w):
            return DV.do(lambda e: e.scalar_tensor_tensor(out=o, in0=x, scalar=s, in1=y, op0=op0, op1=op1), *w)

        def act(o, x, f, *w, bias=0.0, scale=1.0, accum=None):
            if accum is not None:
                return AC.do(lambda e: e.activation(o, x, f, bias=bias, scale=scale, accum_out=accum), *w)
            return AC.do(lambda e: e.activation(o, x, f, bias=bias, scale=scale), *w)

        def mm(o, l, r, start, stop, *w, last=False, skip=False):
            f = lambda e: e.matmul(o, l, r, start=start, stop=stop, skip_group_check=skip)
            if last:
                return PE.do(f, *w)
            PE.quiet(f, *w)

        def tr(o, i, *w, last=False):
            k = i.shape[0]
            f = lambda e: e.transpose(o, i, ident[0:k, 0:k])
            if last:
                return PE.do(f, *w)
            PE.quiet(f, *w)

        normed = []
        free = [[] for _ in range(8)]
        late = [0]
        stream = []

        def tile_in(src, q=PE):
            n = len(stream) - late[0]
            stream.append([src, None])
            q.wait(((s_late if late[0] else s_ring)[n % NS], 16 * (n // NS + 1)))
            return ring[n % NS]

        def tile_used(tok):
            stream[-1][1] = tok

        def sp_load(first, end, start):
            for n in range(first, end):
                m = n - late[0]
                SP.dma(ring[m % NS][:, :], stream[n][0], (s_late if late[0] else s_ring)[m % NS], 0,
                       stream[n - NS][1] if m >= NS else start)

        def P(name, i=0, n=1):
            at = _PAR[name][0] + i
            return par[:, at:at + n]

        t_par = AC.dma(par[:, :], a["par"], s_par, 16)
        t_x = AC.dma(X[:, :, :], a["xT"], s_x, 16)
        t_wdt = AC.dma(wdt[:, :, :], a["wdt"], s_wdt, 16)
        AC.dma(rowb[:, 0:32], a["dtb"].partition_broadcast(128), s_row, 16)
        AC.dma(rowb[:, 32:64], a["alog"].partition_broadcast(128), s_row, 32)
        t_row = AC.dma(rowb[:, 64:128], a["rb"].partition_broadcast(128), s_row, 48)
        t_wrt = AC.dma(wrt[:, :, :], a["wrt"], s_wrt, 16)

        t_ones = PO.do(lambda e: e.memset(ones[:, :], 1.0))
        t_z = PO.do(lambda e: e.memset(ident[:, :], 0.0))
        t_id = PO.do(lambda e: e.affine_select(out=ident[:, :], in_=ident[:, :], compare_op=ALU.not_equal,
                     fill=1.0, base=0, pattern=[[-1, 128]], channel_multiplier=1), t_z)
        def tri(dst, step, base):
            return PO.do(lambda e: e.affine_select(out=dst[:, :], in_=ones[:, :], compare_op=ALU.is_ge,
                         fill=0.0, base=base, pattern=[[step, 128]], channel_multiplier=-step), t_ones)
        t_triU = tri(triU, 1, 0)
        t_triS = tri(triS, 1, -1)
        t_triG = tri(triG, -1, 0)
        t_const = t_triG

        cz = sb("cz", [128, 2, 8, 32])
        RA = [sb(f"RA{i}", [128, 512]) for i in range(2)]
        t_z = PO.do(lambda e: e.memset(cz[:, :, :, :], 0.0))
        t_cz = act(cz[:, :, :, 0], P("c", 0, 16).rearrange("p (a k) -> p a k", a=2), ACT.Silu, t_par, t_z)
        t_mod = {}
        ada_open = []
        t_ra = {}
        ada_n = [0]

        def ada_group(which, i, b):
            src = a["ada2" if which else "ada"]
            n = ada_n[0]
            ada_n[0] += 1
            for half in range(2):
                w = tile_in(src[2 * i + half])
                PE.wait(t_cz, free[b])
                for k in range(4):
                    tok = mm(bank[b][32 * k:32 * k + 32, :], cz[:, which, 4 * half + k, :],
                             w[:, k * 512:k * 512 + 512], half == 0, half == 1, last=(k == 3))
                tile_used(tok)
            t = act(RA[n % 2][:, :], bank[b][:, :], ACT.Copy, tok, t_ra.get(n - 2))
            free[b] = [t]
            ada_open.append((which, i, n, t))

        def ada_close(b):
            if not ada_open:
                return
            which, i, n, t = ada_open.pop(0)
            PE.wait(t, free[b], t_id)
            for j in range(4):
                tok = tr(bank[b][:, j * 128:j * 128 + 128], RA[n % 2][:, j * 128:j * 128 + 128], last=(j == 3))
            t_ra[n] = tok
            at = 48 * which + 4 * i
            t = DV.do(lambda e: e.tensor_reduce(
                mod[:, at:at + 4], bank[b][:, :].rearrange("p (j g c) -> p j g c", j=4, g=4)[:, :, :, 0],
                AX.X, ALU.add), tok)
            free[b] = [t]
            t = tt(DV, mod[:, at:at + 4], mod[:, at:at + 4], P("b_ada2" if which else "b_ada", 4 * i, 4),
                   ALU.add, t)
            if i // 2 in (1, 4):
                t = ts(DV, mod[:, at:at + 4], mod[:, at:at + 4], 1.0, None, ALU.add, None, t)
            for j in (2 * i, 2 * i + 1):
                t_mod[which, j] = t

        def norm(S, Q, toks, b1, b2, center, rms_n, eps, chunks=8, q_free=()):
            n = chunks
            pairs = [slice(2 * p, 2 * p + 2) for p in range(n // 2)]
            done = list(toks)
            if center:
                for k in range(n):
                    tok = mm(bank[b1][:, 0:T], ones[:, :], S[:, k, :], k == 0, k == n - 1, t_ones, toks[k],
                             free[b1] if k == 0 else None, last=(k == n - 1))
                mean = bank[b1][:, 0:T].unsqueeze(1).to_broadcast([128, 2, T])
                done = []
                for p in pairs:
                    t = stt(S[:, p, :], mean, -1.0 / 1024.0, S[:, p, :], ALU.mult, ALU.add, tok)
                    done += [t, t]
                free[b1] = [done[-1]]
            for i, p in enumerate(pairs):
                t = act(Q[:, p, :], S[:, p, :], ACT.Square, done[2 * i], done[2 * i + 1], *(q_free if i == 0 else ()))
                for k in (2 * i, 2 * i + 1):
                    tok = mm(bank[b2][:, 0:T], ones[:, :], Q[:, k, :], k == 0, k == n - 1, t, t_ones,
                             free[b2] if k == 0 else None, last=(k == n - 1))
            r = small[:, 256:256 + T]
            t = ts(DV, r, bank[b2][:, 0:T], 1.0 / rms_n, eps, ALU.mult, ALU.add, tok, normed)
            free[b2] = [t]
            t = act(r, r, ACT.Sqrt, t)
            t = DV.do(lambda e: e.reciprocal(r, r), t)
            rb = r.unsqueeze(1).to_broadcast([128, 2, T])
            res = []
            for p in pairs:
                t = tt(DV, S[:, p, :], S[:, p, :], rb, ALU.mult, t)
                res += [t, t]
            normed[:] = [t]
            return res

        def affine(O, S, scale, bias, toks, *w):
            res = []
            for k in range(8):
                if k % 2:
                    res.append(act(O[:, k, :], S[:, k, :], ACT.Identity, toks[k], *w, bias=bias(k), scale=scale(k)))
                else:
                    res.append(ts(DV, O[:, k, :], S[:, k, :], scale(k), bias(k), ALU.mult, ALU.add, toks[k], *w))
            return res

        def M(i, which=0):
            return mod[:, 48 * which + i:48 * which + i + 1]

        AH, AL = (FR[:, i * 2048:i * 2048 + 2048].rearrange("p (n t) -> p n t", n=8) for i in range(2))
        a_read = []
        w_order = []
        w_split = []
        w_read = []

        def split_next():
            n = len(w_split) // 2
            if n >= len(w_order):
                return
            w = tile_in(w_order[n], AC)
            for c in range(2):
                m = len(w_split)
                o = 4096 + 2048 * (m % NW)
                hi, lo = FR[:, o:o + 1024], FR[:, o + 1024:o + 2048]
                x = w[:, c * 1024:c * 1024 + 1024]
                t = act(hi, x, ACT.Copy, w_read[m - NW] if m >= NW else None)
                t = tt(PO if c in POOL_HALF else DV, lo, x, hi.bitcast(fp), ALU.subtract, t)
                w_split.append((hi, lo, t))
                stream[-1][1] = (stream[-1][1] or []) + [t]

        def split(R, toks, chunks=8):
            res = []
            for k in range(0, chunks, 2):
                t = act(AH[:, k:k + 2, :], R[:, k:k + 2, :], ACT.Copy, toks[k], toks[k + 1], a_read)
                t = tt(DV, AL[:, k:k + 2, :], R[:, k:k + 2, :], AH[:, k:k + 2, :].bitcast(fp), ALU.subtract, t)
                res += [t, t]
            return res

        def gemm(src, toks, b):
            n = len(w_read) // 2
            assert w_order[n] is src
            if len(w_split) == 2 * n:
                split_next()
            for c in range(2):
                hi, lo, t = w_split[2 * n + c]
                PE.wait(t)
                for k in range(8):
                    j = k * 128
                    o = bank[b][:, c * T:c * T + T]
                    mm(o, hi[:, j:j + 128], AH[:, k, :], k == 0, False, free[b] if c == k == 0 else None, toks[k])
                    mm(o, hi[:, j:j + 128], AL[:, k, :], False, False)
                    tok = mm(o, lo[:, j:j + 128], AH[:, k, :], False, k == 7, last=(k == 7))
                w_read.append(tok)
            a_read[:] = [tok]
            free[b] = []
            split_next()
            return tok

        tiles = {n: [a[n][i] for i in range(a[n].shape[0])]
                 for n in ("w_in", "sc_out", "w_o", "sh_gate", "sh_up", "qk", "w_out2", "w_up2")}
        w_order += [t for n in ("w_in", "sc_out", "w_o", "sh_gate", "sh_up") for t in tiles[n]]

        Q8 = arena(82, 8)
        for i in range(4):
            ada_group(0, i, i % 2)
            if i:
                ada_close(4 + i % 2)
        ada_close(4)
        XC = arena(0, 8)
        t_cp = [ts(DV, XC[:, 2 * p:2 * p + 2, :], X[:, 2 * p:2 * p + 2, :], 1.0, None, ALU.mult, None, t_x)
                for p in range(4)]
        t_ln = norm(XC, Q8, [t_cp[k // 2] for k in range(8)], 2, 3, True, 1024.0, 1e-5)
        t_h = affine(H, XC, lambda k: M(8 + k), lambda k: M(k), t_ln, t_mod[0, 3], t_mod[0, 7])
        t_hs = split(H, t_h)

        dt = small[:, 512:576]
        e1 = small[:, 576:640]
        u1 = small[:, 640:704]
        r1 = small[:, 704:768]
        dA = small[:, 768:832]
        acsT = small[:, 832:896]
        dec = small[:, 896:928]
        dtd = small[:, 928:960]
        acsF = small[0:32, 1024:1280]
        for t in range(2):
            for k in range(8):
                tok = mm(bank[2][:, t * 32:t * 32 + 32], H[:, k, t * 128:t * 128 + 128], wdt[:, k, :],
                         k == 0, k == 7, t_wdt, t_h[k], free[2], last=(t == 1 and k == 7))
        v2 = lambda x: x.rearrange("p (t h) -> p t h", t=2)
        t0 = tt(DV, v2(dt), v2(bank[2][:, 0:64]), rowb[:, 0:32].unsqueeze(1).to_broadcast([128, 2, 32]),
                ALU.add, tok, t_row)
        free[2] = [t0]
        t1 = act(e1, dt, ACT.Abs, t0)
        t1 = act(e1, e1, ACT.Exp, t1, scale=-1.0)
        t_A = act(small[:, 960:992], rowb[:, 32:64], ACT.Exp, t_row)
        t2 = ts(DV, u1, e1, 1.0, None, ALU.add, None, t1)
        t3 = act(r1, u1, ACT.Ln, t2)
        t4 = stt(e1, u1, -1.0, e1, ALU.add, ALU.subtract, t2)
        t5 = DV.do(lambda e: e.reciprocal(u1, u1), t3, t4)
        t5 = tt(DV, e1, e1, u1, ALU.mult, t5)
        t5 = tt(DV, r1, r1, e1, ALU.subtract, t5, t3)
        t5 = stt(dt, dt, 0.0, r1, ALU.max, ALU.add, t5)
        t_dt = t5
        t6 = stt(v2(dA), v2(dt), -1.0, small[:, 960:992].unsqueeze(1).to_broadcast([128, 2, 32]),
                 ALU.mult, ALU.mult, t5, t_A)
        for c in range(2):
            mm(bank[3][:, c * 32:c * 32 + 32], triU[:, :], dA[:, c * 32:c * 32 + 32], True, True, t_const, t6, free[3])
        tok = mm(bank[3][:, 64:96], ones[:, :], dA[:, 0:32], True, True, last=True)
        for c in range(2):
            tokF = mm(bank[2][0:32, c * 128:c * 128 + 128], dA[:, c * 32:c * 32 + 32], triU[:, :], True, True,
                      free[2], last=(c == 1))
        t7 = DV.do(lambda e: e.tensor_copy(acsT, bank[3][:, 0:64]), tok)
        t8 = tt(DV, dec, bank[3][:, 64:96], acsT[:, 0:32], ALU.subtract, t7)
        free[3] = [t8]
        t8 = act(dec, dec, ACT.Exp, t8)
        t_dtd = tt(DV, dtd, dt[:, 0:32], dec, ALU.mult, t8)
        t_acs = DV.do(lambda e: e.tensor_copy(acsF, bank[2][0:32, 0:256]), tokF)
        free[2] = [t_acs]
        t_acsT = t7

        XS, Z, BB, CC = arena(0, 16), arena(16, 16), arena(32, 8), arena(40, 8)

        def conv(o, x, cw, n, K, at, bias, tok):
            if bias is None:
                t = ts(DV, o, x, P(cw, (K - 1) * n + at), None, ALU.mult, None, tok)
            else:
                t = ts(DV, o, x, P(cw, (K - 1) * n + at), bias, ALU.mult, ALU.add, tok)
            for s in range(1, K):
                t = stt(o[:, s:T], x[:, 0:T - s], P(cw, (K - 1 - s) * n + at), o[:, s:T], ALU.mult, ALU.add, t)
            return t

        nb = [0]

        def next_bank():
            nb[0] ^= 1
            return nb[0]

        def xbc_tile(i, dst, at, chunk, *w):
            b = next_bank()
            tok = gemm(tiles["w_in"][i], t_hs, b)
            res = []
            for c in range(2):
                t = conv(dst[:, at + c, :], bank[b][:, c * T:c * T + T], "cw", 32, 4, chunk + c,
                         P("cb", chunk + c), [tok, *w])
                res.append(t)
            free[b] = [t]
            t = act(dst[:, at:at + 2, :], dst[:, at:at + 2, :], ACT.Silu, *res)
            return t

        t_B, t_C, t_XS = {}, {}, {}
        for i in range(4):
            t_B[i] = xbc_tile(i, BB, 2 * i, 16 + 2 * i)
        for i in range(4):
            t_C[i] = xbc_tile(4 + i, CC, 2 * i, 24 + 2 * i)
        for g in range(8):
            t_XS[g] = xbc_tile(8 + g, XS, 2 * g, 2 * g, t_h)

        U = arena(48, 8)
        t_z = [None] * 8
        t_u = [None] * 8

        def z_tile(i):
            b = next_bank()
            tok = gemm(tiles["w_in"][16 + i], t_hs, b)
            t_z[i] = act(Z[:, 2 * i:2 * i + 2, :], bank[b][:, :].rearrange("p (n t) -> p n t", n=2), ACT.Silu, tok)
            free[b] = [t_z[i]]

        sc_tmp = arena(88, 2)

        def sc_tile(j):
            b = next_bank()
            tok = gemm(tiles["w_in"][24 + j], t_hs, b)
            prev = t_u[j - 1] if j else None
            t1 = act(sc_tmp[:, 0, :], bank[b][:, 0:T], ACT.Copy, tok, prev)
            t2 = tt(DV, sc_tmp[:, 1, :], bank[b][:, T:2 * T], sc_tmp[:, 0, :], ALU.mult, t1)
            free[b] = [t2]
            t_u[j] = conv(U[:, j, :], sc_tmp[:, 1, :], "scw", 8, 3, j, None, t2)

        def scb_tile(i):
            b = next_bank()
            tok = gemm(tiles["w_in"][32 + i], t_hs, b)
            t = tt(DV, U[:, 2 * i:2 * i + 2, :], U[:, 2 * i:2 * i + 2, :],
                   bank[b][:, :].rearrange("p (n t) -> p n t", n=2), ALU.mult, tok, t_u[2 * i], t_u[2 * i + 1])
            free[b] = [t]
            t_u[2 * i] = t_u[2 * i + 1] = t

        fill = []
        main = [lambda i=i: z_tile(i) for i in range(8)] + [lambda j=j: sc_tile(j) for j in range(8)] \
            + [lambda i=i: scb_tile(i) for i in range(4)]
        adas = [(0, i) for i in range(4, 12)] + [(1, i) for i in range(12)]
        fill = list(zip(main, adas))

        def filler():
            if fill:
                f, (which, i) = fill.pop(0)
                ada_close(next_bank())
                f()
                ada_group(which, i, next_bank())

        t_Y = [None] * 8
        prevY = {}
        for g in range(8):
            S = AR[:, (56 + 16 * (g % 2)) * 256:(72 + 16 * (g % 2)) * 256]
            Xdt, Xd, BT = S[:, 0:512], S[:, 512:768], S[:, 768:896]
            CBm, D = S[:, 896:1152], S[:, 1152:2176]
            CE, PV = S[:, 2176:2688], S[:, 2688:2944]
            RM = S[0:32, 2944:3968]
            old = prevY.get(g - 2)
            r3 = lambda x, n: x.rearrange("p (n t) -> p n t", n=n)
            for c in range(2):
                tR = tt(PO, r3(RM[:, c * 512:c * 512 + 512], 4),
                        acsF[:, c * 128:c * 128 + 128].unsqueeze(1).to_broadcast([32, 4, 128]),
                        ident[0:32, 4 * g:4 * g + 4].unsqueeze(2).to_broadcast([32, 4, 128]), ALU.mult,
                        t_acs, t_id, old)
            PE.wait(free[2], free[3], t_XS[g], t_B[g // 2], t_C[g // 2], t_id)
            for t in range(2):
                for j in range(2):
                    tX = tr(bank[2][:, (2 * t + j) * 128:(2 * t + j) * 128 + 128],
                            XS[:, 2 * g + j, t * 128:t * 128 + 128], last=(t == j == 1))
            tr(bank[3][:, 0:128], BB[:, g, 0:128])
            for c in range(2):
                tC = mm(bank[3][:, 128 + c * 128:256 + c * 128], BB[:, g, c * 128:c * 128 + 128],
                        CC[:, g, c * 128:c * 128 + 128], True, True, last=(c == 1))
            for c in range(2):
                tS = mm(bank[4 + c][:, :], ones[0:32, :], RM[:, c * 512:c * 512 + 512], True, True,
                        tR, free[4 + c], last=(c == 1))
            tBT = act(BT, bank[3][:, 0:128], ACT.Copy, tC, old)
            tE = act(CE, bank[5][:, :], ACT.Exp, tS)
            t1 = tt(DV, Xdt.rearrange("p (t r q) -> p t r q", t=2, r=4),
                    bank[2][:, :].rearrange("p (t r q) -> p t r q", t=2, r=4),
                    v2(dt)[:, :, 4 * g:4 * g + 4].unsqueeze(3).to_broadcast([128, 2, 4, 64]), ALU.mult, tX, t_dt, old)
            t1b = tt(DV, r3(Xd, 4), r3(bank[2][:, 0:256], 4),
                     dtd[:, 4 * g:4 * g + 4].unsqueeze(2).to_broadcast([128, 4, 64]), ALU.mult, t_dtd)
            free[2] = [t1b]
            t2 = tt(DV, r3(CBm, 2), r3(bank[3][:, 128:384], 2),
                    triU[:, :].unsqueeze(1).to_broadcast([128, 2, 128]), ALU.mult, tC, tBT, t_const)
            free[3] = [t2, tBT]
            for c in range(2):
                for r in range(4):
                    o = c * 512 + r * 128
                    t3 = ts(DV, D[:, o:o + 128], bank[4 + c][:, r * 128:r * 128 + 128],
                            acsT[:, c * 32 + 4 * g + r:c * 32 + 4 * g + r + 1], 0.0, ALU.subtract, ALU.min,
                            tS, tE, t_acsT)
                free[4 + c] = [t3]
                t3 = act(D[:, c * 512:c * 512 + 512], D[:, c * 512:c * 512 + 512], ACT.Exp, t3)
                tD = tt(DV, r3(D[:, c * 512:c * 512 + 512], 4), r3(D[:, c * 512:c * 512 + 512], 4),
                        CBm[:, c * 128:c * 128 + 128].unsqueeze(1).to_broadcast([128, 4, 128]), ALU.mult, t3, t2)
            tCE = tt(PO, r3(CE, 4), r3(CE, 4), CC[:, g, 128:256].unsqueeze(1).to_broadcast([128, 4, 128]),
                     ALU.mult, tE)
            filler()
            tok = mm(bank[6][:, 0:256], BT, Xd, True, True, tBT, t1b, free[6], last=True)
            tPV = act(PV, bank[6][:, 0:256], ACT.Copy, tok)
            free[6] = [tPV]
            filler()
            PE.wait(tPV, tD, tCE, t1, free[7])
            for j in range(2):
                for h in range(2):
                    r = 2 * j + h
                    o = bank[7][h * 64:h * 64 + 64, j * T:j * T + T]
                    mm(o[:, 0:128], Xdt[:, r * 64:r * 64 + 64], D[:, r * 128:r * 128 + 128], True, True)
                    mm(o[:, 128:256], Xdt[:, 256 + r * 64:256 + r * 64 + 64],
                       D[:, 512 + r * 128:512 + r * 128 + 128], True, False)
                    tok = mm(o[:, 128:256], PV[:, r * 64:r * 64 + 64], CE[:, r * 128:r * 128 + 128],
                             False, True, last=(r == 3))
            for j in range(2):
                t = stt(XS[:, 2 * g + j, :], XS[:, 2 * g + j, :], P("D", 2 * g + j), bank[7][:, j * T:j * T + T],
                        ALU.mult, ALU.add, tok)
            free[7] = [t]
            t_Y[g] = t
            prevY[g] = [t, tok]
            filler()
        while fill:
            filler()
        ada_close(next_bank())

        GA, GB = BB, CC
        GQ = [arena(90, 2), arena(92, 2)]
        rs = [small[:, 1280:1536], small[:, 1536:1792]]
        t_gq, t_yn, t_rs, t_sq = {}, {}, {}, {}

        def gated(g):
            sl = slice(2 * g, 2 * g + 2)
            t = tt(DV, XS[:, sl, :], XS[:, sl, :], Z[:, sl, :], ALU.mult, t_Y[g], t_z[g])
            t_sq[g] = act(GQ[g % 2], XS[:, sl, :], ACT.Square, t, t_gq.get(g - 2), t_u[7])

        def rooted(g):
            b = 2 + g % 2
            for k in range(2):
                tok = mm(bank[b][:, 0:T], ones[:, :], GQ[g % 2][:, k, :], k == 0, k == 1, t_sq[g], free[b],
                         last=(k == 1))
            t_gq[g] = tok
            r = rs[g % 2]
            t = ts(DV, r, bank[b][:, 0:T], 1.0 / 256.0, 1e-5, ALU.mult, ALU.add, tok, t_rs.get(g - 2))
            free[b] = [t]
            t = act(r, r, ACT.Sqrt, t)
            t = DV.do(lambda e, r=r: e.reciprocal(r, r), t)
            for k in range(2):
                t = stt(XS[:, 2 * g + k, :], XS[:, 2 * g + k, :], P("nw", 2 * g + k), r, ALU.mult, ALU.mult, t)
            t_rs[g] = t
            t_yn[2 * g] = t_yn[2 * g + 1] = t

        t_g = []
        for i in range(8):
            b = next_bank()
            gated(i)
            tok = gemm(tiles["w_in"][36 + i], t_hs, b)
            dst = (GA if i < 4 else GB)[:, 2 * (i % 4):2 * (i % 4) + 2, :]
            t = act(dst, bank[b][:, :].rearrange("p (n t) -> p n t", n=2), ACT.Sigmoid, tok, t_Y[7], tCE)
            free[b] = [t]
            t_g.append(t)
            if i:
                rooted(i - 1)
        rooted(7)
        t_us = split(U, t_u)

        t_m = [None] * 8
        for i in range(4):
            b = next_bank()
            for c in range(2):
                w = tile_in(a["ssd_out"][2 * i + c])
                for k in range(16):
                    tok = mm(bank[b][:, c * T:c * T + T], w[:, k * 128:k * 128 + 128], XS[:, k, :],
                             k == 0, k == 15, free[b], t_yn[k], last=(k == 15))
                tile_used(tok)
            t = tt(DV, GA[:, 2 * i:2 * i + 2, :], GA[:, 2 * i:2 * i + 2, :],
                   bank[b][:, :].rearrange("p (n t) -> p n t", n=2), ALU.mult, tok, t_g[i])
            free[b] = [t]
            b = next_bank()
            tok = gemm(tiles["sc_out"][i], t_us, b)
            t = tt(DV, GB[:, 2 * i:2 * i + 2, :], GB[:, 2 * i:2 * i + 2, :],
                   bank[b][:, :].rearrange("p (n t) -> p n t", n=2), ALU.mult, tok, t_g[4 + i], t)
            free[b] = [t]
            t = tt(DV, GA[:, 2 * i:2 * i + 2, :], GA[:, 2 * i:2 * i + 2, :], GB[:, 2 * i:2 * i + 2, :], ALU.add, t)
            t_m[2 * i] = t_m[2 * i + 1] = t
        for k in range(8):
            t_xa = ts(DV, X[:, k, :], X[:, k, :], ALPHA, None, ALU.mult, None, t_cp[3])

        def residual(tok, b, i, gcol, which):
            for c in range(2):
                t = stt(X[:, 2 * i + c, :], bank[b][:, c * T:c * T + T], M(gcol + 2 * i + c, which),
                        X[:, 2 * i + c, :], ALU.mult, ALU.add, tok)
            free[b] = [t]
            return [t, t]

        t_ms = split(GA, t_m)
        t_x1 = []
        for i in range(4):
            b = next_bank()
            tok = gemm(tiles["w_o"][i], t_ms, b)
            t_x1 += residual([tok, t_xa, t_mod[0, 11]], b, i, 16, 0)
        t_ln = norm(X, Q8, t_x1, 2, 3, True, 1024.0, 1e-5)
        t_x1 = affine(X, X, lambda k: P("ln1g", k), lambda k: P("ln1b", k), t_ln)
        XC = arena(74, 8)
        t_cp = [DV.do(lambda e, k=k, XC=XC: e.tensor_copy(XC[:, k, :], X[:, k, :]), t_x1[k]) for k in range(8)]
        t_ln = norm(XC, Q8, t_cp, 2, 3, True, 1024.0, 1e-5)
        t_h = affine(H, XC, lambda k: M(32 + k), lambda k: M(24 + k), t_ln, t_mod[0, 15], t_mod[0, 19])
        t_hs = split(H, t_h)
        for k in range(8):
            t_xa = ts(DV, X[:, k, :], X[:, k, :], ALPHA, None, ALU.mult, None, t_cp[k])

        for t in range(2):
            for k in range(8):
                tok = mm(bank[2][:, t * 64:t * 64 + 64], H[:, k, t * 128:t * 128 + 128], wrt[:, k, :],
                         k == 0, k == 7, t_wrt, t_h[k], free[2], last=(t == 1 and k == 7))
        sc = small[:, 256 + 256:256 + 384]
        bi = small[:, 640:768]
        m8 = small[:, 768:896]
        gs = small[:, 896:912]
        rk = small[:, 912:928]
        rk2 = small[:, 928:944]
        lt = small[:, 1024:1088]
        cmpb = small[:, 1088:1216]
        v8 = small[:, 944:960]
        rep = small[:, 1280:1408]
        gate = small[:, 1408:1536]
        s1 = small[:, 960:962]
        v3 = lambda x: x.rearrange("p (t g h) -> p t g h", t=2, g=8)
        t = PO.do(lambda e: e.memset(lt, 1.0), t_acs, t_rs[7])
        t_lt = PO.do(lambda e: e.affine_select(out=lt, in_=lt, compare_op=ALU.is_ge, fill=0.0, base=-1,
                     pattern=[[1, 8], [-1, 8]], channel_multiplier=0), t)
        t0 = act(sc, bank[2][:, 0:128], ACT.Sigmoid, tok)
        free[2] = [t0]
        t0 = tt(DV, v2(bi), v2(sc), rowb[:, 64:128].unsqueeze(1).to_broadcast([128, 2, 64]), ALU.add, t0)
        for t in range(2):
            for g in range(8):
                o = (t * 8 + g) * 8
                t1 = DV.do(lambda e, o=o: e.max(m8[:, o:o + 8], bi[:, o:o + 8]), t0)
        m8v = m8.rearrange("p (n k) -> p n k", k=8)
        t1 = tt(DV, gs.unsqueeze(2), m8v[:, :, 0:1], m8v[:, :, 1:2], ALU.add, t1)
        gsv = gs.rearrange("p (t g) -> p t g", t=2)
        inner = gsv.unsqueeze(2).to_broadcast([128, 2, 8, 8])
        outer = gsv.unsqueeze(3).to_broadcast([128, 2, 8, 8])
        t2 = tt(DV, v3(cmpb), inner, outer, ALU.is_gt, t1)
        t2 = DV.do(lambda e: e.tensor_reduce(rk, cmpb.rearrange("p (n k) -> p n k", k=8), AX.X, ALU.add), t2)
        t3 = tt(DV, v3(cmpb), inner, outer, ALU.is_equal, t2)
        t3 = tt(DV, v3(cmpb), v3(cmpb), lt.rearrange("p (g h) -> p g h", g=8).unsqueeze(1)
                .to_broadcast([128, 2, 8, 8]), ALU.mult, t3, t_lt)
        t3 = DV.do(lambda e: e.tensor_reduce(rk2, cmpb.rearrange("p (n k) -> p n k", k=8), AX.X, ALU.add), t3)
        t3 = tt(DV, rk, rk, rk2, ALU.add, t3, t2)
        t3 = ts(DV, rk, rk, 3.5, None, ALU.is_lt, None, t3)
        t3 = ts(DV, rk, rk, -1.0, 1e30, ALU.add, ALU.mult, t3)
        t3 = tt(DV, bi.rearrange("p (n k) -> p n k", k=8), bi.rearrange("p (n k) -> p n k", k=8),
                rk.unsqueeze(2).to_broadcast([128, 16, 8]), ALU.add, t3)
        for t in range(2):
            bt, vt, rt = bi[:, t * 64:t * 64 + 64], v8[:, t * 8:t * 8 + 8], rep[:, t * 64:t * 64 + 64]
            t4 = DV.do(lambda e, bt=bt, vt=vt: e.max(vt, bt), t3)
            t4 = DV.do(lambda e, bt=bt, vt=vt, rt=rt: e.match_replace(rt, vt, bt, -3e30), t4)
            t4 = ts(DV, rt, rt, -2e30, None, ALU.is_lt, None, t4)
            gt = gate[:, t * 64:t * 64 + 64]
            t4 = tt(DV, gt, rt, sc[:, t * 64:t * 64 + 64], ALU.mult, t4)
            t4 = DV.do(lambda e, t=t, gt=gt: e.tensor_reduce(s1[:, t:t + 1], gt, AX.X, ALU.add), t4)
            t4 = DV.do(lambda e, t=t: e.reciprocal(s1[:, t:t + 1], s1[:, t:t + 1]), t4)
            t_gate = ts(DV, gt, gt, s1[:, t:t + 1], 2.5, ALU.mult, ALU.mult, t4)

        RT = AR[:, 90 * 256:94 * 256]
        relp, gV = RT[:, 0:192], RT[:, 192:384]
        v64, vI, io64, thr, eI = RT[:, 384:480], RT[:, 480:576], RT[:, 576:640], RT[:, 640:644], RT[:, 644:645]
        posT, gateT = small[0:64, 1536:1792], small[0:64, 1792:2048]
        OH, mi = small[0:64, 256:352], small[0:64, 352:368]

        def iota(dst, pattern, cm):
            return PO.do(lambda e: e.iota(dst, pattern=pattern, base=0, channel_multiplier=cm,
                                          allow_small_or_imprecise_dtypes=True), t_u[7], t_m[7])
        iota(v64, [[64, NBLK]], 0)
        iota(vI, [[1, NBLK]], 0)
        iota(io64, [[1, BLK]], 0)
        iota(thr, [[64, 4]], 0)
        t_io = iota(eI, [[1, 1]], 1)
        mk = [rep[:, 0:64], rep[:, 64:128]]

        SHH, SHG = arena(21, 2), arena(23, 2)
        tg = gemm(tiles["sh_gate"][0], t_hs, 0)
        tu = gemm(tiles["sh_up"][0], t_hs, 1)
        t = act(SHG, bank[0][:, :].rearrange("p (n t) -> p n t", n=2), ACT.Silu, tg)
        free[0] = [t]
        t_sh = tt(DV, SHH, bank[1][:, :].rearrange("p (n t) -> p n t", n=2), SHG, ALU.mult, t, tu)
        free[1] = [t_sh]
        H2 = AR[:, 0:2048].rearrange("p (t d) -> p t d", t=2)
        for t in range(2):
            for half in range(2):
                b = 6 + half
                PE.wait(free[b], t_id, t_h)
                for c in range(4):
                    tok = tr(bank[b][:, c * 128:c * 128 + 128], H[:, 4 * half + c, t * 128:t * 128 + 128],
                             last=(c == 3))
                t_H2 = act(H2[:, t, half * 512:half * 512 + 512], bank[b][:, :], ACT.Copy, tok, t_m, t_ln)
                free[b] = [t_H2]
        PE.wait(t_gate, free[2], free[3], free[4], free[5], t_const, t_id)
        mm(bank[2][0:64, 0:128], mk[0], triS[:, :], True, True)
        mm(bank[2][0:64, 128:256], mk[0], ones[:, :], True, False)
        mm(bank[2][0:64, 128:256], mk[1], triS[:, :], False, True)
        mm(bank[4][0:64, 0:1], mk[0], ones[:, 0:1], True, False)
        t_cnt = mm(bank[4][0:64, 0:1], mk[1], ones[:, 0:1], False, True, last=True)
        for t in range(2):
            tr(bank[3][0:64, t * 128:t * 128 + 128], mk[t])
            t_T = tr(bank[3][0:64, 256 + t * 128:384 + t * 128], gate[:, t * 64:t * 64 + 64], last=(t == 1))
        t = ts(DV, mi[:, 0:4], thr[0:64, :], bank[4][0:64, 0:1], None, ALU.is_lt, None, t_cnt, t_io, normed)
        free[4] = [t]
        t_nb = DV.do(lambda e: e.tensor_reduce(mi[:, 4:5], mi[:, 0:4], AX.X, ALU.add), t)
        mm(bank[5][0:64, 0:1], triS[0:64, 0:64], mi[:, 4:5], True, True, t_nb)
        tok = mm(bank[5][0:1, 4:5], mi[:, 4:5], ones[0:64, 0:1], True, True, last=True)
        t = DV.do(lambda e: e.tensor_copy(mi[:, 5:6], bank[5][0:64, 0:1]), tok)
        DV.do(lambda e: e.tensor_copy(tab[0:1, NBLK:NBLK + 1], bank[5][0:1, 4:5]))
        free[5] = [(s_dve, DV.count)]
        t1 = tt(DV, mi[:, 6:7], mi[:, 5:6], mi[:, 4:5], ALU.add, t)
        t2 = ts(DV, mi[:, 7:8], mi[:, 5:6], float(BLK), 8192.0, ALU.mult, ALU.add, t)
        t = ts(DV, OH, vI[0:64, :], mi[:, 5:6], None, ALU.is_ge, None, t, normed)
        t_OH = stt(OH, vI[0:64, :], mi[:, 6:7], OH, ALU.is_lt, ALU.mult, t, t1)
        t = ts(DV, posT, bank[2][0:64, 0:256], mi[:, 7:8], None, ALU.add, None, t2, t_cnt)
        free[2] = [t]
        t = tt(DV, posT, posT, bank[3][0:64, 0:256], ALU.mult, t, t_T)
        t_pos = ts(DV, posT, posT, -8192.0, None, ALU.add, None, t)
        t_gT = DV.do(lambda e: e.tensor_copy(gateT, bank[3][0:64, 256:512]), t_T)
        free[3] = [t_gT]
        PE.wait(t_OH, t_pos, t_gT, free[4], free[2])
        tok = mm(bank[4][0:1, 0:NBLK], eI[0:64, :], OH, True, True, last=True)
        for t in range(2):
            mm(bank[2][:, t * NBLK:t * NBLK + NBLK], posT[:, t * 128:t * 128 + 128], OH, True, True)
            tok2 = mm(bank[2][:, (2 + t) * NBLK:(3 + t) * NBLK], gateT[:, t * 128:t * 128 + 128], OH, True, True,
                      last=(t == 1))
        t_tab = DV.do(lambda e: e.tensor_copy(tab[0:1, 0:NBLK], bank[4][0:1, 0:NBLK]), tok)
        free[4] = [t_tab]
        t = tt(DV, v2(relp), v2(bank[2][:, 0:192]), v64.unsqueeze(1).to_broadcast([128, 2, NBLK]), ALU.subtract, tok2)
        t_rel = DV.do(lambda e: e.tensor_copy(gV, bank[2][:, 192:384]))
        free[2] = [t_rel]

        w = tile_in(a["sh_down"][0])
        PE.wait(t_sh)
        for j in range(8):
            for i in range(2):
                tok = mm(bank[4 + j // 2][:, (j % 2) * T:(j % 2) * T + T],
                         w[:, (2 * j + i) * 128:(2 * j + i) * 128 + 128], SHH[:, i, :],
                         i == 0 and j % 2 == 0, True, free[4 + j // 2], last=(j == 7 and i == 1), skip=True)
        tile_used(tok)

        XG = arena(8, 8, 128)
        SX = [AR[:, (12 + i) * 256:(13 + i) * 256] for i in range(2)]
        GX = [AR[:, (14 + i) * 256:(15 + i) * 256] for i in range(2)]
        GT = [AR[:, (16 + i) * 256:(17 + i) * 256] for i in range(2)]
        HD, SG, HT = AR[:, 18 * 256:19 * 256], AR[:, 19 * 256:20 * 256], AR[:, 20 * 256:21 * 256]
        gsum = [small[:, 0:1], small[:, 1:2]]
        YH, YL = FR[:, 0:1024], FR[:, 1024:2048]
        ST = [FR[:, 2048:2304], FR[:, 2304:2560]]
        slots = [r[:, :] for r in ring] + [AR[:, (25 + 8 * i) * 256:(33 + 8 * i) * 256] for i in range(NX - NS)]
        held = [None] * NX
        for n, (_, tok) in enumerate(stream):
            held[n % NS] = tok
        for n in range(NS, NX):
            held[n] = [t_h, tok2, t_sh]
        sp_load(0, len(stream), None)
        xn = [0]
        q_pair = {}
        regs = {}

        def x_tiles(p):
            out_ = []
            for v in range(2):
                SP.branch(lambda e, v=v: regs.__setitem__(v, e.value_load(
                    tab[0:1, 2 * p + v:2 * p + v + 1], min_val=0, max_val=63)))
            for j in range(3):
                for v in range(2):
                    n = xn[0]
                    xn[0] += 1
                    SP.wait(held[n % NX])
                    held[n % NX] = None
                    SP.branch(lambda e, n=n, j=j, v=v: e.dma_start(
                        slots[n % NX], a["wx"][bass.ds(regs[v], 1), j, :, :].rearrange("a p n -> p (a n)"))
                        .then_inc(s_xr[n % NX], 16))
                    out_.append((n % NX, 16 * (n // NX + 1)))
            return out_

        def select(p):
            s = SX[p % 2].rearrange("p (t v s) -> p t v s", t=2, v=2)
            g = GX[p % 2].rearrange("p (t v s) -> p t v s", t=2, v=2)
            t = tt(DV, s, io64.unsqueeze(1).unsqueeze(1).to_broadcast([128, 2, 2, BLK]),
                   v2(relp)[:, :, 2 * p:2 * p + 2].unsqueeze(3).to_broadcast([128, 2, 2, BLK]), ALU.is_equal,
                   t_rel, q_pair.get(("xg", p - 2)), t_io)
            q_pair["s", p] = t
            q_pair["g", p] = tt(PO, g, s, v2(gV)[:, :, 2 * p:2 * p + 2].unsqueeze(3).to_broadcast([128, 2, 2, BLK]),
                                ALU.mult, t, q_pair.get(("t", p - 2)))

        def turn(p):
            PE.wait(q_pair["g", p], free[2])
            for t in range(2):
                tok = tr(bank[2][:, t * 128:t * 128 + 128], GX[p % 2][:, t * 128:t * 128 + 128], last=(t == 1))
            q_pair["t", p] = tok
            t = act(GT[p % 2], bank[2][:, 0:256], ACT.Copy, tok, q_pair.get(("st", p - 2)), q_pair.get(("y", p - 2)),
                    accum=gsum[p % 2])
            free[2] = [t]
            q_pair["gs", p] = t
            q_pair["st", p] = ts(DV, ST[p % 2], GT[p % 2], 0.0, None, ALU.is_gt, None, t, q_pair.get(("c", p - 2)))

        def gather(p, half):
            b = 1 - half
            PE.wait(q_pair["s", p], free[b], t_H2)
            s = SX[p % 2].rearrange("p (t q) -> p t q", t=2)
            for c in range(4):
                for t in range(2):
                    d = (4 * half + c) * 128
                    tok = mm(bank[b][:, c * 128:c * 128 + 128], H2[:, t, d:d + 128], s[:, t, :], t == 0, t == 1,
                             last=(c == 3 and t == 1))
            q_pair["xg", p] = tok
            o = XG[:, 4 * half:4 * half + 4, :]
            i = bank[b][:, :].rearrange("p (c s) -> p c s", c=4)
            if half == 0:
                t = act(o, i, ACT.Copy, tok, q_pair.get(("gu", p - 1)))
            else:
                t = DV.do(lambda e: e.tensor_copy(o, i), tok, q_pair.get(("gu", p - 1)))
            free[b] = [t]
            q_pair["x", p, half] = t

        def pair(p):
            tiles = x_tiles(p)
            PE.wait(free[0])
            for half in range(2):
                PE.wait(q_pair["x", p, half])
                for v in range(2):
                    n, val = tiles[2 * half + v]
                    PE.wait((s_xr[n], val))
                for k in range(4):
                    for v in range(2):
                        tok = mm(bank[0][64 * v:64 * v + 64, :], XG[:, 4 * half + k, 64 * v:64 * v + 64],
                                 slots[tiles[2 * half + v][0]][:, k * 512:k * 512 + 512],
                                 half == 0 and k == 0, half == 1 and k == 3, last=(k == 3 and v == 1))
                for v in range(2):
                    held[tiles[2 * half + v][0]] = tok
            q_pair["gu", p] = tok
            t = act(SG, bank[0][:, 0:256], ACT.Silu, tok, q_pair.get(("hd", p - 1)))
            t = tt(DV, HD, bank[0][:, 256:512], SG, ALU.mult, t, q_pair.get(("ht", p - 1)))
            free[0] = [t]
            q_pair["hd", p] = t
            if 2 * p + 2 < NBLK:
                turn(p + 1)
                gather(p + 1, 0)
            PE.wait(t, free[2], t_id)
            for i in range(2):
                tok = tr(bank[2][:, i * 128:i * 128 + 128], HD[:, i * 128:i * 128 + 128], last=(i == 1))
            q_pair["ht", p] = tok
            t = act(HT, bank[2][:, 0:256], ACT.Copy, tok, q_pair.get(("d", p - 1)))
            free[2] = [t]
            if 2 * p + 2 < NBLK:
                gather(p + 1, 1)
            if 2 * p + 4 < NBLK:
                select(p + 2)
            for h in range(2):
                b = 3 if h == 0 else 1
                PE.wait(free[b], t)
                for v in range(2):
                    n, val = tiles[4 + v]
                    PE.wait((s_xr[n], val))
                for i in range(2):
                    for v in range(2):
                        o = i * 1024 + h * 512
                        tok = mm(bank[b][64 * v:64 * v + 64, :], HT[:, i * 128 + 64 * v:i * 128 + 64 * v + 64],
                                 slots[tiles[4 + v][0]][:, o:o + 512], i == 0, i == 1, last=(i == 1 and v == 1))
                yh, yl = YH[:, h * 512:h * 512 + 512], YL[:, h * 512:h * 512 + 512]
                gs = gsum[p % 2]
                t1 = act(yh, bank[b][:, :], ACT.Copy, tok, q_pair["gs", p], q_pair.get(("c", p - 1)), scale=gs)
                t1 = stt(yl, bank[b][:, :], gs, yh.bitcast(fp), ALU.mult, ALU.subtract, t1, q_pair.get(("c", p - 1)))
                free[b] = [t1]
                q_pair["y", p, h] = t1
            q_pair["y", p] = t1
            q_pair["d", p] = tok
            for v in range(2):
                held[tiles[4 + v][0]] = tok
            for j in range(8):
                PE.wait(q_pair["y", p, j // 4], q_pair["st", p])
                o = bank[4 + j // 2][:, (j % 2) * T:(j % 2) * T + T]
                mm(o, YH[:, j * 128:j * 128 + 128], ST[p % 2], False, True, skip=True)
                tok = mm(o, YL[:, j * 128:j * 128 + 128], ST[p % 2], False, True, last=(j == 7), skip=True)
            q_pair["c", p] = tok

        select(0)
        select(1)
        turn(0)
        gather(0, 0)
        gather(0, 1)
        queues = (PE, AC, DV, PO, SP)
        for q in queues:
            q.wait(t_tab)
        nests = {}
        for q in queues:
            def load(e, q=q):
                nests[id(q)] = (ExitStack(), e.value_load(tab[0:1, NBLK:NBLK + 1], min_val=0, max_val=NBLK))
            q.branch(load)
        before = [dict(q.seen) for q in queues]
        for p in range(NBLK // 2):
            if p >= 16:
                for q in queues:
                    q.branch(lambda e, q=q, p=p: nests[id(q)][0].enter_context(e.If(nests[id(q)][1] > 2 * p)))
            pair(p)
        for q, seen in zip(queues, before):
            q.branch(lambda e, q=q: nests[id(q)][0].close())
            q.seen = seen
        PE.sem, AC.sem, DV.sem, PO.sem = s_pe2, s_act2, s_dve2, s_pool2
        for q in (PE, AC, DV, PO):
            q.count = 0
        tok = mm(bank[3][0:32, 0:1], ones[:, 0:32], ones[:, 0:1], True, True, last=True)
        e_act = act(small[:, 2:3], ones[:, 0:1], ACT.Copy)
        e_dve = DV.do(lambda e: e.memset(small[:, 3:4], 0.0))
        e_pool = PO.do(lambda e: e.memset(small[:, 4:5], 0.0))
        late[0] = len(stream)
        t_over = [tok, e_act, e_dve, e_pool]
        for b in range(8):
            free[b] = list(t_over)
        t_x2 = []
        for i in range(4):
            t_x2 += residual([tok, t_xa, t_mod[0, 23]], 4 + i, i, 40, 0)
        t_ln = norm(X, Q8, t_x2, 2, 3, True, 1024.0, 1e-5)
        t_x2 = affine(X, X, lambda k: P("ln2g", k), lambda k: P("ln2b", k), t_ln)

        XC = arena(0, 8)
        t_cp = [DV.do(lambda e, k=k, XC=XC: e.tensor_copy(XC[:, k, :], X[:, k, :]), t_x2[k], t_over) for k in range(8)]
        t_ln = norm(XC, Q8, t_cp, 2, 3, False, 1024.0, 1e-6)
        t_h = affine(H, XC, lambda k: M(8 + k, 1), lambda k: M(k, 1), t_ln, t_mod[1, 3], t_mod[1, 7], tok)
        w_order += tiles["qk"] + tiles["w_out2"] + tiles["w_up2"]
        t_hs = split(H, t_h)

        BIAS = arena(70, 8, 384)
        t_bias = SP
        t_bias = AC.dma(BIAS, a["relb"], s_bias, 16, t_ln)
        for o in (0, 256):
            t_bias = PO.do(lambda e, o=o: e.memset(BIAS[0:64, :, o + 64:o + 128], -1e30), t_bias)
        QK = arena(8, 16)
        VV = arena(24, 4, 512)
        t_qk = {}
        for i in range(8):
            b = next_bank()
            tok = gemm(tiles["qk"][i], t_hs, b)
            t = act(QK[:, 2 * i:2 * i + 2, :], bank[b][:, :].rearrange("p (n t) -> p n t", n=2), ACT.Copy, tok)
            free[b] = [t]
            t_qk[2 * i] = t_qk[2 * i + 1] = t
        t_v = {}
        for sec in range(2):
            for half in range(2):
                w = tile_in(a["vv"][2 * sec + half])
                for t in range(2):
                    for k in range(4):
                        kk = 4 * half + k
                        tok = mm(bank[4 + t][:, :], H[:, kk, t * 128:t * 128 + 128], w[:, k * 512:k * 512 + 512],
                                 kk == 0, kk == 7, t_h[kk], free[4 + t] if kk == 0 else None,
                                 last=(k == 3))
                    if half == 1:
                        t_v[sec, t] = DV.do(lambda e, sec=sec, t=t: e.tensor_copy(
                            VV[:, 2 * sec + t, :], bank[4 + t][:, :]), tok)
                        free[4 + t] = [t_v[sec, t]]
                tile_used(tok)

        OA, OB = arena(32, 4), arena(36, 4)
        SB = [arena(40 + 6 * i, 1, 384)[:, 0, :] for i in range(2)]
        PT = [arena(42 + 6 * i, 1, 384)[:, 0, :] for i in range(2)]
        ZB = [arena(52 + 8 * i, 1, 384)[:, 0, :] for i in range(2)]
        EB = [arena(54 + 8 * i, 1, 384)[:, 0, :] for i in range(2)]
        SPB = [arena(56 + 8 * i, 1, 384)[:, 0, :] for i in range(2)]
        nm = [small[:, 512 + 8 * i:520 + 8 * i] for i in range(2)]
        MK = arena(68, 1, 384)[:, 0, :]
        for o, s in ((0, triS), (128, ones), (256, triS)):
            t_mk = PO.do(lambda e, o=o, s=s: e.tensor_copy(MK[:, o:o + 128], s[:, :]), t_const, t_over)
        ta, tb = {}, {}

        def a_scores(h):
            r0, cq = (h % 2) * 64, h // 2
            q, k = QK[r0:r0 + 64, cq, :], QK[r0:r0 + 64, 4 + cq, :]
            PE.wait(t_qk[cq], t_qk[4 + cq], free[2])
            mm(bank[2][:, 0:128], q[:, 0:128], k[:, 0:128], True, True)
            tok = mm(bank[2][:, 128:384], q[:, 128:256], k[:, 0:256], True, True, last=True)
            S, n = SB[h % 2], nm[h % 2]
            t = stt(S, bank[2][:, 0:384], 0.125, BIAS[:, h, :], ALU.mult, ALU.add, tok, t_bias, ta.get(("pt", h - 2)))
            free[2] = [t]
            DV.do(lambda e: e.tensor_reduce(n[:, 0:1], S[:, 0:128], AX.X, ALU.max), t)
            t = DV.do(lambda e: e.tensor_reduce(n[:, 1:2], S[:, 128:384], AX.X, ALU.max), t)
            t = ts(DV, n[:, 2:4], n[:, 0:2], -1.0, None, ALU.mult, None, t)
            act(S[:, 0:128], S[:, 0:128], ACT.Exp, t, bias=n[:, 2:3], accum=n[:, 4:5])
            t = act(S[:, 128:384], S[:, 128:384], ACT.Exp, t, bias=n[:, 3:4], accum=n[:, 5:6])
            t = DV.do(lambda e: e.reciprocal(n[:, 6:8], n[:, 4:6]), t)
            ts(DV, S[:, 0:128], S[:, 0:128], n[:, 6:7], None, ALU.mult, None, t)
            ta["p", h] = ts(DV, S[:, 128:384], S[:, 128:384], n[:, 7:8], None, ALU.mult, None, t)

        def a_turn(h):
            PE.wait(ta["p", h], free[3], t_id)
            for i in range(3):
                tok = tr(bank[3][:, i * 128:i * 128 + 128], SB[h % 2][:, i * 128:i * 128 + 128], last=(i == 2))
            ta["pt", h] = tok
            t = act(PT[h % 2], bank[3][:, 0:384], ACT.Copy, tok, ta.get(("o", h - 2)))
            free[3] = [t]
            ta["c", h] = t

        def a_out(h):
            r0, b = (h % 2) * 64, 6
            PE.wait(ta["c", h], t_v[0, 0], t_v[0, 1], free[b] if h % 2 == 0 else None)
            o = bank[b][r0:r0 + 64, 0:T]
            mm(o, VV[:, 0, h * 64:h * 64 + 64], PT[h % 2][:, 0:256], True, False)
            tok = mm(o[:, 128:256], VV[:, 1, h * 64:h * 64 + 64], PT[h % 2][:, 256:384], False, True, last=True)
            ta["o", h] = tok
            if h % 2:
                t = act(OA[:, h // 2, :], bank[b][:, 0:T], ACT.Copy, tok)
                free[b] = [t]
                ta["e", h // 2] = t

        def b_scores(h):
            r0, cq = (h % 2) * 64, h // 2
            q, k = QK[r0:r0 + 64, 8 + cq, :], QK[r0:r0 + 64, 12 + cq, :]
            PE.wait(t_qk[8 + cq], t_qk[12 + cq], free[4])
            mm(bank[4][:, 0:256], k[:, 0:128], q[:, 0:256], True, True)
            tok = mm(bank[4][:, 256:384], k[:, 128:256], q[:, 128:256], True, True, last=True)
            Zb, E, S = ZB[h % 2], EB[h % 2], SPB[h % 2]
            t = act(Zb, bank[4][:, 0:384], ACT.Copy, tok, tb.get(("w", h - 2)), scale=0.125)
            free[4] = [t]
            t1 = act(E, Zb, ACT.Abs, t, tb.get(("o", h - 2)))
            t1 = act(E, E, ACT.Exp, t1, scale=-1.0)
            t1 = act(E, E, ACT.Ln, t1, bias=1.0)
            t2 = stt(S, Zb, 0.0, E, ALU.max, ALU.add, t1, tb.get(("r", h - 2)))
            tb["s", h] = tt(PO, S, S, MK, ALU.mult, t2, t_mk)

        def b_tail(h):
            Zb, E, S = ZB[h % 2], EB[h % 2], SPB[h % 2]
            PE.wait(tb["s", h], free[5], t_const)
            mm(bank[5][:, 0:256], triG[:, :], S[:, 0:256], True, False)
            mm(bank[5][:, 128:256], ones[:, :], S[:, 256:384], False, True)
            tok = mm(bank[5][:, 256:384], triG[:, :], S[:, 256:384], True, True, last=True)
            tb["r", h] = tok
            t = tt(DV, Zb, Zb, bank[5][:, 0:384], ALU.subtract, tok)
            free[5] = [t]
            t = ts(DV, Zb, Zb, 0.0, None, ALU.min, None, t)
            t = act(E, Zb, ACT.Exp, t)
            tb["w", h] = t
            tb["m", h] = tt(PO, E, E, MK, ALU.mult, t)

        def b_out(h):
            r0, b = (h % 2) * 64, 7
            PE.wait(tb["m", h], t_v[1, 0], t_v[1, 1], free[b] if h % 2 == 0 else None)
            o = bank[b][r0:r0 + 64, 0:T]
            mm(o, VV[:, 2, h * 64:h * 64 + 64], EB[h % 2][:, 0:256], True, False)
            tok = mm(o[:, 128:256], VV[:, 3, h * 64:h * 64 + 64], EB[h % 2][:, 256:384], False, True, last=True)
            tb["o", h] = tok
            if h % 2:
                t = act(OB[:, h // 2, :], bank[b][:, 0:T], ACT.Copy, tok)
                free[b] = [t]
                tb["e", h // 2] = t

        for s in range(10):
            if s >= 2:
                a_out(s - 2)
                b_out(s - 2)
            if s < 8:
                a_scores(s)
                b_scores(s)
            if 1 <= s < 9:
                a_turn(s - 1)
                b_tail(s - 1)
        t_o = []
        for O, tk in ((OA, ta), (OB, tb)):
            t_o += norm(O, Q8, [tk["e", k] for k in range(4)], 2, 3, False, 512.0, 1e-6, chunks=4)
        OO = arena(32, 8)
        t_o = [ts(DV, OO[:, k, :], OO[:, k, :], P("gab", k), None, ALU.mult, None, t_o[k]) for k in range(8)]
        t_o = split(OO, t_o)
        t_x3 = []
        for i in range(4):
            b = next_bank()
            tok = gemm(tiles["w_out2"][i], t_o, b)
            t_x3 += residual([tok, t_mod[1, 11]], b, i, 16, 1)
        XC = arena(0, 8)
        t_cp = [DV.do(lambda e, k=k, XC=XC: e.tensor_copy(XC[:, k, :], X[:, k, :]), t_x3[k]) for k in range(8)]
        t_ln = norm(XC, Q8, t_cp, 2, 3, False, 1024.0, 1e-6)
        t_h = affine(H, XC, lambda k: M(32 + k, 1), lambda k: M(24 + k, 1), t_ln, t_mod[1, 15], t_mod[1, 19])
        t_hs = split(H, t_h)
        HF = arena(8, 22)
        CV = [arena(30 + 2 * i, 2) for i in range(4)]
        t_f = {}
        for i in range(22):
            b = next_bank()
            tok = gemm(tiles["w_up2"][i], t_hs, b)
            cv = CV[i % 4]
            for c in range(2):
                t = conv(cv[:, c, :], bank[b][:, c * T:c * T + T], "cw2", 44, 3, i + 22 * c, P("cb2", i + 22 * c),
                         [tok, t_f.get(i - 4)] if c == 0 else tok)
            free[b] = [t]
            t = act(cv[:, 0, :], cv[:, 0, :], ACT.Silu, t)
            t_f[i] = tt(PO, HF[:, i, :], cv[:, 0, :], cv[:, 1, :], ALU.mult, t)
        t_x4 = []
        n = 0
        for j in range(8):
            if j % 2 == 0:
                b = next_bank()
            for k in range(22):
                if n % 16 == 0:
                    w = tile_in(a["w_down2"][n // 16])
                o = (n % 16) * 128
                n += 1
                tok = mm(bank[b][:, (j % 2) * T:(j % 2) * T + T], w[:, o:o + 128], HF[:, k, :], k == 0, k == 21,
                         free[b] if k == 0 and j % 2 == 0 else None, t_f[k], last=(k == 21 or n % 16 == 0))
                if n % 16 == 0:
                    tile_used(tok)
            if j % 2:
                t_x4 += residual([tok, t_mod[1, 23]], b, j // 2, 40, 1)
        t_ln = norm(X, Q8, t_x4, 2, 3, False, 1024.0, 1e-6)
        t_y = [ts(DV, H[:, k, :], X[:, k, :], P("fg", k), None, ALU.mult, None, t_ln[k]) for k in range(8)]
        AC.dma(out, H[:, :, :], s_out, 16, t_y)
        AC.wait((s_out, 16))

        sp_load(late[0], len(stream), t_over)

        block = ctx.enter_context(nc.Block())

        @block.sync
        def _(eng):
            SP.play(eng)

        @block.scalar
        def _(eng):
            AC.play(eng)

        @block.vector
        def _(eng):
            DV.play(eng)

        @block.gpsimd
        def _(eng):
            PO.play(eng)

        @block.tensor
        def _(eng):
            PE.play(eng)


def pack_blocks(w):
    k, n = w.shape
    b = w.reshape(k // 128, 128, n // 128, 128).transpose(2, 0, 1, 3).reshape(-1, 16, 128, 128)
    return b.transpose(0, 2, 1, 3).reshape(-1, 128, 2048)


def lay_out(np, x):
    chunk = lambda v: v.reshape(-1, 128).T
    a = {}
    w_in = x["w_in"][0]
    pair = lambda m, first, second: np.concatenate(
        [np.concatenate([m[:, first + 128 * j:first + 128 * j + 128], m[:, second + 128 * j:second + 128 * j + 128]],
                        axis=1) for j in range((second - first) // 128)], axis=1)
    a["w_in"] = pack_blocks(np.concatenate(
        [w_in[:, 4096:6144], w_in[:, 2048:4096], w_in[:, 0:2048], pair(w_in, 7200, 8224), w_in[:, 6176:7200],
         w_in[:, 9248:11296]], axis=1))
    a["wdt"] = w_in[:, 6144:6176].reshape(8, 128, 32).transpose(1, 0, 2)
    a["wrt"] = x["router_w"][0].reshape(8, 128, 64).transpose(1, 0, 2)
    a["dtb"], a["alog"], a["rb"] = x["ssd_dt_bias"][0], x["ssd_A_log"][0], x["router_bias"][0]
    a["xT"] = x["x"][0].T.reshape(8, 128, T).transpose(1, 0, 2)
    a["ada"], a["ada2"] = (x[n][0].reshape(2, 4, 128, 12, 512).transpose(3, 0, 2, 1, 4).reshape(24, 128, 2048)
                           for n in ("w_ada", "w_ada_2"))
    a["ssd_out"], a["sc_out"], a["w_o"] = (pack_blocks(x[n][0]) for n in ("w_ssd_out", "w_sc_out", "w_o"))
    for n in ("sh_gate", "sh_up", "sh_down"):
        a[n] = pack_blocks(x[n][0])
    g, u, d = x["w_gate"][0], x["w_up"][0], x["w_down"][0]
    wx = np.empty((N_EXP, 3, 128, 2048), g.dtype)
    wx[:, 0:2].reshape(N_EXP, 2, 128, 4, 2, 256)[:] = np.stack(
        [w.reshape(N_EXP, 2, 4, 128, 256).transpose(0, 1, 3, 2, 4) for w in (g, u)], axis=4)
    wx[:, 2] = d.reshape(N_EXP, 2, 128, 1024).transpose(0, 2, 1, 3).reshape(N_EXP, 128, 2048)
    a["wx"] = wx
    w2 = x["w_in_2"][0]
    a["qk"] = pack_blocks(np.concatenate([w2[:, 0:1024], w2[:, 1536:2560]], axis=1))
    a["vv"] = np.concatenate([w2[:, c:c + 512].reshape(2, 4, 128, 512).transpose(0, 2, 1, 3).reshape(2, 128, 2048)
                              for c in (1024, 2560)], axis=0)
    a["w_out2"], a["w_down2"] = pack_blocks(x["w_out_2"][0]), pack_blocks(x["w_down_2"][0])
    a["w_up2"] = pack_blocks(pair(x["w_up_2"][0], 0, 2816))
    taps = lambda w: np.concatenate([chunk(w[k]) for k in range(w.shape[0])], axis=1)
    cols = {
        "b_ada": chunk(x["b_ada"][0]), "cw": taps(x["ssd_conv_w"][0]), "cb": chunk(x["ssd_conv_b"][0]),
        "D": chunk(np.repeat(x["ssd_D"][0], 64)), "nw": chunk(x["ssd_norm_w"][0]), "scw": taps(x["sc_conv_w"][0]),
        "ln1g": chunk(x["ln1_g"][0]), "ln1b": chunk(x["ln1_b"][0]), "ln2g": chunk(x["ln2_g"][0]),
        "ln2b": chunk(x["ln2_b"][0]), "b_ada2": chunk(x["b_ada_2"][0]),
        "gab": chunk(np.concatenate([x["g_a_2"][0], x["g_b_2"][0]])), "cw2": taps(x["conv_w_2"][0]),
        "cb2": chunk(x["conv_b_2"][0]), "fg": chunk(x["final_g_2"]), "c": chunk(x["c"][0]), "c2": chunk(x["c_2"][0]),
    }
    a["par"] = np.concatenate([cols[n] for n in _PAR], axis=1)
    q, k = np.arange(128)[:, None], np.arange(128)[None, :]
    at = lambda d: np.clip(d, -128, 128) + 128
    idx = np.concatenate([at(q - k), at(q + 128 - k), at(q - k)], axis=1)
    a["relb"] = x["rel_bias_2"][0][:, idx].transpose(1, 0, 2)
    return a


def kernel(**inputs):
    import numpy as np
    import concourse.bacc as bacc
    from concourse.bass_utils import run_bass_kernel_spmd

    x = {n: np.asarray(v) for n, v in inputs.items()}
    laid = {n: np.ascontiguousarray(v) for n, v in lay_out(np, x).items()}
    nc = bacc.Bacc("TRN2", target_bir_lowering=False, num_devices=1)
    aps = {n: nc.dram_tensor(f"in_{n}", v.shape, mybir.dt.from_np(v.dtype), kind="ExternalInput").ap()
           for n, v in laid.items()}
    out = nc.dram_tensor("out_x", (128, 8, T), mybir.dt.float32, kind="ExternalOutput").ap()
    build(nc, aps, out)
    r = run_bass_kernel_spmd(nc, [{f"in_{n}": v for n, v in laid.items()}], core_ids=[0])
    y = r.results[0]["out_x"]
    return np.ascontiguousarray(y.transpose(2, 1, 0).reshape(1, T, 1024))
```

```python
import concourse.bass as bass
from concourse import mybir
from contextlib import ExitStack

T = 256
NS = 4
POOL_HALF = (1,)
NW = 3
NX = 12
NIT = 40
BLK = 32
NBLK = 4 * NIT
ALPHA = 2.0 ** 0.25
N_EXP = 64

_PAR = {}


def par_columns():
    at = 0
    for name, n in (("b_ada", 48), ("cw", 128), ("cb", 32), ("D", 16), ("nw", 16), ("scw", 24),
                    ("ln1g", 8), ("ln1b", 8), ("ln2g", 8), ("ln2b", 8), ("b_ada2", 48), ("gab", 8),
                    ("cw2", 132), ("cb2", 44), ("fg", 8), ("c", 8), ("c2", 8)):
        _PAR[name] = (at, n)
        at += n
    return at


NPAR = par_columns()


class Queue:

    def __init__(self, sem):
        self.sem, self.count, self.items, self.seen = sem, 0, [], {}

    def wait(self, *tokens):
        for t in tokens:
            if t is None:
                continue
            if isinstance(t, list):
                self.wait(*t)
                continue
            sem, value = t
            if self.seen.get(sem.name, 0) < value:
                self.seen[sem.name] = value
                self.items.append(lambda e, s=sem, v=value: e.wait_ge(s, v))

    def do(self, fn, *tokens):
        self.wait(*tokens)
        self.count += 1
        self.items.append(lambda e, f=fn, s=self.sem: f(e).then_inc(s, 1))
        return (self.sem, self.count)

    def quiet(self, fn, *tokens):
        self.wait(*tokens)
        self.items.append(fn)

    def branch(self, fn):
        self.items.append(fn)

    def dma(self, out, in_, sem, value, *tokens):
        self.wait(*tokens)
        self.items.append(lambda e: e.dma_start(out, in_).then_inc(sem, 16))
        return (sem, value)

    def play(self, eng):
        for item in self.items:
            item(eng)


def build(nc, a, out):
    fp = mybir.dt.float32
    fr = mybir.dt.float32r
    ALU = mybir.AluOpType
    ACT = mybir.ActivationFunctionType
    AX = mybir.AxisListType
    ctx = ExitStack()
    with ctx:
        def sb(name, shape):
            return ctx.enter_context(nc.sbuf_tensor(name, shape, fp))

        def sem(name):
            return ctx.enter_context(nc.semaphore(name))

        ring = [sb(f"ring{i}", [128, 2048]) for i in range(NS)]
        X = sb("X", [128, 8, T])
        H = sb("H", [128, 8, T])
        par = sb("par", [128, NPAR])
        ones = sb("ones", [128, 128])
        ident = sb("ident", [128, 128])
        triU = sb("triU", [128, 128])
        triS = sb("triS", [128, 128])
        triG = sb("triG", [128, 128])
        small = sb("small", [128, 2048])
        wdt = small[:, 1280:1536].rearrange("p (k n) -> p k n", k=8)
        wrt = sb("wrt", [128, 8, 64])
        rowb, mod = small[:, 8:136], small[:, 136:232]
        AR = sb("AR", [128, 90 * 256])
        FR = ctx.enter_context(nc.sbuf_tensor("FR", [128, (24 + 8 * NW) * 256], fr))
        tab = ctx.enter_context(nc.sbuf_tensor("tab", [1, NBLK + NIT + 4], mybir.dt.int32))
        bank = [ctx.enter_context(nc.psum_tensor(f"bank{i}", [128, 512], fp)) for i in range(8)]

        def arena(kb, n, cols=T):
            return AR[:, kb * 256:kb * 256 + n * cols].rearrange("p (n t) -> p n t", t=cols)

        s_pe, s_act, s_dve, s_pool = sem("s_pe"), sem("s_act"), sem("s_dve"), sem("s_pool")
        s_xr = [sem(f"s_xr{i}") for i in range(NX)]
        s_late = [sem(f"s_late{i}") for i in range(NS)]
        s_pe2, s_act2, s_dve2, s_pool2 = sem("s_pe2"), sem("s_act2"), sem("s_dve2"), sem("s_pool2")
        s_ring = [sem(f"s_ring{i}") for i in range(NS)]
        s_par, s_x, s_wdt, s_wrt, s_row, s_bias, s_out = (
            sem("s_par"), sem("s_x"), sem("s_wdt"), sem("s_wrt"), sem("s_row"), sem("s_bias"), sem("s_out"))
        PE, AC, DV, PO, SP = Queue(s_pe), Queue(s_act), Queue(s_dve), Queue(s_pool), Queue(None)

        def tt(q, o, x, y, op, *w):
            return q.do(lambda e: e.tensor_tensor(o, x, y, op), *w)

        def ts(q, o, x, s1, s2, op0, op1, *w):
            if s2 is None:
                return q.do(lambda e: e.tensor_scalar(o, x, s1, None, op0), *w)
            return q.do(lambda e: e.tensor_scalar(o, x, s1, s2, op0, op1), *w)

        def stt(o, x, s, y, op0, op1, *w):
            return DV.do(lambda e: e.scalar_tensor_tensor(out=o, in0=x, scalar=s, in1=y, op0=op0, op1=op1), *w)

        def act(o, x, f, *w, bias=0.0, scale=1.0, accum=None):
            if accum is not None:
                return AC.do(lambda e: e.activation(o, x, f, bias=bias, scale=scale, accum_out=accum), *w)
            return AC.do(lambda e: e.activation(o, x, f, bias=bias, scale=scale), *w)

        def mm(o, l, r, start, stop, *w, last=False, skip=False):
            f = lambda e: e.matmul(o, l, r, start=start, stop=stop, skip_group_check=skip)
            if last:
                return PE.do(f, *w)
            PE.quiet(f, *w)

        def tr(o, i, *w, last=False):
            k = i.shape[0]
            f = lambda e: e.transpose(o, i, ident[0:k, 0:k])
            if last:
                return PE.do(f, *w)
            PE.quiet(f, *w)

        normed = []
        free = [[] for _ in range(8)]
        late = [0]
        stream = []

        def tile_in(src, q=PE):
            n = len(stream) - late[0]
            stream.append([src, None])
            q.wait(((s_late if late[0] else s_ring)[n % NS], 16 * (n // NS + 1)))
            return ring[n % NS]

        def tile_used(tok):
            stream[-1][1] = tok

        def sp_load(first, end, start):
            for n in range(first, end):
                m = n - late[0]
                SP.dma(ring[m % NS][:, :], stream[n][0], (s_late if late[0] else s_ring)[m % NS], 0,
                       stream[n - NS][1] if m >= NS else start)

        def P(name, i=0, n=1):
            at = _PAR[name][0] + i
            return par[:, at:at + n]

        t_par = AC.dma(par[:, :], a["par"], s_par, 16)
        t_x = AC.dma(X[:, :, :], a["xT"], s_x, 16)
        t_wdt = AC.dma(wdt, a["wdt"], s_wdt, 16)
        AC.dma(rowb[:, 0:32], a["dtb"].partition_broadcast(128), s_row, 16)
        AC.dma(rowb[:, 32:64], a["alog"].partition_broadcast(128), s_row, 32)
        t_row = AC.dma(rowb[:, 64:128], a["rb"].partition_broadcast(128), s_row, 48)
        t_wrt = AC.dma(wrt[:, :, :], a["wrt"], s_wrt, 16)

        t_ones = PO.do(lambda e: e.memset(ones[:, :], 1.0))
        t_z = PO.do(lambda e: e.memset(ident[:, :], 0.0))
        t_id = PO.do(lambda e: e.affine_select(out=ident[:, :], in_=ident[:, :], compare_op=ALU.not_equal,
                     fill=1.0, base=0, pattern=[[-1, 128]], channel_multiplier=1), t_z)
        def tri(dst, step, base):
            return PO.do(lambda e: e.affine_select(out=dst[:, :], in_=ones[:, :], compare_op=ALU.is_ge,
                         fill=0.0, base=base, pattern=[[step, 128]], channel_multiplier=-step), t_ones)
        t_triU = tri(triU, 1, 0)
        t_triS = tri(triS, 1, -1)
        t_triG = tri(triG, -1, 0)
        t_const = t_triG

        cz = sb("cz", [128, 2, 8, 32])
        RA = [sb(f"RA{i}", [128, 512]) for i in range(2)]
        t_z = PO.do(lambda e: e.memset(cz[:, :, :, :], 0.0))
        t_cz = act(cz[:, :, :, 0], P("c", 0, 16).rearrange("p (a k) -> p a k", a=2), ACT.Silu, t_par, t_z)
        t_mod = {}
        ada_open = []
        t_ra = {}
        ada_n = [0]

        def ada_group(which, i, b):
            src = a["ada2" if which else "ada"]
            n = ada_n[0]
            ada_n[0] += 1
            for half in range(2):
                w = tile_in(src[2 * i + half])
                PE.wait(t_cz, free[b])
                for k in range(4):
                    tok = mm(bank[b][32 * k:32 * k + 32, :], cz[:, which, 4 * half + k, :],
                             w[:, k * 512:k * 512 + 512], half == 0, half == 1, last=(k == 3))
                tile_used(tok)
            t = act(RA[n % 2][:, :], bank[b][:, :], ACT.Copy, tok, t_ra.get(n - 2))
            free[b] = [t]
            ada_open.append((which, i, n, t))

        def ada_close(b):
            if not ada_open:
                return
            which, i, n, t = ada_open.pop(0)
            PE.wait(t, free[b], t_id)
            for j in range(4):
                tok = tr(bank[b][:, j * 128:j * 128 + 128], RA[n % 2][:, j * 128:j * 128 + 128], last=(j == 3))
            t_ra[n] = tok
            at = 48 * which + 4 * i
            t = DV.do(lambda e: e.tensor_reduce(
                mod[:, at:at + 4], bank[b][:, :].rearrange("p (j g c) -> p j g c", j=4, g=4)[:, :, :, 0],
                AX.X, ALU.add), tok)
            free[b] = [t]
            t = tt(DV, mod[:, at:at + 4], mod[:, at:at + 4], P("b_ada2" if which else "b_ada", 4 * i, 4),
                   ALU.add, t)
            if i // 2 in (1, 4):
                t = ts(DV, mod[:, at:at + 4], mod[:, at:at + 4], 1.0, None, ALU.add, None, t)
            for j in (2 * i, 2 * i + 1):
                t_mod[which, j] = t

        def norm(S, O, D, Q, toks, b1, b2, center, rms_n, eps, scale, bias=None, w=(), chunks=8, between=None,
                 parts=None):
            n = chunks
            done = list(toks)
            if center:
                for k in range(n):
                    tok = mm(bank[b1][:, 0:T], ones[:, :], S[:, k, :], k == 0, k == n - 1, t_ones, toks[k],
                             free[b1] if k == 0 else None, last=(k == n - 1))
                if between:
                    between()
                mean = bank[b1][:, 0:T].unsqueeze(1).to_broadcast([128, 2, T])
                done = []
                for p in range(n // 2):
                    p = slice(2 * p, 2 * p + 2)
                    t = stt(O[:, p, :], mean, -1.0 / 1024.0, S[:, p, :], ALU.mult, ALU.add, tok)
                    done += [t, t]
                free[b1] = [done[-1]]
                S = O
            for i in range(n // 2):
                t = act(Q[:, 2 * i:2 * i + 2, :], S[:, 2 * i:2 * i + 2, :], ACT.Square, done[2 * i], done[2 * i + 1])
                for k in (2 * i, 2 * i + 1):
                    tok = mm(bank[b2][:, 0:T], ones[:, :], Q[:, k, :], k == 0, k == n - 1, t, t_ones,
                             free[b2] if k == 0 else None, last=(k == n - 1))
            if between:
                between()
            if callable(w):
                w = w()
            r = small[:, 256:256 + T]
            t = ts(DV, r, bank[b2][:, 0:T], 1.0 / rms_n, eps, ALU.mult, ALU.add, tok, normed)
            free[b2] = [t]
            t = act(r, r, ACT.Sqrt, t)
            t = DV.do(lambda e: e.reciprocal(r, r), t)
            scaled, res, halves = [], [], []
            for k in range(n):
                o = D if bias is None else O
                t1 = stt(o[:, k, :], S[:, k, :], scale(k), r, ALU.mult, ALU.mult, t, *w)
                scaled.append(t1)
            if bias is None:
                res = scaled
            else:
                for k in range(n):
                    res.append(act(D[:, k, :], O[:, k, :], ACT.Identity, scaled[k], bias=bias(k)))
                    if parts is not None and k % 2:
                        halves.append(split_hi(D, k - 1, res[k - 1:k + 1]))
            for i, th in enumerate(halves):
                parts += split_lo(D, 2 * i, th)
            normed[:] = [t1]
            return res

        def M(i, which=0):
            return mod[:, 48 * which + i:48 * which + i + 1]

        AH, AL = (FR[:, i * 2048:i * 2048 + 2048].rearrange("p (n t) -> p n t", n=8) for i in range(2))
        a_read = []
        w_order = []
        w_split = []
        w_read = []

        def split_next():
            n = len(w_split) // 2
            if n >= len(w_order):
                return
            w = tile_in(w_order[n], AC)
            for c in range(2):
                m = len(w_split)
                o = 6144 + 2048 * (m % NW)
                hi, lo = FR[:, o:o + 1024], FR[:, o + 1024:o + 2048]
                x = w[:, c * 1024:c * 1024 + 1024]
                t = act(hi, x, ACT.Copy, w_read[m - NW] if m >= NW else None)
                t = tt(PO if c in POOL_HALF else DV, lo, x, hi.bitcast(fp), ALU.subtract, t)
                w_split.append((hi, lo, t))
                stream[-1][1] = (stream[-1][1] or []) + [t]

        def split_hi(R, k, toks):
            return act(AH[:, k:k + 2, :], R[:, k:k + 2, :], ACT.Copy, toks, a_read)

        def split_lo(R, k, t):
            t = tt(DV, AL[:, k:k + 2, :], R[:, k:k + 2, :], AH[:, k:k + 2, :].bitcast(fp), ALU.subtract, t)
            return [t, t]

        def split(R, toks, chunks=8):
            res = []
            for k in range(0, chunks, 2):
                res += split_lo(R, k, split_hi(R, k, toks[k:k + 2]))
            return res

        def gemm(src, toks, b):
            n = len(w_read) // 2
            assert w_order[n] is src
            if len(w_split) == 2 * n:
                split_next()
            for c in range(2):
                hi, lo, t = w_split[2 * n + c]
                PE.wait(t)
                for k in range(8):
                    j = k * 128
                    o = bank[b][:, c * T:c * T + T]
                    mm(o, hi[:, j:j + 128], AH[:, k, :], k == 0, False, free[b] if c == k == 0 else None, toks[k])
                    mm(o, hi[:, j:j + 128], AL[:, k, :], False, False)
                    tok = mm(o, lo[:, j:j + 128], AH[:, k, :], False, k == 7, last=(k == 7))
                w_read.append(tok)
            a_read[:] = [tok]
            free[b] = []
            split_next()
            return tok

        pair_n = [0]
        pair_read = {}

        def split_pair(x, *w):
            n = pair_n[0]
            pair_n[0] += 1
            o = 4096 + 1024 * (n % 2)
            xh, xl = FR[:, o:o + 512], FR[:, o + 512:o + 1024]
            v = lambda y: y.rearrange("p (n t) -> p n t", n=2)
            t = act(v(xh), x, ACT.Copy, *w, pair_read.get(n - 2))
            t = tt(DV, v(xl), x, v(xh).bitcast(fp), ALU.subtract, t)
            return xh, xl, t, n

        def by_rows(src, k, n_k, x):
            xh, xl, tx, n = x
            m = len(w_read)
            assert w_order[m // 2] is src
            if len(w_split) == m:
                split_next()
            hi, lo, t = w_split[m]
            PE.wait(t, tx)
            c = (k % 2) * T
            for j in range(8):
                o = bank[4 + j // 2][:, (j % 2) * T:(j % 2) * T + T]
                d = j * 128
                mm(o, hi[:, d:d + 128], xh[:, c:c + T], k == 0 and j % 2 == 0, False,
                   free[4 + j // 2] if k == 0 else None, skip=True)
                mm(o, hi[:, d:d + 128], xl[:, c:c + T], False, False, skip=True)
                tok = mm(o, lo[:, d:d + 128], xh[:, c:c + T], False, k == n_k - 1, last=(j == 7), skip=True)
            w_read.append(tok)
            pair_read[n] = tok
            if k % 2:
                split_next()
            return tok

        tiles = {n: [a[n][i] for i in range(a[n].shape[0])]
                 for n in ("w_in", "ssd_out", "sc_out", "w_o", "sh_gate", "sh_up", "qk", "vv", "w_out2", "w_up2", "w_down2")}
        w_order += tiles["w_in"][:39]
        for i in range(5):
            w_order += [tiles["w_in"][39 + i], tiles["ssd_out"][i]]
        w_order += tiles["ssd_out"][5:] + [t for n in ("sc_out", "w_o", "sh_gate", "sh_up") for t in tiles[n]]

        Q8 = arena(81, 8)
        first = [0, 1, 2, 3]

        def first_ada():
            for _ in range(2):
                i = first.pop(0)
                ada_group(0, i, i % 2)
                if i:
                    ada_close(4 + i % 2)
            if not first:
                ada_close(4)
                split_next()

        XC = arena(0, 8)
        t_hs = []
        t_h = norm(X, XC, H, Q8, [t_x] * 8, 2, 3, True, 1024.0, 1e-5, lambda k: M(8 + k), lambda k: M(k),
                   lambda: (t_mod[0, 3], t_mod[0, 7]), between=first_ada)
        t_hs = split(H, t_h)

        dt = small[:, 512:576]
        e1 = small[:, 576:640]
        u1 = small[:, 640:704]
        r1 = small[:, 704:768]
        dA = small[:, 768:832]
        acsT = small[:, 832:896]
        dec = small[:, 896:928]
        dtd = small[:, 928:960]
        acsF = small[0:32, 1024:1280]
        for t in range(2):
            for k in range(8):
                tok = mm(bank[2][:, t * 32:t * 32 + 32], H[:, k, t * 128:t * 128 + 128], wdt[:, k, :],
                         k == 0, k == 7, t_wdt, t_h[k], free[2], last=(t == 1 and k == 7))
        v2 = lambda x: x.rearrange("p (t h) -> p t h", t=2)
        t0 = tt(DV, v2(dt), v2(bank[2][:, 0:64]), rowb[:, 0:32].unsqueeze(1).to_broadcast([128, 2, 32]),
                ALU.add, tok, t_row)
        free[2] = [t0]
        t1 = act(e1, dt, ACT.Abs, t0)
        t1 = act(e1, e1, ACT.Exp, t1, scale=-1.0)
        t_A = act(small[:, 960:992], rowb[:, 32:64], ACT.Exp, t_row)
        t2 = ts(DV, u1, e1, 1.0, None, ALU.add, None, t1)
        t3 = act(r1, u1, ACT.Ln, t2)
        t4 = stt(e1, u1, -1.0, e1, ALU.add, ALU.subtract, t2)
        t5 = DV.do(lambda e: e.reciprocal(u1, u1), t3, t4)
        t5 = tt(DV, e1, e1, u1, ALU.mult, t5)
        t5 = tt(DV, r1, r1, e1, ALU.subtract, t5, t3)
        t5 = stt(dt, dt, 0.0, r1, ALU.max, ALU.add, t5)
        t_dt = t5
        t6 = stt(v2(dA), v2(dt), -1.0, small[:, 960:992].unsqueeze(1).to_broadcast([128, 2, 32]),
                 ALU.mult, ALU.mult, t5, t_A)
        XS, Z, BB, CC = arena(0, 16), arena(16, 16), arena(32, 8), arena(40, 8)

        def conv(o, x, cw, n, K, at, bias, tok):
            if bias is None:
                t = ts(DV, o, x, P(cw, (K - 1) * n + at), None, ALU.mult, None, tok)
            else:
                t = ts(DV, o, x, P(cw, (K - 1) * n + at), bias, ALU.mult, ALU.add, tok)
            for s in range(1, K):
                t = stt(o[:, s:T], x[:, 0:T - s], P(cw, (K - 1 - s) * n + at), o[:, s:T], ALU.mult, ALU.add, t)
            return t

        nb = [0]

        def next_bank():
            nb[0] ^= 1
            return nb[0]

        def xbc_tile(i, dst, at, chunk, store, *w):
            b = next_bank()
            tok = gemm(tiles["w_in"][i], t_hs, b)
            silu_xbc()
            res = []
            for c in range(2):
                t = conv(dst[:, at + c, :], bank[b][:, c * T:c * T + T], "cw", 32, 4, chunk + c,
                         P("cb", chunk + c), [tok, *w])
                res.append(t)
            free[b] = [t]
            o = dst[:, at:at + 2, :]
            waiting.append((o, res, store))

        waiting = []

        def silu_xbc():
            if waiting:
                o, res, (t, i) = waiting.pop()
                t[i] = act(o, o, ACT.Silu, *res)

        t_B, t_C, t_XS = {}, {}, {}
        for i in range(4):
            xbc_tile(i, BB, 2 * i, 16 + 2 * i, (t_B, i))
            if i == 1:
                for c in range(2):
                    mm(bank[3][:, c * 32:c * 32 + 32], triU[:, :], dA[:, c * 32:c * 32 + 32], True, True, t_const, t6, free[3])
                tok = mm(bank[3][:, 64:96], ones[:, :], dA[:, 0:32], True, True, last=True)
                for c in range(2):
                    tokF = mm(bank[2][0:32, c * 128:c * 128 + 128], dA[:, c * 32:c * 32 + 32], triU[:, :], True, True,
                              free[2], last=(c == 1))
                t7 = DV.do(lambda e: e.tensor_copy(acsT, bank[3][:, 0:64]), tok)
                t8 = tt(DV, dec, bank[3][:, 64:96], acsT[:, 0:32], ALU.subtract, t7)
                free[3] = [t8]
                t8 = act(dec, dec, ACT.Exp, t8)
                t_dtd = tt(DV, dtd, dt[:, 0:32], dec, ALU.mult, t8)
                t_acs = DV.do(lambda e: e.tensor_copy(acsF, bank[2][0:32, 0:256]), tokF)
                free[2] = [t_acs]
                t_acsT = t7
        for i in range(4):
            xbc_tile(4 + i, CC, 2 * i, 24 + 2 * i, (t_C, i))
        for g in range(8):
            xbc_tile(8 + g, XS, 2 * g, 2 * g, (t_XS, g), t_h)
        silu_xbc()

        U = arena(48, 8)
        t_z = [None] * 8
        t_u = [None] * 8

        def z_tile(i):
            b = next_bank()
            tok = gemm(tiles["w_in"][16 + i], t_hs, b)
            t_z[i] = act(Z[:, 2 * i:2 * i + 2, :], bank[b][:, :].rearrange("p (n t) -> p n t", n=2), ACT.Silu, tok)
            free[b] = [t_z[i]]

        sc_tmp = arena(88, 2)

        def sc_tile(j):
            b = next_bank()
            tok = gemm(tiles["w_in"][24 + j], t_hs, b)
            prev = t_u[j - 1] if j else None
            t1 = act(sc_tmp[:, 0, :], bank[b][:, 0:T], ACT.Copy, tok, prev)
            t2 = tt(DV, sc_tmp[:, 1, :], bank[b][:, T:2 * T], sc_tmp[:, 0, :], ALU.mult, t1)
            free[b] = [t2]
            t_u[j] = conv(U[:, j, :], sc_tmp[:, 1, :], "scw", 8, 3, j, None, t2)

        def scb_tile(i):
            b = next_bank()
            tok = gemm(tiles["w_in"][32 + i], t_hs, b)
            t = tt(DV, U[:, 2 * i:2 * i + 2, :], U[:, 2 * i:2 * i + 2, :],
                   bank[b][:, :].rearrange("p (n t) -> p n t", n=2), ALU.mult, tok, t_u[2 * i], t_u[2 * i + 1])
            free[b] = [t]
            t_u[2 * i] = t_u[2 * i + 1] = t

        fill = []
        main = [lambda i=i: z_tile(i) for i in range(8)] + [lambda j=j: sc_tile(j) for j in range(8)] \
            + [lambda i=i: scb_tile(i) for i in range(4)]
        fill = [(f, (0, 4 + n // 2) if n % 2 == 0 and n < 16 else None) for n, f in enumerate(main)]

        def filler():
            if fill:
                f, g = fill.pop(0)
                ada_close(next_bank())
                f()
                if g:
                    ada_group(*g, next_bank())

        t_Y = [None] * 8
        prevY = {}
        for g in range(8):
            S = AR[:, (56 + 16 * (g % 2)) * 256:(72 + 16 * (g % 2)) * 256]
            Xdt, Xd, BT = S[:, 0:512], S[:, 512:768], S[:, 768:896]
            CBm, D = S[:, 896:1152], S[:, 1152:2176]
            CE, PV = S[:, 2176:2688], S[:, 2688:2944]
            RM = S[0:32, 2944:3968]
            old = prevY.get(g - 2)
            r3 = lambda x, n: x.rearrange("p (n t) -> p n t", n=n)
            for c in range(2):
                tR = tt(PO, r3(RM[:, c * 512:c * 512 + 512], 4),
                        acsF[:, c * 128:c * 128 + 128].unsqueeze(1).to_broadcast([32, 4, 128]),
                        ident[0:32, 4 * g:4 * g + 4].unsqueeze(2).to_broadcast([32, 4, 128]), ALU.mult,
                        t_acs, t_id, old)
            PE.wait(free[2], free[3], t_XS[g], t_B[g // 2], t_C[g // 2], t_id)
            for t in range(2):
                for j in range(2):
                    tX = tr(bank[2][:, (2 * t + j) * 128:(2 * t + j) * 128 + 128],
                            XS[:, 2 * g + j, t * 128:t * 128 + 128], last=(t == j == 1))
            tr(bank[3][:, 0:128], BB[:, g, 0:128])
            for c in range(2):
                tC = mm(bank[3][:, 128 + c * 128:256 + c * 128], BB[:, g, c * 128:c * 128 + 128],
                        CC[:, g, c * 128:c * 128 + 128], True, True, last=(c == 1))
            for c in range(2):
                tS = mm(bank[4 + c][:, :], ones[0:32, :], RM[:, c * 512:c * 512 + 512], True, True,
                        tR, free[4 + c], last=(c == 1))
            tBT = act(BT, bank[3][:, 0:128], ACT.Copy, tC, old)
            tE = act(CE, bank[5][:, :], ACT.Exp, tS)
            t1 = tt(DV, Xdt.rearrange("p (t r q) -> p t r q", t=2, r=4),
                    bank[2][:, :].rearrange("p (t r q) -> p t r q", t=2, r=4),
                    v2(dt)[:, :, 4 * g:4 * g + 4].unsqueeze(3).to_broadcast([128, 2, 4, 64]), ALU.mult, tX, t_dt, old)
            t1b = tt(DV, r3(Xd, 4), r3(bank[2][:, 0:256], 4),
                     dtd[:, 4 * g:4 * g + 4].unsqueeze(2).to_broadcast([128, 4, 64]), ALU.mult, t_dtd)
            free[2] = [t1b]
            t2 = tt(DV, r3(CBm, 2), r3(bank[3][:, 128:384], 2),
                    triU[:, :].unsqueeze(1).to_broadcast([128, 2, 128]), ALU.mult, tC, tBT, t_const)
            free[3] = [t2, tBT]
            for c in range(2):
                for r in range(4):
                    o = c * 512 + r * 128
                    t3 = ts(DV, D[:, o:o + 128], bank[4 + c][:, r * 128:r * 128 + 128],
                            acsT[:, c * 32 + 4 * g + r:c * 32 + 4 * g + r + 1], 0.0, ALU.subtract, ALU.min,
                            tS, tE, t_acsT)
                free[4 + c] = [t3]
                t3 = act(D[:, c * 512:c * 512 + 512], D[:, c * 512:c * 512 + 512], ACT.Exp, t3)
                tD = tt(DV, r3(D[:, c * 512:c * 512 + 512], 4), r3(D[:, c * 512:c * 512 + 512], 4),
                        CBm[:, c * 128:c * 128 + 128].unsqueeze(1).to_broadcast([128, 4, 128]), ALU.mult, t3, t2)
            tCE = tt(PO, r3(CE, 4), r3(CE, 4), CC[:, g, 128:256].unsqueeze(1).to_broadcast([128, 4, 128]),
                     ALU.mult, tE)
            filler()
            tok = mm(bank[6][:, 0:256], BT, Xd, True, True, tBT, t1b, free[6], last=True)
            tPV = act(PV, bank[6][:, 0:256], ACT.Copy, tok)
            free[6] = [tPV]
            filler()
            PE.wait(tPV, tD, tCE, t1, free[7])
            for j in range(2):
                for h in range(2):
                    r = 2 * j + h
                    o = bank[7][h * 64:h * 64 + 64, j * T:j * T + T]
                    mm(o[:, 0:128], Xdt[:, r * 64:r * 64 + 64], D[:, r * 128:r * 128 + 128], True, True)
                    mm(o[:, 128:256], Xdt[:, 256 + r * 64:256 + r * 64 + 64],
                       D[:, 512 + r * 128:512 + r * 128 + 128], True, False)
                    tok = mm(o[:, 128:256], PV[:, r * 64:r * 64 + 64], CE[:, r * 128:r * 128 + 128],
                             False, True, last=(r == 3))
            for j in range(2):
                t = stt(XS[:, 2 * g + j, :], XS[:, 2 * g + j, :], P("D", 2 * g + j), bank[7][:, j * T:j * T + T],
                        ALU.mult, ALU.add, tok)
            free[7] = [t]
            t_Y[g] = t
            prevY[g] = [t, tok]
            filler()
        while fill:
            filler()
        ada_close(next_bank())

        GA, GB = BB, CC
        GQ = [arena(56, 2), arena(58, 2)]
        rs = [small[:, 1280:1536], small[:, 1536:1792]]
        t_gq, t_yn, t_rs, t_sq = {}, {}, {}, {}

        def gated(g):
            sl = slice(2 * g, 2 * g + 2)
            t = tt(DV, XS[:, sl, :], XS[:, sl, :], Z[:, sl, :], ALU.mult, t_Y[g], t_z[g])
            t_sq[g] = act(GQ[g % 2], XS[:, sl, :], ACT.Square, t, t_gq.get(g - 2), prevY[6])

        def rooted(g):
            b = 2 + g % 2
            for k in range(2):
                tok = mm(bank[b][:, 0:T], ones[:, :], GQ[g % 2][:, k, :], k == 0, k == 1, t_sq[g], free[b],
                         last=(k == 1))
            t_gq[g] = tok
            r = rs[g % 2]
            t = ts(DV, r, bank[b][:, 0:T], 1.0 / 256.0, 1e-5, ALU.mult, ALU.add, tok, t_rs.get(g - 2))
            free[b] = [t]
            t = act(r, r, ACT.Sqrt, t)
            t = DV.do(lambda e, r=r: e.reciprocal(r, r), t)
            for k in range(2):
                t = stt(XS[:, 2 * g + k, :], XS[:, 2 * g + k, :], P("nw", 2 * g + k), r, ALU.mult, ALU.mult, t)
            t_rs[g] = t
            t_yn[2 * g] = t_yn[2 * g + 1] = t

        def ssd_split(g):
            return split_pair(XS[:, 2 * g:2 * g + 2, :], t_yn[2 * g])

        def ssd_out(g, x):
            for k in (2 * g, 2 * g + 1):
                t_so[0] = by_rows(tiles["ssd_out"][g], k, 16, x)

        t_so = [None]
        t_g = []
        for i in range(8):
            b = next_bank()
            gated(i)
            if i > 2:
                x = ssd_split(i - 3)
            tok = gemm(tiles["w_in"][36 + i], t_hs, b)
            dst = (GA if i < 4 else GB)[:, 2 * (i % 4):2 * (i % 4) + 2, :]
            t = act(dst, bank[b][:, :].rearrange("p (n t) -> p n t", n=2), ACT.Sigmoid, tok, t_Y[7], tCE)
            free[b] = [t]
            t_g.append(t)
            if i:
                rooted(i - 1)
            if i > 2:
                ssd_out(i - 3, x)
        rooted(7)
        t_us = split(U, t_u)
        for g in (5, 6, 7):
            ssd_out(g, ssd_split(g))

        t_m = [None] * 8
        for i in range(4):
            t = tt(DV, GA[:, 2 * i:2 * i + 2, :], GA[:, 2 * i:2 * i + 2, :],
                   bank[4 + i][:, :].rearrange("p (n t) -> p n t", n=2), ALU.mult, t_so[0], t_g[i])
            free[4 + i] = [t]
            b = next_bank()
            tok = gemm(tiles["sc_out"][i], t_us, b)
            t = tt(DV, GB[:, 2 * i:2 * i + 2, :], GB[:, 2 * i:2 * i + 2, :],
                   bank[b][:, :].rearrange("p (n t) -> p n t", n=2), ALU.mult, tok, t_g[4 + i], t)
            free[b] = [t]
            t = tt(DV, GA[:, 2 * i:2 * i + 2, :], GA[:, 2 * i:2 * i + 2, :], GB[:, 2 * i:2 * i + 2, :], ALU.add, t)
            t_m[2 * i] = t_m[2 * i + 1] = t
        for k in range(8):
            t_xa = ts(DV, X[:, k, :], X[:, k, :], ALPHA, None, ALU.mult, None, t_h)

        def residual(tok, b, i, gcol, which):
            for c in range(2):
                t = stt(X[:, 2 * i + c, :], bank[b][:, c * T:c * T + T], M(gcol + 2 * i + c, which),
                        X[:, 2 * i + c, :], ALU.mult, ALU.add, tok)
            free[b] = [t]
            return [t, t]

        t_ms = split(GA, t_m)
        t_x1 = []
        for i in range(4):
            b = next_bank()
            tok = gemm(tiles["w_o"][i], t_ms, b)
            t_x1 += residual([tok, t_xa, t_mod[0, 11]], b, i, 16, 0)
        later = [(1, i) for i in range(12)]

        def more_ada():
            ada_close(next_bank())
            if later:
                ada_group(*later.pop(0), next_bank())

        t_x1 = norm(X, X, X, Q8, t_x1, 2, 3, True, 1024.0, 1e-5, lambda k: P("ln1g", k), lambda k: P("ln1b", k),
                    between=more_ada)
        XC = arena(73, 8)
        t_hs = []
        t_h = norm(X, XC, H, Q8, t_x1, 2, 3, True, 1024.0, 1e-5, lambda k: M(32 + k), lambda k: M(24 + k),
                   (t_mod[0, 15], t_mod[0, 19]), between=more_ada)
        t_hs = split(H, t_h)
        t_ln = t_h
        for k in range(8):
            t_xa = ts(DV, X[:, k, :], X[:, k, :], ALPHA, None, ALU.mult, None, t_h)

        for t in range(2):
            for k in range(8):
                tok = mm(bank[2][:, t * 64:t * 64 + 64], H[:, k, t * 128:t * 128 + 128], wrt[:, k, :],
                         k == 0, k == 7, t_wrt, t_h[k], free[2], last=(t == 1 and k == 7))
        sc = small[:, 256 + 256:256 + 384]
        bi = small[:, 640:768]
        m8 = small[:, 768:896]
        gs = small[:, 896:912]
        rk = small[:, 912:928]
        rk2 = small[:, 928:944]
        lt = small[:, 1024:1088]
        cmpb = small[:, 1088:1216]
        v8 = small[:, 944:960]
        rep = small[:, 1280:1408]
        gate = small[:, 1408:1536]
        s1 = small[:, 960:962]
        v3 = lambda x: x.rearrange("p (t g h) -> p t g h", t=2, g=8)
        t = PO.do(lambda e: e.memset(lt, 1.0), t_acs, t_rs[7])
        t_lt = PO.do(lambda e: e.affine_select(out=lt, in_=lt, compare_op=ALU.is_ge, fill=0.0, base=-1,
                     pattern=[[1, 8], [-1, 8]], channel_multiplier=0), t)
        t0 = act(sc, bank[2][:, 0:128], ACT.Sigmoid, tok)
        free[2] = [t0]
        t0 = tt(DV, v2(bi), v2(sc), rowb[:, 64:128].unsqueeze(1).to_broadcast([128, 2, 64]), ALU.add, t0)
        for t in range(2):
            for g in range(8):
                o = (t * 8 + g) * 8
                t1 = DV.do(lambda e, o=o: e.max(m8[:, o:o + 8], bi[:, o:o + 8]), t0)
        m8v = m8.rearrange("p (n k) -> p n k", k=8)
        t1 = tt(DV, gs.unsqueeze(2), m8v[:, :, 0:1], m8v[:, :, 1:2], ALU.add, t1)
        gsv = gs.rearrange("p (t g) -> p t g", t=2)
        inner = gsv.unsqueeze(2).to_broadcast([128, 2, 8, 8])
        outer = gsv.unsqueeze(3).to_broadcast([128, 2, 8, 8])
        t2 = tt(DV, v3(cmpb), inner, outer, ALU.is_gt, t1)
        t2 = DV.do(lambda e: e.tensor_reduce(rk, cmpb.rearrange("p (n k) -> p n k", k=8), AX.X, ALU.add), t2)
        t3 = tt(DV, v3(cmpb), inner, outer, ALU.is_equal, t2)
        t3 = tt(DV, v3(cmpb), v3(cmpb), lt.rearrange("p (g h) -> p g h", g=8).unsqueeze(1)
                .to_broadcast([128, 2, 8, 8]), ALU.mult, t3, t_lt)
        t3 = DV.do(lambda e: e.tensor_reduce(rk2, cmpb.rearrange("p (n k) -> p n k", k=8), AX.X, ALU.add), t3)
        t3 = tt(DV, rk, rk, rk2, ALU.add, t3, t2)
        t3 = ts(DV, rk, rk, 3.5, None, ALU.is_lt, None, t3)
        t3 = ts(DV, rk, rk, -1.0, 1e30, ALU.add, ALU.mult, t3)
        t3 = tt(DV, bi.rearrange("p (n k) -> p n k", k=8), bi.rearrange("p (n k) -> p n k", k=8),
                rk.unsqueeze(2).to_broadcast([128, 16, 8]), ALU.add, t3)
        for t in range(2):
            bt, vt, rt = bi[:, t * 64:t * 64 + 64], v8[:, t * 8:t * 8 + 8], rep[:, t * 64:t * 64 + 64]
            t4 = DV.do(lambda e, bt=bt, vt=vt: e.max(vt, bt), t3)
            t4 = DV.do(lambda e, bt=bt, vt=vt, rt=rt: e.match_replace(rt, vt, bt, -3e30), t4)
            t4 = ts(DV, rt, rt, -2e30, None, ALU.is_lt, None, t4)
            gt = gate[:, t * 64:t * 64 + 64]
            t4 = tt(DV, gt, rt, sc[:, t * 64:t * 64 + 64], ALU.mult, t4)
            t4 = DV.do(lambda e, t=t, gt=gt: e.tensor_reduce(s1[:, t:t + 1], gt, AX.X, ALU.add), t4)
            t4 = DV.do(lambda e, t=t: e.reciprocal(s1[:, t:t + 1], s1[:, t:t + 1]), t4)
            t_gate = ts(DV, gt, gt, s1[:, t:t + 1], 2.5, ALU.mult, ALU.mult, t4)

        RT = AR[:, 85 * 256:90 * 256]
        relp, gV = RT[:, 0:2 * NBLK], RT[:, 2 * NBLK:4 * NBLK]
        vB, vI, ioB = RT[:, 640:640 + NBLK], RT[:, 800:800 + NBLK], RT[:, 960:992]
        th4, th2, eI = RT[:, 992:1008], RT[:, 1008:1040], RT[:, 1040:1041]
        posT, gateT = small[0:64, 1536:1792], small[0:64, 1792:2048]
        OH, OW, RG = small[0:64, 512:672], small[0:64, 672:832], small[0:64, 832:992]
        mi, cmp_ = small[0:64, 1024:1072], small[0:64, 1088:1184]

        def iota(dst, pattern, cm, base=0):
            return PO.do(lambda e: e.iota(dst, pattern=pattern, base=base, channel_multiplier=cm,
                                          allow_small_or_imprecise_dtypes=True), t_h)
        iota(vB, [[BLK, NBLK]], 0)
        iota(vI, [[1, NBLK]], 0)
        iota(ioB, [[1, BLK]], 0)
        iota(th4, [[4, 16]], 0, 4)
        iota(th2, [[2, 32]], 0, 2)
        t_io = iota(eI, [[1, 1]], 1)
        mk = [rep[:, 0:64], rep[:, 64:128]]

        SHH, SHG = arena(21, 2), arena(23, 2)
        tg = gemm(tiles["sh_gate"][0], t_hs, 0)
        tu = gemm(tiles["sh_up"][0], t_hs, 1)
        t = act(SHG, bank[0][:, :].rearrange("p (n t) -> p n t", n=2), ACT.Silu, tg)
        free[0] = [t]
        t_sh = tt(DV, SHH, bank[1][:, :].rearrange("p (n t) -> p n t", n=2), SHG, ALU.mult, t, tu)
        free[1] = [t_sh]
        H2 = AR[:, 0:2048].rearrange("p (t d) -> p t d", t=2)
        for t in range(2):
            for half in range(2):
                b = 6 + half
                PE.wait(free[b], t_id, t_h)
                for c in range(4):
                    tok = tr(bank[b][:, c * 128:c * 128 + 128], H[:, 4 * half + c, t * 128:t * 128 + 128],
                             last=(c == 3))
                t_H2 = act(H2[:, t, half * 512:half * 512 + 512], bank[b][:, :], ACT.Copy, tok, t_m, t_ln)
                free[b] = [t_H2]
        more_ada()
        more_ada()
        ada_close(next_bank())
        PE.wait(t_gate, free[2], free[3], free[0], free[1], t_const, t_id)
        mm(bank[2][0:64, 0:128], mk[0], triS[:, :], True, True)
        mm(bank[2][0:64, 128:256], mk[0], ones[:, :], True, False)
        mm(bank[2][0:64, 128:256], mk[1], triS[:, :], False, True)
        mm(bank[0][0:64, 0:1], mk[0], ones[:, 0:1], True, False)
        t_cnt = mm(bank[0][0:64, 0:1], mk[1], ones[:, 0:1], False, True, last=True)
        for t in range(2):
            tr(bank[3][0:64, t * 128:t * 128 + 128], mk[t])
            t_T = tr(bank[3][0:64, 256 + t * 128:384 + t * 128], gate[:, t * 64:t * 64 + 64], last=(t == 1))
        last = [t_gate]

        def step(f, *w):
            last[0] = DV.do(f, last[0], *w)
            return last[0]

        def s_ts(o, x, s1, op0, s2=None, op1=None, *w):
            if s2 is None:
                return step(lambda e: e.tensor_scalar(o, x, s1, None, op0), *w)
            return step(lambda e: e.tensor_scalar(o, x, s1, s2, op0, op1), *w)

        def s_tt(o, x, y, op):
            return step(lambda e: e.tensor_tensor(o, x, y, op))

        def s_stt(o, x, s1, y, op0, op1):
            return step(lambda e: e.scalar_tensor_tensor(out=o, in0=x, scalar=s1, in1=y, op0=op0, op1=op1))

        col = lambda i, n=1: mi[:, i:i + n]
        cnt, a1, a2 = col(0), col(4), col(5)
        uA, uB, uQ = col(1), col(2), col(3)
        free[0] = [step(lambda e: e.tensor_copy(cnt, bank[0][0:64, 0:1]), t_cnt, t_io)]
        s_ts(a1, cnt, 64.0, ALU.is_gt)
        s_ts(a2, cnt, 192.0, ALU.is_gt)
        s_tt(uA, a1, a2, ALU.add)
        s_stt(col(6), uA, -128.0, cnt, ALU.mult, ALU.add)
        s_ts(uB, col(6), 32.0, ALU.is_gt)
        t = s_stt(uQ, col(6), 0.0, uB, ALU.is_gt, ALU.subtract)
        mm(bank[1][0:64, 0:3], triS[0:64, 0:64], col(1, 3), True, True, t)
        t_un = mm(bank[1][0:64, 4:7], ones[0:64, 0:64], col(1, 3), True, True, last=True)
        w = tile_in(a["sh_down"][0])
        PE.wait(t_sh)
        for j in range(8):
            for i in range(2):
                tok = mm(bank[4 + j // 2][:, (j % 2) * T:(j % 2) * T + T],
                         w[:, (2 * j + i) * 128:(2 * j + i) * 128 + 128], SHH[:, i, :],
                         i == 0 and j % 2 == 0, True, free[4 + j // 2], last=(j == 7 and i == 1), skip=True)
        tile_used(tok)
        t_down = tok

        step(lambda e: e.tensor_copy(col(8, 3), bank[1][0:64, 0:3]), t_un)
        free[1] = [step(lambda e: e.tensor_copy(col(12, 3), bank[1][0:64, 4:7]))]
        s_ts(col(16), col(14), 3.0, ALU.add)
        s_ts(col(17), col(13), 1.0, ALU.add)
        s_ts(cmp_[:, 0:16], th4[0:64, :], col(10), ALU.is_le)
        s_ts(cmp_[:, 16:32], th4[0:64, :], col(16), ALU.is_le)
        s_ts(cmp_[:, 32:64], th2[0:64, :], col(9), ALU.is_le)
        s_ts(cmp_[:, 64:96], th2[0:64, :], col(17), ALU.is_le)
        step(lambda e: e.tensor_reduce(col(18, 2), cmp_[:, 0:32].rearrange("p (n k) -> p n k", n=2), AX.X, ALU.add))
        step(lambda e: e.tensor_reduce(col(20, 2), cmp_[:, 32:96].rearrange("p (n k) -> p n k", n=2), AX.X, ALU.add))
        qp, nC, bp, nBp, nR = col(18), col(19), col(20), col(21), col(22)
        s_tt(nR, col(12), nBp, ALU.add)
        s_tt(col(23), nR, nC, ALU.add)
        t_n = step(lambda e: e.tensor_copy(tab[0:1, NBLK + NIT:NBLK + NIT + 1], mi[0:1, 23:24]))
        s_ts(col(24), col(8), 0.0, ALU.add)
        s_ts(col(25), col(8), 1.0, ALU.add)
        s_tt(col(26), col(12), bp, ALU.add)
        s_ts(col(28, 3), col(24, 3), nC, ALU.min)
        s_tt(col(28, 3), col(28, 3), col(24, 3), ALU.add)
        s_ts(col(28, 3), col(28, 3), 4.0, ALU.mult)
        s_stt(col(30), col(9), 2.0, col(30), ALU.mult, ALU.add)
        s_stt(col(30), bp, -4.0, col(30), ALU.mult, ALU.add)
        s_ts(col(31), qp, 1.0, ALU.add, nR, ALU.min)
        s_stt(col(31), col(31), 4.0, col(10), ALU.mult, ALU.add)
        s_tt(col(30, 2), col(30, 2), col(2, 2), ALU.mult)
        s_tt(col(34), col(30), col(31), ALU.add)
        s_tt(col(36), uB, uQ, ALU.add)
        s_ts(col(36), col(36), -1.0, ALU.add, 1000.0, ALU.mult)
        s_tt(col(34), col(34), col(36), ALU.add)
        s_ts(col(28, 2), col(28, 2), 1000.0, ALU.add)
        s_tt(col(28, 2), col(28, 2), col(4, 2), ALU.mult)
        s_ts(col(32, 2), col(28, 2), -1000.0, ALU.add)
        s_stt(col(35), uB, 2.0, uQ, ALU.mult, ALU.add)
        s_ts(col(37, 2), col(32, 2), 4.0, ALU.add)
        s_tt(col(39), col(34), col(35), ALU.add)
        s_ts(col(40, 2), col(32, 2), col(34), ALU.subtract)
        s_tt(col(40, 2), col(40, 2), col(4, 2), ALU.mult)
        s_ts(col(40, 2), col(40, 2), col(34), ALU.add, float(BLK), ALU.mult)
        s_tt(col(42), col(41), col(40), ALU.subtract)
        s_ts(col(42), col(42), -128.0, ALU.add)
        s_ts(col(43), col(40), 8192.0, ALU.add)
        vE = vI[0:64, :]
        s_ts(OH, vE, col(32), ALU.is_ge)
        s_stt(OH, vE, col(37), OH, ALU.is_lt, ALU.mult)
        s_ts(RG, vE, col(33), ALU.is_ge)
        s_stt(RG, vE, col(38), RG, ALU.is_lt, ALU.mult)
        s_tt(OH, OH, RG, ALU.add)
        s_ts(RG, vE, col(34), ALU.is_ge)
        s_stt(RG, vE, col(39), RG, ALU.is_lt, ALU.mult)
        s_ts(OW, RG, col(35), ALU.mult)
        s_stt(OW, OH, 4.0, OW, ALU.mult, ALU.add)
        s_tt(OH, OH, RG, ALU.add)
        s_ts(posT, bank[2][0:64, 0:256], 128.0, ALU.is_ge, col(42), ALU.mult)
        free[2] = [s_stt(posT, bank[2][0:64, 0:256], col(43), posT, ALU.add, ALU.add)]
        step(lambda e: e.tensor_tensor(posT, posT, bank[3][0:64, 0:256], ALU.mult), t_T)
        s_ts(posT, posT, -8192.0, ALU.add)
        t = step(lambda e: e.tensor_copy(gateT, bank[3][0:64, 256:512]))
        free[3] = [t]
        PE.wait(t, free[0], free[2])
        mm(bank[0][0:1, 0:NBLK], eI[0:64, :], OH, True, True)
        tok = mm(bank[0][0:1, NBLK:2 * NBLK], ones[0:64, 0:1], OW, True, True, last=True)
        for t in range(2):
            mm(bank[2][:, t * NBLK:t * NBLK + NBLK], posT[:, t * 128:t * 128 + 128], OH, True, True)
            tok2 = mm(bank[3][:, t * NBLK:t * NBLK + NBLK], gateT[:, t * 128:t * 128 + 128], OH, True, True,
                      last=(t == 1))
        DV.do(lambda e: e.tensor_copy(tab[0:1, 0:NBLK], bank[0][0:1, 0:NBLK]), tok, t_n)
        t_tab = DV.do(lambda e: e.tensor_copy(
            tab[0:1, NBLK:NBLK + NIT].unsqueeze(2),
            bank[0][0:1, NBLK:2 * NBLK].rearrange("p (n k) -> p n k", k=4)[:, :, 0:1]))
        free[0] = [t_tab]
        t = tt(DV, v2(relp), v2(bank[2][:, 0:2 * NBLK]), vB.unsqueeze(1).to_broadcast([128, 2, NBLK]), ALU.subtract,
               tok2)
        free[2] = [t]
        t_rel = DV.do(lambda e: e.tensor_copy(gV, bank[3][:, 0:2 * NBLK]))
        free[3] = [t_rel]

        XG = arena(8, 8, 128)
        SX = [AR[:, (12 + i) * 256:(13 + i) * 256] for i in range(2)]
        GX = [AR[:, (14 + i) * 256:(15 + i) * 256] for i in range(2)]
        GT = [AR[:, (16 + i) * 256:(17 + i) * 256] for i in range(2)]
        HD, SG, HT = AR[:, 18 * 256:19 * 256], AR[:, 19 * 256:20 * 256], AR[:, 20 * 256:21 * 256]
        gsum = [small[:, 0:1], small[:, 1:2]]
        YH, YL = FR[:, 0:1024], FR[:, 1024:2048]
        ST = FR[:, 2048:2304]
        slots = [r[:, :] for r in ring] + [AR[:, (21 + 8 * i) * 256:(29 + 8 * i) * 256] for i in range(NX - NS)]
        held = [None] * NX
        for n, (_, tok) in enumerate(stream):
            held[n % NS] = tok
        for n in range(NS, NX):
            held[n] = [t_h, tok2, t_sh, t_down]
        sp_load(0, len(stream), None)
        xn = [0]
        q_pair = {}
        regs = {}

        def by_kind(q, p, body):
            kind = {}
            q.branch(lambda e: kind.__setitem__(0, e.value_load(tab[0:1, NBLK + p:NBLK + p + 1],
                                                                min_val=0, max_val=4)))
            seen, count = dict(q.seen), q.count
            for k, tests in ((4, (lambda r: r > 3,)), (2, (lambda r: r > 1, lambda r: r < 4)),
                             (1, (lambda r: r < 2,))):
                q.seen, q.count = dict(seen), count
                nest = {}

                def enter(e, nest=nest, tests=tests):
                    nest[0] = ExitStack()
                    for test in tests:
                        nest[0].enter_context(e.If(test(kind[0])))
                q.branch(enter)
                res = body(k)
                q.branch(lambda e, nest=nest: nest[0].close())
            return res

        def x_tiles(p):
            first = xn[0]
            xn[0] += 12
            for v in range(4):
                SP.branch(lambda e, v=v: regs.__setitem__(v, e.value_load(
                    tab[0:1, 4 * p + v:4 * p + v + 1], min_val=0, max_val=63)))

            def body(k):
                n = first
                for j in range(3):
                    for v in range(4):
                        SP.wait(held[n % NX])
                        w, at = 2048 // k, (v % k) * (2048 // k)
                        SP.branch(lambda e, n=n, j=j, v=v, w=w, at=at: e.dma_start(
                            slots[n % NX][:, 0:w],
                            a["wx"][bass.ds(regs[v], 1), j, :, at:at + w].rearrange("a p n -> p (a n)"))
                            .then_inc(s_xr[n % NX], 16))
                        n += 1
            by_kind(SP, p, body)
            for n in range(first, first + 12):
                held[n % NX] = None
            return [(n % NX, 16 * (n // NX + 1)) for n in range(first, first + 12)]

        def weights(tiles, j, k, u, q):
            per = 4 // k
            n = tiles[4 * j + k * u + q // per][0]
            return slots[n][:, (q % per) * 512:(q % per) * 512 + 512]

        def select(p):
            s = SX[p % 2].rearrange("p (t v s) -> p t v s", t=2, v=4)
            g = GX[p % 2].rearrange("p (t v s) -> p t v s", t=2, v=4)
            t = tt(DV, s, ioB.unsqueeze(1).unsqueeze(1).to_broadcast([128, 2, 4, BLK]),
                   v2(relp)[:, :, 4 * p:4 * p + 4].unsqueeze(3).to_broadcast([128, 2, 4, BLK]), ALU.is_equal,
                   t_rel, q_pair.get(("xg", p - 2)), t_io)
            q_pair["s", p] = t
            q_pair["g", p] = tt(PO, g, s, v2(gV)[:, :, 4 * p:4 * p + 4].unsqueeze(3).to_broadcast([128, 2, 4, BLK]),
                                ALU.mult, t, q_pair.get(("t", p - 2)))

        def turn(p):
            PE.wait(q_pair["g", p], free[2])
            for t in range(2):
                tok = tr(bank[2][:, t * 128:t * 128 + 128], GX[p % 2][:, t * 128:t * 128 + 128], last=(t == 1))
            q_pair["t", p] = tok
            t = act(GT[p % 2], bank[2][:, 0:256], ACT.Copy, tok, q_pair.get(("st", p - 2)), q_pair.get(("y", p - 2)),
                    accum=gsum[p % 2])
            free[2] = [t]
            q_pair["gs", p] = t

        def gather(p, half):
            b = 1 - half
            PE.wait(q_pair["s", p], free[b], t_H2)
            s = SX[p % 2].rearrange("p (t q) -> p t q", t=2)
            for c in range(4):
                for t in range(2):
                    d = (4 * half + c) * 128
                    tok = mm(bank[b][:, c * 128:c * 128 + 128], H2[:, t, d:d + 128], s[:, t, :], t == 0, t == 1,
                             last=(c == 3 and t == 1))
            q_pair["xg", p] = tok
            o = XG[:, 4 * half:4 * half + 4, :]
            i = bank[b][:, :].rearrange("p (c s) -> p c s", c=4)
            if half == 0:
                t = act(o, i, ACT.Copy, tok, q_pair.get(("gu", p - 1)))
            else:
                t = DV.do(lambda e: e.tensor_copy(o, i), tok, q_pair.get(("gu", p - 1)))
            free[b] = [t]
            q_pair["x", p, half] = t

        def group(p):
            tiles = x_tiles(p)
            PE.wait(free[0])

            def gate_up(k):
                for half in range(2):
                    PE.wait(q_pair["x", p, half])
                    for n, val in tiles[4 * half:4 * half + 4]:
                        PE.wait((s_xr[n], val))
                    for c in range(4):
                        for u in range(4 // k):
                            at = slice(BLK * k * u, BLK * k * (u + 1))
                            tok = mm(bank[0][at, :], XG[:, 4 * half + c, at], weights(tiles, half, k, u, c),
                                     half == 0 and c == 0, half == 1 and c == 3, last=(c == 3 and u == 4 // k - 1))
                    for n, _ in tiles[4 * half:4 * half + 4]:
                        held[n] = tok
                return tok
            tok = by_kind(PE, p, gate_up)
            q_pair["gu", p] = tok
            if p:
                PE.wait(q_pair["y", p - 1], q_pair["st", p - 1])
                q_pair["c", p - 1] = combine()
            q_pair["st", p] = ts(DV, ST, GT[p % 2], 0.0, None, ALU.is_gt, None, q_pair["gs", p],
                                 q_pair.get(("c", p - 1)))
            t = act(SG, bank[0][:, 0:256], ACT.Silu, tok, q_pair.get(("hd", p - 1)))
            t = tt(DV, HD, bank[0][:, 256:512], SG, ALU.mult, t, q_pair.get(("ht", p - 1)))
            free[0] = [t]
            q_pair["hd", p] = t
            if p + 1 < NIT:
                turn(p + 1)
                gather(p + 1, 0)
            PE.wait(t, free[2], t_id)
            for i in range(2):
                tok = tr(bank[2][:, i * 128:i * 128 + 128], HD[:, i * 128:i * 128 + 128], last=(i == 1))
            q_pair["ht", p] = tok
            t = act(HT, bank[2][:, 0:256], ACT.Copy, tok, q_pair.get(("d", p - 1)))
            free[2] = [t]
            if p + 1 < NIT:
                gather(p + 1, 1)
            if p + 2 < NIT:
                select(p + 2)
            for h in range(2):
                b = 3 if h == 0 else 1
                PE.wait(free[b], t)

                def down(k, h=h, b=b):
                    for n, val in tiles[8:12]:
                        PE.wait((s_xr[n], val))
                    for i in range(2):
                        for u in range(4 // k):
                            at = slice(BLK * k * u, BLK * k * (u + 1))
                            tok = mm(bank[b][at, :], HT[:, i * 128 + BLK * k * u:i * 128 + BLK * k * (u + 1)],
                                     weights(tiles, 2, k, u, 2 * i + h), i == 0, i == 1,
                                     last=(i == 1 and u == 4 // k - 1))
                    return tok
                tok = by_kind(PE, p, down)
                yh, yl = YH[:, h * 512:h * 512 + 512], YL[:, h * 512:h * 512 + 512]
                gs = gsum[p % 2]
                t1 = act(yh, bank[b][:, :], ACT.Copy, tok, q_pair["gs", p], q_pair.get(("c", p - 1)), scale=gs)
                t1 = stt(yl, bank[b][:, :], gs, yh.bitcast(fp), ALU.mult, ALU.subtract, t1, q_pair.get(("c", p - 1)))
                free[b] = [t1]
                q_pair["y", p, h] = t1
            q_pair["y", p] = t1
            q_pair["d", p] = tok
            for n, _ in tiles[8:12]:
                held[n] = tok

        def combine():
            for j in range(8):
                o = bank[4 + j // 2][:, (j % 2) * T:(j % 2) * T + T]
                mm(o, YH[:, j * 128:j * 128 + 128], ST, False, True, skip=True)
                tok = mm(o, YL[:, j * 128:j * 128 + 128], ST, False, True, last=(j == 7), skip=True)
            return tok

        select(0)
        select(1)
        turn(0)
        gather(0, 0)
        gather(0, 1)
        queues = (PE, AC, DV, PO, SP)
        for q in queues:
            q.wait(t_tab)
        nests = {}
        for q in queues:
            def load(e, q=q):
                nests[id(q)] = (ExitStack(), e.value_load(tab[0:1, NBLK + NIT:NBLK + NIT + 1], min_val=0, max_val=NIT))
            q.branch(load)
        before = [dict(q.seen) for q in queues]
        for p in range(NIT):
            if p >= 16:
                for q in queues:
                    q.branch(lambda e, q=q, p=p: nests[id(q)][0].enter_context(e.If(nests[id(q)][1] > p)))
            group(p)
        for q, seen in zip(queues, before):
            q.branch(lambda e, q=q: nests[id(q)][0].close())
            q.seen = seen
        PE.sem, AC.sem, DV.sem, PO.sem = s_pe2, s_act2, s_dve2, s_pool2
        for q in (PE, AC, DV, PO):
            q.count = 0
        e_act = act(small[:, 2:3], ones[:, 0:1], ACT.Copy)
        e_dve = DV.do(lambda e: e.memset(small[:, 3:4], 0.0))
        e_pool = PO.do(lambda e: e.memset(small[:, 4:5], 0.0))
        PE.wait(e_act, e_dve)
        tok = combine()
        late[0] = len(stream)
        t_over = [tok, e_act, e_dve, e_pool]
        for b in range(8):
            free[b] = list(t_over)
        w_order += tiles["vv"] + [tiles["qk"][i] for i in (0, 2, 4, 6, 1, 5, 3, 7)] + tiles["w_out2"]
        for i in range(0, 22, 2):
            w_order += tiles["w_up2"][i:i + 2] + (tiles["w_down2"][i // 2 - 1:i // 2] if i else [])
        w_order.append(tiles["w_down2"][10])
        t_x2 = []
        for i in range(4):
            t_x2 += residual([tok, t_xa, t_mod[0, 23]], 4 + i, i, 40, 0)
        for q in (AC, DV, PO):
            q.wait(t_over)
        gap = [lambda: None, split_next]
        t_x2 = norm(X, X, X, Q8, t_x2, 2, 3, True, 1024.0, 1e-5, lambda k: P("ln2g", k), lambda k: P("ln2b", k),
                    between=lambda: gap.pop(0)())

        XC = arena(0, 8)
        t_hs = []
        t_h = norm(X, XC, H, Q8, t_x2, 2, 3, False, 1024.0, 1e-6, lambda k: M(8 + k, 1), lambda k: M(k, 1),
                   (t_mod[1, 3], t_mod[1, 7]), parts=t_hs)
        t_ln = t_h

        BIAS = arena(69, 8, 384)
        t_bias = AC.dma(BIAS, a["relb"], s_bias, 16, t_ln)
        for o in (0, 256):
            t_bias = PO.do(lambda e, o=o: e.memset(BIAS[0:64, :, o + 64:o + 128], -1e30), t_bias)
        QK = arena(8, 16)
        VV = arena(24, 4, 512)
        t_qk = {}

        def qk_tile(i):
            b = next_bank()
            tok = gemm(tiles["qk"][i], t_hs, b)
            t = act(QK[:, 2 * i:2 * i + 2, :], bank[b][:, :].rearrange("p (n t) -> p n t", n=2), ACT.Copy, tok)
            free[b] = [t]
            t_qk[2 * i] = t_qk[2 * i + 1] = t
        t_v = {}
        for sec in range(2):
            for half in range(2):
                m = len(w_read)
                assert w_order[m // 2] is tiles["vv"][2 * sec + half]
                if len(w_split) == m:
                    split_next()
                for c in range(2):
                    hi, lo, tw = w_split[m + c]
                    PE.wait(tw)
                    for t in range(2):
                        o = bank[4 + t][:, :]
                        for i in range(2):
                            kk = 4 * half + 2 * c + i
                            sl, d = slice(t * 128, t * 128 + 128), slice(i * 512, i * 512 + 512)
                            mm(o, AH[:, kk, sl], hi[:, d], kk == 0, False, t_hs[kk],
                               free[4 + t] if kk == 0 else None)
                            mm(o, AL[:, kk, sl], hi[:, d], False, False)
                            tok = mm(o, AH[:, kk, sl], lo[:, d], False, kk == 7, last=(i == 1))
                        if kk == 7:
                            t_v[sec, t] = DV.do(lambda e, sec=sec, t=t: e.tensor_copy(
                                VV[:, 2 * sec + t, :], bank[4 + t][:, :]), tok)
                            free[4 + t] = [t_v[sec, t]]
                    w_read.append(tok)
                a_read[:] = [tok]
                split_next()
        for i in (0, 2, 4, 6):
            qk_tile(i)

        OA, OB = arena(32, 4), arena(36, 4)
        buf = lambda n: AR[:, 40 * 256 + 384 * n:40 * 256 + 384 * n + 384]
        SB, PT, ZB = [buf(i) for i in (0, 1, 2)], [buf(i) for i in (3, 4)], [buf(i) for i in (5, 6, 7)]
        EB, SPB = [buf(i) for i in (8, 9, 10, 11)], [buf(i) for i in (12, 13, 14)]
        nm = [small[:, 512 + 8 * i:520 + 8 * i] for i in range(3)]
        MK = arena(64, 1, 384)[:, 0, :]
        for o, s in ((0, triS), (128, ones), (256, triS)):
            t_mk = PO.do(lambda e, o=o, s=s: e.tensor_copy(MK[:, o:o + 128], s[:, :]), t_const, t_over)
        ta, tb = {}, {}

        def a_scores(h):
            r0, cq = (h % 2) * 64, h // 2
            q, k = QK[r0:r0 + 64, cq, :], QK[r0:r0 + 64, 4 + cq, :]
            PE.wait(t_qk[cq], t_qk[4 + cq], free[2])
            mm(bank[2][:, 0:128], q[:, 0:128], k[:, 0:128], True, True)
            tok = mm(bank[2][:, 128:384], q[:, 128:256], k[:, 0:256], True, True, last=True)
            S, n = SB[h % 3], nm[h % 3]
            t = stt(S, bank[2][:, 0:384], 0.125, BIAS[:, h, :], ALU.mult, ALU.add, tok, t_bias, ta.get(("pt", h - 3)))
            free[2] = [t]
            DV.do(lambda e: e.tensor_reduce(n[:, 0:1], S[:, 0:128], AX.X, ALU.max), t)
            t = DV.do(lambda e: e.tensor_reduce(n[:, 1:2], S[:, 128:384], AX.X, ALU.max), t)
            t = ts(DV, n[:, 2:4], n[:, 0:2], -1.0, None, ALU.mult, None, t)
            act(S[:, 0:128], S[:, 0:128], ACT.Exp, t, bias=n[:, 2:3], accum=n[:, 4:5])
            ta["x", h] = act(S[:, 128:384], S[:, 128:384], ACT.Exp, t, bias=n[:, 3:4], accum=n[:, 5:6])

        def a_norm(h):
            S, n, t = SB[h % 3], nm[h % 3], ta["x", h]
            t = DV.do(lambda e: e.reciprocal(n[:, 6:8], n[:, 4:6]), t)
            ts(DV, S[:, 0:128], S[:, 0:128], n[:, 6:7], None, ALU.mult, None, t)
            ta["p", h] = ts(DV, S[:, 128:384], S[:, 128:384], n[:, 7:8], None, ALU.mult, None, t)

        def a_turn(h):
            PE.wait(ta["p", h], free[3], t_id)
            for i in range(3):
                tok = tr(bank[3][:, i * 128:i * 128 + 128], SB[h % 3][:, i * 128:i * 128 + 128], last=(i == 2))
            ta["pt", h] = tok
            t = act(PT[h % 2], bank[3][:, 0:384], ACT.Copy, tok, ta.get(("o", h - 2)))
            free[3] = [t]
            ta["c", h] = t

        def a_out(h):
            r0, b = (h % 2) * 64, 6
            PE.wait(ta["c", h], t_v[0, 0], t_v[0, 1], free[b] if h % 2 == 0 else None)
            o = bank[b][r0:r0 + 64, 0:T]
            mm(o, VV[:, 0, h * 64:h * 64 + 64], PT[h % 2][:, 0:256], True, False)
            tok = mm(o[:, 128:256], VV[:, 1, h * 64:h * 64 + 64], PT[h % 2][:, 256:384], False, True, last=True)
            ta["o", h] = tok
            if h % 2:
                t = act(OA[:, h // 2, :], bank[b][:, 0:T], ACT.Copy, tok)
                free[b] = [t]
                ta["e", h // 2] = t

        def b_scores(h):
            r0, cq = (h % 2) * 64, h // 2
            q, k = QK[r0:r0 + 64, 8 + cq, :], QK[r0:r0 + 64, 12 + cq, :]
            PE.wait(t_qk[8 + cq], t_qk[12 + cq], free[4])
            mm(bank[4][:, 0:256], k[:, 0:128], q[:, 0:256], True, True)
            tok = mm(bank[4][:, 256:384], k[:, 128:256], q[:, 128:256], True, True, last=True)
            Zb, E, S = ZB[h % 3], EB[h % 4], SPB[h % 3]
            t = act(Zb, bank[4][:, 0:384], ACT.Copy, tok, tb.get(("w", h - 3)), scale=0.125)
            free[4] = [t]
            t1 = act(E, Zb, ACT.Abs, t, tb.get(("o", h - 4)))
            t1 = act(E, E, ACT.Exp, t1, scale=-1.0)
            tb["l", h] = act(E, E, ACT.Ln, t1, bias=1.0)

        def b_soft(h):
            Zb, E, S = ZB[h % 3], EB[h % 4], SPB[h % 3]
            t2 = stt(S, Zb, 0.0, E, ALU.max, ALU.add, tb["l", h], tb.get(("r", h - 3)))
            tb["s", h] = tt(PO, S, S, MK, ALU.mult, t2, t_mk)

        def b_tail(h):
            Zb, E, S = ZB[h % 3], EB[h % 4], SPB[h % 3]
            PE.wait(tb["s", h], free[5], t_const)
            mm(bank[5][:, 0:256], triG[:, :], S[:, 0:256], True, False)
            mm(bank[5][:, 128:256], ones[:, :], S[:, 256:384], False, True)
            tok = mm(bank[5][:, 256:384], triG[:, :], S[:, 256:384], True, True, last=True)
            tb["r", h] = tok
            t = tt(DV, Zb, Zb, bank[5][:, 0:384], ALU.subtract, tok)
            free[5] = [t]
            t = ts(DV, Zb, Zb, 0.0, None, ALU.min, None, t)
            t = act(E, Zb, ACT.Exp, t)
            tb["w", h] = t
            tb["m", h] = tt(PO, E, E, MK, ALU.mult, t)

        def b_out(h):
            r0, b = (h % 2) * 64, 7
            PE.wait(tb["m", h], t_v[1, 0], t_v[1, 1], free[b] if h % 2 == 0 else None)
            o = bank[b][r0:r0 + 64, 0:T]
            mm(o, VV[:, 2, h * 64:h * 64 + 64], EB[h % 4][:, 0:256], True, False)
            tok = mm(o[:, 128:256], VV[:, 3, h * 64:h * 64 + 64], EB[h % 4][:, 256:384], False, True, last=True)
            tb["o", h] = tok
            if h % 2:
                t = act(OB[:, h // 2, :], bank[b][:, 0:T], ACT.Copy, tok)
                free[b] = [t]
                tb["e", h // 2] = t

        for s in range(11):
            if 1 <= s < 9:
                a_norm(s - 1)
                b_soft(s - 1)
            if s < 8:
                b_scores(s)
                a_scores(s)
            if 2 <= s < 10:
                a_turn(s - 2)
                b_tail(s - 2)
            if s >= 3:
                a_out(s - 3)
                b_out(s - 3)
            if s < 4:
                qk_tile((1, 5, 3, 7)[s])
            else:
                more_ada()
        ada_close(next_bank())
        t_o = []
        for n, (O, tk) in enumerate(((OA, ta), (OB, tb))):
            t_o += norm(O, O, O, Q8[:, 4 * n:4 * n + 4, :], [tk["e", k] for k in range(4)], 2, 3, False, 512.0, 1e-6,
                        lambda k, n=n: P("gab", 4 * n + k), chunks=4)
        OO = arena(32, 8)
        t_o = split(OO, t_o)
        t_x3 = []
        for i in range(4):
            b = next_bank()
            tok = gemm(tiles["w_out2"][i], t_o, b)
            t_x3 += residual([tok, t_mod[1, 11]], b, i, 16, 1)
        t_hs = []
        t_h = norm(X, XC, H, Q8, t_x3, 2, 3, False, 1024.0, 1e-6, lambda k: M(32 + k, 1), lambda k: M(24 + k, 1),
                   (t_mod[1, 15], t_mod[1, 19]), parts=t_hs)
        HF = [arena(8 + 2 * i, 2) for i in range(2)]
        CV = [arena(12 + 2 * i, 2) for i in range(4)]
        t_f, t_hf = {}, {}

        def down_split(g):
            x = split_pair(HF[g % 2], t_f[2 * g], t_f[2 * g + 1])
            t_hf[g] = x[2]
            return x

        def down(g, x):
            for k in (2 * g, 2 * g + 1):
                t_d[0] = by_rows(tiles["w_down2"][g], k, 22, x)

        t_d = [None]
        for i in range(22):
            b = next_bank()
            tok = gemm(tiles["w_up2"][i], t_hs, b)
            if i and i % 2 == 0:
                x = down_split(i // 2 - 1)
            cv = CV[i % 4]
            for c in range(2):
                t = conv(cv[:, c, :], bank[b][:, c * T:c * T + T], "cw2", 44, 3, i + 22 * c, P("cb2", i + 22 * c),
                         [tok, t_f.get(i - 4)] if c == 0 else tok)
            free[b] = [t]
            t = act(cv[:, 0, :], cv[:, 0, :], ACT.Silu, t)
            t_f[i] = tt(PO, HF[i // 2 % 2][:, i % 2, :], cv[:, 0, :], cv[:, 1, :], ALU.mult, t, t_hf.get(i // 2 - 2))
            if i % 2 and i > 1:
                down(i // 2 - 1, x)
        down(10, down_split(10))
        t_x4 = []
        for i in range(4):
            t_x4 += residual([t_d[0], t_mod[1, 23]], 4 + i, i, 40, 1)
        t_y = norm(X, X, H, Q8, t_x4, 2, 3, False, 1024.0, 1e-6, lambda k: P("fg", k))
        for k in range(0, 8, 2):
            AC.dma(out[:, k:k + 2, :], H[:, k:k + 2, :], s_out, 16, t_y[k + 1])
        AC.wait((s_out, 64))

        sp_load(late[0], len(stream), t_over)

        block = ctx.enter_context(nc.Block())

        @block.sync
        def _(eng):
            SP.play(eng)

        @block.scalar
        def _(eng):
            AC.play(eng)

        @block.vector
        def _(eng):
            DV.play(eng)

        @block.gpsimd
        def _(eng):
            PO.play(eng)

        @block.tensor
        def _(eng):
            PE.play(eng)


def pack_blocks(w):
    k, n = w.shape
    b = w.reshape(k // 128, 128, n // 128, 128).transpose(2, 0, 1, 3).reshape(-1, 16, 128, 128)
    return b.transpose(0, 2, 1, 3).reshape(-1, 128, 2048)


def lay_out(np, x):
    chunk = lambda v: v.reshape(-1, 128).T
    a = {}
    w_in = x["w_in"][0]
    pair = lambda m, first, second: np.concatenate(
        [np.concatenate([m[:, first + 128 * j:first + 128 * j + 128], m[:, second + 128 * j:second + 128 * j + 128]],
                        axis=1) for j in range((second - first) // 128)], axis=1)
    a["w_in"] = pack_blocks(np.concatenate(
        [w_in[:, 4096:6144], w_in[:, 2048:4096], w_in[:, 0:2048], pair(w_in, 7200, 8224), w_in[:, 6176:7200],
         w_in[:, 9248:11296]], axis=1))
    a["wdt"] = w_in[:, 6144:6176].reshape(8, 128, 32).transpose(1, 0, 2)
    a["wrt"] = x["router_w"][0].reshape(8, 128, 64).transpose(1, 0, 2)
    a["dtb"], a["alog"], a["rb"] = x["ssd_dt_bias"][0], x["ssd_A_log"][0], x["router_bias"][0]
    a["xT"] = x["x"][0].T.reshape(8, 128, T).transpose(1, 0, 2)
    a["ada"], a["ada2"] = (x[n][0].reshape(2, 4, 128, 12, 512).transpose(3, 0, 2, 1, 4).reshape(24, 128, 2048)
                           for n in ("w_ada", "w_ada_2"))
    rows = lambda w: w.reshape(-1, 2, 128, 1024).transpose(0, 2, 1, 3).reshape(-1, 128, 2048)
    a["ssd_out"], a["sc_out"], a["w_o"] = rows(x["w_ssd_out"][0]), pack_blocks(x["w_sc_out"][0]), pack_blocks(x["w_o"][0])
    for n in ("sh_gate", "sh_up", "sh_down"):
        a[n] = pack_blocks(x[n][0])
    g, u, d = x["w_gate"][0], x["w_up"][0], x["w_down"][0]
    wx = np.empty((N_EXP, 3, 128, 2048), g.dtype)
    wx[:, 0:2].reshape(N_EXP, 2, 128, 4, 2, 256)[:] = np.stack(
        [w.reshape(N_EXP, 2, 4, 128, 256).transpose(0, 1, 3, 2, 4) for w in (g, u)], axis=4)
    wx[:, 2] = d.reshape(N_EXP, 2, 128, 1024).transpose(0, 2, 1, 3).reshape(N_EXP, 128, 2048)
    a["wx"] = wx
    w2 = x["w_in_2"][0]
    a["qk"] = pack_blocks(np.concatenate([w2[:, 0:1024], w2[:, 1536:2560]], axis=1))
    a["vv"] = np.concatenate([w2[:, c:c + 512].reshape(2, 4, 128, 512).transpose(0, 2, 1, 3).reshape(2, 128, 2048)
                              for c in (1024, 2560)], axis=0)
    a["w_out2"], a["w_down2"] = pack_blocks(x["w_out_2"][0]), rows(x["w_down_2"][0])
    a["w_up2"] = pack_blocks(pair(x["w_up_2"][0], 0, 2816))
    taps = lambda w: np.concatenate([chunk(w[k]) for k in range(w.shape[0])], axis=1)
    cols = {
        "b_ada": chunk(x["b_ada"][0]), "cw": taps(x["ssd_conv_w"][0]), "cb": chunk(x["ssd_conv_b"][0]),
        "D": chunk(np.repeat(x["ssd_D"][0], 64)), "nw": chunk(x["ssd_norm_w"][0]), "scw": taps(x["sc_conv_w"][0]),
        "ln1g": chunk(x["ln1_g"][0]), "ln1b": chunk(x["ln1_b"][0]), "ln2g": chunk(x["ln2_g"][0]),
        "ln2b": chunk(x["ln2_b"][0]), "b_ada2": chunk(x["b_ada_2"][0]),
        "gab": chunk(np.concatenate([x["g_a_2"][0], x["g_b_2"][0]])), "cw2": taps(x["conv_w_2"][0]),
        "cb2": chunk(x["conv_b_2"][0]), "fg": chunk(x["final_g_2"]), "c": chunk(x["c"][0]), "c2": chunk(x["c_2"][0]),
    }
    a["par"] = np.concatenate([cols[n] for n in _PAR], axis=1)
    q, k = np.arange(128)[:, None], np.arange(128)[None, :]
    at = lambda d: np.clip(d, -128, 128) + 128
    idx = np.concatenate([at(q - k), at(q + 128 - k), at(q - k)], axis=1)
    a["relb"] = x["rel_bias_2"][0][:, idx].transpose(1, 0, 2)
    return a


def kernel(**inputs):
    import numpy as np
    import concourse.bacc as bacc
    from concourse.bass_utils import run_bass_kernel_spmd

    x = {n: np.asarray(v) for n, v in inputs.items()}
    laid = {n: np.ascontiguousarray(v) for n, v in lay_out(np, x).items()}
    nc = bacc.Bacc("TRN2", target_bir_lowering=False, num_devices=1)
    aps = {n: nc.dram_tensor(f"in_{n}", v.shape, mybir.dt.from_np(v.dtype), kind="ExternalInput").ap()
           for n, v in laid.items()}
    out = nc.dram_tensor("out_x", (128, 8, T), mybir.dt.float32, kind="ExternalOutput").ap()
    build(nc, aps, out)
    r = run_bass_kernel_spmd(nc, [{f"in_{n}": v for n, v in laid.items()}], core_ids=[0])
    y = r.results[0]["out_x"]
    return np.ascontiguousarray(y.transpose(2, 1, 0).reshape(1, T, 1024))
```
